# Optimizing a Trainium2 kernel written in Bass

```python
import math
import jax, jax.numpy as jnp
from jax import lax
import numpy as np

"""Hybrid diffusion / flow-matching backbone: DEPTH layers of one shared-weight trunk run over an
un-noised context prefix and the noisy latent tokens.
Inputs: x (BATCH, SEQ, D_MODEL) latent tokens on a flattened grid of width GRID_W,
        c (BATCH, D_MODEL) conditioning vector, ctx (BATCH, CTX_LEN, D_MODEL) context tokens,
        c_ctx (D_MODEL,) learned modulation vector for context tokens, plus per-layer weights.
Output: (BATCH, SEQ, D_MODEL) latent stream after the final RMSNorm.
Each layer: adaLN-modulated RMSNorm -> one combined input projection -> three parallel mixers
(multi-head latent attention, multi-scale pooling, grouped 2-D Fourier) -> per-branch projection to
D_MODEL -> per-channel sigmoid-gated sum -> output projection -> gated residual; then an
adaLN-modulated RMSNorm -> SwiGLU (even layers) / top-2-of-8 expert SwiGLU (odd layers) -> gated residual.
"""

D_MODEL = 1024
BATCH = 1
SEQ = 256
DEPTH = 2

CTX_LEN = 256
GRID_W = 64
N_HEADS = 8
QK_NOPE = 64
QK_ROPE = 32
QK_DIM = QK_NOPE + QK_ROPE
V_DIM = 64
Q_LORA = 384
KV_LORA = 256
ROPE_BASE = 10000.0
Q_BLOCK = 128
ATTN_W = N_HEADS * V_DIM
ATTN_SCALE = QK_DIM ** -0.5
POOL_WINDOWS = (2, 4, 8, 16)
POOL_GROUPS = 4
POOL_GC = 128
POOL_W = POOL_GROUPS * POOL_GC
FFT_GROUPS = 4
FFT_GC = 128
FFT_W = FFT_GROUPS * FFT_GC
N_BRANCH = 3
OFF_Q = 0
OFF_KV = OFF_Q + Q_LORA
OFF_KR = OFF_KV + KV_LORA
OFF_POOL = OFF_KR + QK_ROPE
OFF_FFT = OFF_POOL + POOL_W
OFF_GATE = OFF_FFT + FFT_W
IN_COLS = OFF_GATE + N_BRANCH * D_MODEL
D_FF = 2816
N_EXPERTS = 8
TOP_K = 2
D_FF_EXPERT = 2816
N_DENSE = (DEPTH + 1) // 2
N_MOE = DEPTH // 2
EPS = 1e-6

kernel_name = "hybrid_mla_pool_fourier_moe_dit"

def rmsnorm(x, g):
    xf = x.astype(jnp.float32)
    y = xf * lax.rsqrt(jnp.mean(xf * xf, axis=-1, keepdims=True) + EPS)
    return (y * g.astype(jnp.float32)).astype(x.dtype)

def modulate(h, shift, scale):
    return h * (1 + scale) + shift

def axial_rope_tables(n_rows, dtype):
    rows = jnp.repeat(jnp.arange(n_rows, dtype=jnp.float32), GRID_W)
    cols = jnp.tile(jnp.arange(GRID_W, dtype=jnp.float32), n_rows)
    half = QK_ROPE // 2
    inv = ROPE_BASE ** (-jnp.arange(0, half, 2, dtype=jnp.float32) / half)
    ang = jnp.stack([rows[:, None] * inv, cols[:, None] * inv], axis=1)
    return jnp.cos(ang).astype(dtype), jnp.sin(ang).astype(dtype)

def apply_axial_rope(x, cos, sin):
    nf = QK_ROPE // 4
    shp = x.shape
    xr = x.reshape(*shp[:-1], 2, 2, nf)
    mid = (1,) * (x.ndim - 3)
    c = cos.reshape(cos.shape[0], *mid, 2, nf)
    s = sin.reshape(sin.shape[0], *mid, 2, nf)
    x1 = xr[..., 0, :]
    x2 = xr[..., 1, :]
    out = jnp.stack([x1 * c - x2 * s, x2 * c + x1 * s], axis=-2)
    return out.reshape(shp)

def mla_queries(pq, g_q, w_uq):
    q = jnp.einsum('blr,rhd->blhd', rmsnorm(pq, g_q), w_uq)
    return q[..., :QK_NOPE], q[..., QK_NOPE:]

def mla_keys_values(pkv, g_kv, w_ukv):
    kv = jnp.einsum('blr,rhd->blhd', rmsnorm(pkv, g_kv), w_ukv)
    return kv[..., :QK_NOPE], kv[..., QK_NOPE:]

def attend(q_nope, q_rope, k_nope, k_rope, v):
    s = (jnp.einsum('bqhd,bkhd->bhqk', q_nope, k_nope)
         + jnp.einsum('bqhr,bkr->bhqk', q_rope, k_rope))
    p = jax.nn.softmax(s.astype(jnp.float32) * ATTN_SCALE, axis=-1).astype(v.dtype)
    return jnp.einsum('bhqk,bkhd->bqhd', p, v)

def blocked_attend(q_nope, q_rope, k_nope, k_rope, v):
    B, L = q_nope.shape[:2]
    nb = L // Q_BLOCK

    def to_blocks(t):
        return t.reshape(B, nb, Q_BLOCK, *t.shape[2:]).swapaxes(0, 1)

    out = lax.map(lambda qs: attend(qs[0], qs[1], k_nope, k_rope, v),
                  (to_blocks(q_nope), to_blocks(q_rope)))
    return out.swapaxes(0, 1).reshape(B, L, N_HEADS, V_DIM)

def multiscale_pool(p, w_pool, s_pool):
    B, L, _ = p.shape
    pg = p.reshape(B, L, POOL_GROUPS, POOL_GC).astype(jnp.float32)
    cs = jnp.cumsum(pg, axis=1)
    cs = jnp.concatenate([jnp.zeros_like(cs[:, :1]), cs], axis=1)
    win = jnp.array(POOL_WINDOWS, dtype=jnp.int32)
    left = win // 2
    right = win - 1 - left
    t = jnp.arange(L, dtype=jnp.int32)[:, None]
    hi = jnp.minimum(t + right + 1, L)
    lo = jnp.maximum(t - left, 0)
    g = jnp.arange(POOL_GROUPS, dtype=jnp.int32)[None, :]
    window_sum = cs[:, hi, g, :] - cs[:, lo, g, :]
    mean = window_sum / (hi - lo).astype(jnp.float32)[None, :, :, None]
    mixed = (mean - pg).astype(p.dtype)
    y = jnp.einsum('blgc,gcd->blgd', mixed, w_pool)
    return y.reshape(B, L, POOL_W) * s_pool

def fourier_mix(f):
    B, L, _ = f.shape
    fg = f.reshape(B, L, FFT_GROUPS, FFT_GC).astype(jnp.float32)
    fr = jnp.fft.fft2(fg, axes=(1, 3), norm='ortho').real
    return fr.reshape(B, L, FFT_W).astype(f.dtype)

def gated_merge(attn_out, pooled, fourier, gate_pre, w_oa, w_ob, w_oc, w_out):
    B, L = attn_out.shape[:2]
    g = jax.nn.sigmoid(gate_pre).reshape(B, L, N_BRANCH, D_MODEL)
    y = (g[:, :, 0] * (attn_out.reshape(B, L, ATTN_W) @ w_oa)
         + g[:, :, 1] * (pooled @ w_ob)
         + g[:, :, 2] * (fourier @ w_oc))
    return y @ w_out

def token_mixer(h_lat, h_ctx, w_in, b_gate, g_q, w_uq, g_kv, w_ukv, w_pool, s_pool,
                w_oa, w_ob, w_oc, w_out, cos, sin, with_ctx_out):
    p_lat = h_lat @ w_in
    q_nope, q_rope = mla_queries(p_lat[..., OFF_Q:OFF_KV], g_q, w_uq)
    q_rope = apply_axial_rope(q_rope, cos, sin)
    k_nope_l, v_l = mla_keys_values(p_lat[..., OFF_KV:OFF_KR], g_kv, w_ukv)
    k_rope_l = apply_axial_rope(p_lat[..., OFF_KR:OFF_POOL], cos, sin)
    p_ctx_kv = h_ctx @ w_in[:, OFF_KV:OFF_POOL]
    k_nope_c, v_c = mla_keys_values(p_ctx_kv[..., :KV_LORA], g_kv, w_ukv)
    k_rope_c = p_ctx_kv[..., KV_LORA:]
    k_nope = jnp.concatenate([k_nope_c, k_nope_l], axis=1)
    k_rope = jnp.concatenate([k_rope_c, k_rope_l], axis=1)
    v = jnp.concatenate([v_c, v_l], axis=1)
    attn_l = blocked_attend(q_nope, q_rope, k_nope, k_rope, v)
    pool_l = multiscale_pool(p_lat[..., OFF_POOL:OFF_FFT], w_pool, s_pool)
    fft_l = fourier_mix(p_lat[..., OFF_FFT:OFF_GATE])
    out_lat = gated_merge(attn_l, pool_l, fft_l, p_lat[..., OFF_GATE:] + b_gate,
                          w_oa, w_ob, w_oc, w_out)
    if not with_ctx_out:
        return out_lat, None
    p_ctx_q = h_ctx @ w_in[:, OFF_Q:OFF_KV]
    p_ctx_rest = h_ctx @ w_in[:, OFF_POOL:]
    qc_nope, qc_rope = mla_queries(p_ctx_q, g_q, w_uq)
    attn_c = attend(qc_nope, qc_rope, k_nope_c, k_rope_c, v_c)
    pool_c = multiscale_pool(p_ctx_rest[..., :POOL_W], w_pool, s_pool)
    fft_c = fourier_mix(p_ctx_rest[..., POOL_W:POOL_W + FFT_W])
    out_ctx = gated_merge(attn_c, pool_c, fft_c, p_ctx_rest[..., POOL_W + FFT_W:] + b_gate,
                          w_oa, w_ob, w_oc, w_out)
    return out_lat, out_ctx

def swiglu(h, w1, w3, w2):
    return (jax.nn.silu(h @ w1) * (h @ w3)) @ w2

def moe_swiglu(h, w_router, b_router, w1, w3, w2):
    logits = (h @ w_router).astype(jnp.float32) + b_router.astype(jnp.float32)
    top_v, top_i = lax.top_k(logits, TOP_K)
    top_w = jax.nn.softmax(top_v, axis=-1)
    combine = jnp.sum(jax.nn.one_hot(top_i, N_EXPERTS, dtype=jnp.float32) * top_w[..., None],
                      axis=-2).astype(h.dtype)
    out = jnp.zeros_like(h)
    for e in range(N_EXPERTS):
        out = out + combine[..., e:e + 1] * swiglu(h, w1[e], w3[e], w2[e])
    return out

def setup_inputs(seed: int = 0) -> dict:
    key = jax.random.key(seed)
    ks = iter(jax.random.split(key, 40))
    D = D_MODEL

    def nrm(shape, scale):
        return jax.random.normal(next(ks), shape, jnp.float32) * scale

    def gain(shape):
        return 1.0 + nrm(shape, 0.02)

    return {
        'x': nrm((BATCH, SEQ, D), 1.0),
        'c': nrm((BATCH, D), 1.0),
        'ctx': nrm((BATCH, CTX_LEN, D), 1.0),
        'c_ctx': nrm((D,), 1.0),
        'w_mod': nrm((DEPTH, D, 6 * D), 0.5 * D ** -0.5),
        'b_mod': nrm((DEPTH, 6 * D), 0.02),
        'g_norm1': gain((DEPTH, D)),
        'w_in': nrm((DEPTH, D, IN_COLS), D ** -0.5),
        'b_gate': nrm((DEPTH, N_BRANCH * D), 0.02),
        'g_q': gain((DEPTH, Q_LORA)),
        'w_uq': nrm((DEPTH, Q_LORA, N_HEADS, QK_DIM), Q_LORA ** -0.5),
        'g_kv': gain((DEPTH, KV_LORA)),
        'w_ukv': nrm((DEPTH, KV_LORA, N_HEADS, QK_NOPE + V_DIM), KV_LORA ** -0.5),
        'w_pool': nrm((DEPTH, POOL_GROUPS, POOL_GC, POOL_GC), POOL_GC ** -0.5),
        's_pool': 1.0 + nrm((DEPTH, POOL_W), 0.1),
        'w_oa': nrm((DEPTH, ATTN_W, D), ATTN_W ** -0.5),
        'w_ob': nrm((DEPTH, POOL_W, D), POOL_W ** -0.5),
        'w_oc': nrm((DEPTH, FFT_W, D), FFT_W ** -0.5),
        'w_out': nrm((DEPTH, D, D), D ** -0.5),
        'g_norm2': gain((DEPTH, D)),
        'ffn_w1': nrm((N_DENSE, D, D_FF), D ** -0.5),
        'ffn_w3': nrm((N_DENSE, D, D_FF), D ** -0.5),
        'ffn_w2': nrm((N_DENSE, D_FF, D), D_FF ** -0.5),
        'moe_router': nrm((N_MOE, D, N_EXPERTS), D ** -0.5),
        'moe_bias': nrm((N_MOE, N_EXPERTS), 0.01),
        'moe_w1': nrm((N_MOE, N_EXPERTS, D, D_FF_EXPERT), D ** -0.5),
        'moe_w3': nrm((N_MOE, N_EXPERTS, D, D_FF_EXPERT), D ** -0.5),
        'moe_w2': nrm((N_MOE, N_EXPERTS, D_FF_EXPERT, D), D_FF_EXPERT ** -0.5),
        'g_final': gain((D,)),
    }

def reference(x, c, ctx, c_ctx, w_mod, b_mod, g_norm1, w_in, b_gate, g_q, w_uq, g_kv, w_ukv,
              w_pool, s_pool, w_oa, w_ob, w_oc, w_out, g_norm2, ffn_w1, ffn_w3, ffn_w2,
              moe_router, moe_bias, moe_w1, moe_w3, moe_w2, g_final):
    B, L, D = x.shape
    n_ctx = ctx.shape[1]
    rows = L // GRID_W
    cos, sin = axial_rope_tables(rows, x.dtype)
    xc = ctx
    cond_lat = jax.nn.silu(c)
    cond_ctx = jax.nn.silu(c_ctx)
    for layer in range(DEPTH):
        last = layer == DEPTH - 1
        mod_l = (cond_lat @ w_mod[layer] + b_mod[layer])[:, None, :]
        sh1, sc1, gt1, sh2, sc2, gt2 = jnp.split(mod_l, 6, axis=-1)
        n_mc = 2 if last else 6
        mod_c = cond_ctx @ w_mod[layer][:, :n_mc * D] + b_mod[layer][:n_mc * D]
        mods_c = jnp.split(mod_c, n_mc)
        h_l = modulate(rmsnorm(x, g_norm1[layer]), sh1, sc1)
        h_c = modulate(rmsnorm(xc, g_norm1[layer]), mods_c[0], mods_c[1])
        out_l, out_c = token_mixer(h_l, h_c, w_in[layer], b_gate[layer], g_q[layer], w_uq[layer],
                                   g_kv[layer], w_ukv[layer], w_pool[layer], s_pool[layer],
                                   w_oa[layer], w_ob[layer], w_oc[layer], w_out[layer],
                                   cos, sin, not last)
        x = x + gt1 * out_l
        if not last:
            xc = xc + mods_c[2] * out_c
        h_l = modulate(rmsnorm(x, g_norm2[layer]), sh2, sc2)
        if last:
            h = h_l
        else:
            h_c = modulate(rmsnorm(xc, g_norm2[layer]), mods_c[3], mods_c[4])
            h = jnp.concatenate([h_c, h_l], axis=1)
        if layer % 2 == 0:
            y = swiglu(h, ffn_w1[layer // 2], ffn_w3[layer // 2], ffn_w2[layer // 2])
        else:
            y = moe_swiglu(h, moe_router[layer // 2], moe_bias[layer // 2],
                           moe_w1[layer // 2], moe_w3[layer // 2], moe_w2[layer // 2])
        if last:
            x = x + gt2 * y
        else:
            x = x + gt2 * y[:, n_ctx:]
            xc = xc + mods_c[5] * y[:, :n_ctx]
    return rmsnorm(x, g_final)


_drawn_inputs = setup_inputs


def setup_inputs(seed=0):
    import zlib

    import numpy as np

    out = dict(_drawn_inputs(seed))
    spreads = {}
    factors = {'ctx': 3.38,
     'g_norm1': 5.706,
     'b_gate': 8.0,
     'g_q': 8.0,
     'g_kv': 8.0,
     'g_norm2': 3.626,
     'moe_bias': 3.604,
     'g_final': 2.732}
    for name, (base, spread) in spreads.items():
        noise = np.random.default_rng([zlib.crc32(name.encode()), seed]).standard_normal(out[name].shape)
        drawn = base * np.exp(spread * noise) if base else spread * noise
        out[name] = __import__('jax').numpy.asarray(drawn.astype(out[name].dtype))
    for name, factor in factors.items():
        out[name] = (out[name] * factor).astype(out[name].dtype)
    return out
```

```python
import concourse.bass as bass
from concourse import mybir
from concourse.alu_op_type import AluOpType as ALU

ACT = mybir.ActivationFunctionType
F32 = mybir.dt.float32
F32R = mybir.dt.float32r
I32 = mybir.dt.int32
U32 = mybir.dt.uint32
AX = mybir.AxisListType.X

P = 128
D = 1024
KD = D // P
SEQ = 256
T = 2 * SEQ
DEPTH = 2
HEADS = 8
NOPE = 64
ROPE = 32
QK = NOPE + ROPE
VD = 64
Q_LORA = 384
KV_LORA = 256
KQ = Q_LORA // P
KKV = KV_LORA // P
SCALE = float(QK) ** -0.5
GROUPS = 4
PAD = 8
PW = SEQ + 2 * PAD
BRANCH_W = 512
KB = BRANCH_W // P
BRANCHES = 3
FF = 2816
NF = FF // P
EXPERTS = 8
EPS = 1e-6
MODS = 6 * KD

SPLIT_BLOCKS = 16
DIRECT_BLOCKS = 8
STAGE = 6
SPLIT = 3
DIRECT = 4
DENSE_SPLIT = 2

TILES = ["kv0", "kv1", "kr", "q0", "q1", "q2"] + [f"fft{g}" for g in range(GROUPS)] + [f"pool{g}" for g in range(GROUPS)]
NT = len(TILES)
UP_FIRST = 12
DOWN = [list(range(UP_FIRST)), list(range(UP_FIRST, NF))]
USLOTS = UP_FIRST

CW = 256
CHUNKS = FF // CW
UNITS = 3 * CHUNKS
PAIR = 2
SLOTS = 128


def expert_units():
    out = [("ga", 0), ("gb", 0)]
    for c in range(1, CHUNKS):
        out += [("ga", c), ("gb", c), ("w", c - 1)]
    return out + [("w", CHUNKS - 1)]


def split_stream():
    tiles = []
    for layer in range(DEPTH):
        tiles += [(("in", layer, j), KD) for j in range(NT)]
        tiles += [(("gate", layer, m), KD) for m in range(KD * BRANCHES)]
        tiles += [(("out", layer, j), KD) for j in range(KD)]
        if layer == 0:
            for half, ks in enumerate(DOWN):
                tiles += [((name, i), KD) for i in ks for name in ("upg", "upu")]
                tiles += [(("down", half, j), len(ks)) for j in range(KD)]
    return tiles


class Walk:

    def __init__(self):
        self.first, at, ends = {}, 0, set()
        for key, n in split_stream():
            self.first[key] = at
            at += n
            ends.add(at - 1)
            self.first[key + ("end",)] = at - 1
        self.blocks = at
        self.units = at // SPLIT_BLOCKS
        assert at % SPLIT_BLOCKS == 0
        ends |= {SPLIT_BLOCKS * (u + 1) - 1 for u in range(self.units)}
        self.marks = sorted(ends)
        self.number = {b: n + 1 for n, b in enumerate(self.marks)}

    def tile(self, *key):
        return self.number[self.first[key + ("end",)]]

    def unit(self, u):
        return self.number[SPLIT_BLOCKS * (u + 1) - 1]

    def units_up_to(self, *key):
        return self.first[key + ("end",)] // SPLIT_BLOCKS + 1


def direct_stream():
    out = [("mod", 0, j) for j in range(MODS)]
    for layer in range(DEPTH):
        out += [("pool", layer), ("v", layer)]
        out += [("head", layer, n) for n in range(HEADS // 2)]
        out += [("proj", layer, n) for n in range(KD * BRANCHES // 2)]
        if layer == 0:
            out += [("mod", 1, j) for j in range(MODS)]
    return out


_ITEMS = HEADS * T // P
FIRST_LAYER = {
    "in_evac": NT - 1, "kr": 4, "lsq": KKV + KQ, "lss": KKV + KQ, "lvar": 2, "lstd": 2, "lrstd": 2, "lnorm": KKV + KQ,
    "fa_full": 2 * GROUPS, "fg": 2 * GROUPS, "fb_full": 2 * GROUPS, "br_c": 2 * GROUPS,
    "pads": 1, "win": sum(g + 3 for g in range(GROUPS)), "mixed": GROUPS, "pool_full": GROUPS, "br_b": GROUPS,
    "v_full": T // P, "v_sb": T // P, "qk_full": HEADS, "qk_rows": 2 * HEADS, "q_rope": 3 * HEADS,
    "s_full": _ITEMS, "max": _ITEMS, "neg_max": _ITEMS, "prob": _ITEMS, "rden": _ITEMS, "pn": _ITEMS,
    "t_full": _ITEMS, "pT": _ITEMS, "pv": _ITEMS, "br_a": HEADS,
    "gate": KD * BRANCHES, "o_full": KD * BRANCHES, "o_used": KD * BRANCHES, "y_part": KD, "y_sum": KD,
    "y_hi": KD, "y_lo": KD, "x_mix": KD, "mods": 4,
}
_UNITS, _CHUNKS, _GATHERS = EXPERTS * UNITS, EXPERTS * CHUNKS, EXPERTS + 1
FIRST_PASS = {
    "e_in": 16 * _UNITS // STAGE, "e_hi_done": _UNITS, "e_lo_done": _UNITS, "e_used": _UNITS,
    "et": _CHUNKS, "em": _CHUNKS, "eu": _CHUNKS, "tr_full": _CHUNKS, "ehT_hi": _CHUNKS, "ehT_lo": _CHUNKS,
    "sel": 2 * _GATHERS, "ga_full": 4 * _GATHERS, "xg_hi": 2 * _GATHERS, "xg_lo": 2 * _GATHERS,
    "st_full": _GATHERS, "selT": _GATHERS, "w_slot": _GATHERS,
    "y_hi_e": 2 * EXPERTS, "y_lo_e": 2 * EXPERTS, "sc_full": 4 * EXPERTS, "x_add": KD * EXPERTS,
}


def load_order(walk, direct_at):
    out, seen = [], set()

    def add(item):
        if item not in seen:
            seen.add(item)
            out.append(item)

    def tile(*key):
        for u in range(walk.first[key] // SPLIT_BLOCKS, walk.first[key + ("end",)] // SPLIT_BLOCKS + 1):
            add(("s", u))

    def mods(layer, first, last):
        for j in range(first, last):
            add(("d", direct_at[("mod", layer, j)]))

    mods(0, 0, 2 * KD)
    for layer in range(DEPTH):
        for j in range(NT):
            tile("in", layer, j)
            if layer == 0:
                mods(0, 2 * KD + 2 * j, 2 * KD + 2 * j + 2)
        if layer == 0:
            mods(0, 2 * KD + 2 * NT, MODS)
        for m in range(2 * DENSE_SPLIT):
            tile("gate", layer, m)
        for key in [("pool", layer), ("v", layer)] + [("head", layer, n) for n in range(HEADS // 2)]:
            add(("d", direct_at[key]))
        for m in range(KD * BRANCHES):
            tile("gate", layer, m)
            add(("d", direct_at[("proj", layer, m // 2)]))
        for j in range(KD):
            tile("out", layer, j)
        if layer == 0:
            for half, ks in enumerate(DOWN):
                for i in ks:
                    tile("upg", i)
                    tile("upu", i)
                    mods(1, 2 * i, 2 * i + 2)
                for j in range(KD):
                    tile("down", half, j)
            mods(1, 2 * NF, MODS)
    assert len(out) == walk.units + len(direct_at)
    return out


def build(nc, A):
    walk = Walk()
    direct = direct_stream()
    direct_at = {key: n for n, key in enumerate(direct)}
    eunits = expert_units()

    base = -(-nc.sbuf_base // 32) * 32
    end = nc.sbuf_usable_end

    class Region:

        def __init__(self, at):
            self.at = at

        def take(self, name, shape, dtype=F32):
            size = 4
            for n in shape[1:]:
                size *= n
            t = nc.alloc_sbuf_tensor_at(name, shape, dtype, offset=self.at)
            self.at = -(-(self.at + size) // 32) * 32
            assert self.at <= end, (name, self.at - end)
            return t

    fixed = Region(base)
    xT = fixed.take("xT", [P, KD, T])
    ones = fixed.take("ones", [P, P])
    ident = fixed.take("ident", [P, P])
    iota = fixed.take("iota", [P, P])
    before = fixed.take("before", [P, P])
    cond_in = fixed.take("cond_in", [P, KD, 2])
    cond_t = fixed.take("cond_t", [P, KD, 2])
    cond = fixed.take("cond", [P, KD, 2])
    mod = fixed.take("mod", [P, DEPTH, 2, MODS])
    b_mod = fixed.take("b_mod", [P, DEPTH, MODS])
    gains = fixed.take("gains", [P, 2 * DEPTH + 1, KD])
    coef = fixed.take("coef", [P, 2 * DEPTH, 2, KD])
    b_gate = fixed.take("b_gate", [P, DEPTH, BRANCHES * KD])
    half_b = fixed.take("half_b", [P, DEPTH, BRANCHES * KD])
    s_pool = fixed.take("s_pool", [P, DEPTH, GROUPS])
    g_q = fixed.take("g_q", [P, DEPTH, KQ])
    g_kv = fixed.take("g_kv", [P, DEPTH, KKV])
    router = fixed.take("router", [P, KD, EXPERTS])
    r_bias = fixed.take("r_bias", [P, EXPERTS])
    stat = fixed.take("stat", [P, 4, 4])
    phase = fixed.at

    dense = Region(phase)
    stage = dense.take("stage", [P, 3, SPLIT_BLOCKS * P])
    whi = dense.take("whi", [P, DENSE_SPLIT, SPLIT_BLOCKS, P], F32R)
    wlo = dense.take("wlo", [P, DENSE_SPLIT, SPLIT_BLOCKS, P], F32R)
    dw = dense.take("dw", [P, DIRECT, DIRECT_BLOCKS, P])
    h_hi = dense.take("h_hi", [P, KD, T], F32R)
    h_lo = dense.take("h_lo", [P, KD, T], F32R)
    rope = dense.take("rope", [P, T])
    dft_c = dense.take("dft_c", [P, 2 * P])
    dft_l = dense.take("dft_l", [P, 2, 2, SEQ])
    inv_n = dense.take("inv_n", [P, GROUPS, SEQ])
    free = dense.at
    mixer = Region(free)
    br = mixer.take("br", [P, BRANCHES, KB, T])
    late = Region(mixer.at)
    pkv = mixer.take("pkv", [P, KKV, T])
    pq = mixer.take("pq", [P, KQ, T])
    kT = mixer.take("kT", [P, 2, T])
    early = Region(mixer.at)
    pf = mixer.take("pf", [P, GROUPS, T])
    fg = mixer.take("fg", [P, 2, 2 * SEQ])
    pool_in = mixer.take("pool_in", [P, GROUPS, 2, PW])
    win = mixer.take("win", [P, 2, 2, PW])
    mixed = br
    v_sb = early.take("v_sb", [P, T // P, HEADS * VD])
    qT = early.take("qT", [P, 2, T])
    rt = early.take("rt", [P, T])
    prob = early.take("prob", [P, 3, T])
    pT = early.take("pT", [P, 2, T])
    yacc = late.take("yacc", [P, KD, T])
    gate = late.take("gate", [P, 2, T])
    gm = late.take("gm", [P, T])
    nr = Region(free)
    sq = nr.take("sq", [P, 2, T])
    var = nr.take("var", [P, T])
    std = nr.take("std", [P, T])
    rstd = nr.take("rstd", [P, T])
    nt = nr.take("nt", [P, 2, T])
    hf = nr.take("hf", [P, KD, SEQ])
    lr = Region(free)
    lsq = lr.take("lsq", [P, 2, T])
    lstd = lr.take("lstd", [P, 2, T])
    ff = Region(free)
    u_hi = ff.take("u_hi", [P, USLOTS, T], F32R)
    u_lo = ff.take("u_lo", [P, USLOTS, T], F32R)
    ft = ff.take("ft", [P, 2, T])
    fm = ff.take("fm", [P, T])
    fu = ff.take("fu", [P, 2, T])
    ex = Region(phase)
    estage = ex.take("estage", [P, STAGE, 4 * 512])
    ehi = ex.take("ehi", [P, SPLIT, 4 * 512], F32R)
    elo = ex.take("elo", [P, SPLIT, 4 * 512], F32R)
    htok = Region(max(ex.at, free + 5 * 2048 + 4096 + 8192))
    assert htok.at >= nr.at
    htok_hi = htok.take("htok_hi", [P, 2, D], F32R)
    htok_lo = htok.take("htok_lo", [P, 2, D], F32R)
    rt_logit = htok.take("rt_logit", [P, 2, EXPERTS])
    rt_top = htok.take("rt_top", [P, 2, 8])
    rt_index = htok.take("rt_index", [P, 2, 8], U32)
    rt_indexf = htok.take("rt_indexf", [P, 2, 8])
    rt_one = htok.take("rt_one", [P, 2, 2, EXPERTS])
    rt_w = htok.take("rt_w", [P, 2, 5])
    comb = htok.take("comb", [P, 2, 2 * EXPERTS])
    mask = htok.take("mask", [P, 2, EXPERTS])
    posm = htok.take("posm", [P, 2, 2, 2 * EXPERTS])
    most = htok.take("most", [P, 1])
    most_i = htok.take("most_i", [P, 1], I32)
    sel = htok.take("sel", [P, 2, SLOTS], F32R)
    selT = htok.take("selT", [P, 2, SEQ], F32R)
    w_slot = htok.take("w_slot", [P, 2])
    et = htok.take("et", [P, 2, CW])
    em = htok.take("em", [P, 2, CW])
    eu = htok.take("eu", [P, 2, CW])
    ehT_hi = htok.take("ehT_hi", [P, 2, 2, SLOTS], F32R)
    ehT_lo = htok.take("ehT_lo", [P, 2, 2, SLOTS], F32R)
    xg_hi = htok.take("xg_hi", [P, KD, SLOTS], F32R)
    xg_lo = htok.take("xg_lo", [P, KD, SLOTS], F32R)
    y_hi = htok.take("y_hi", [P, D], F32R)
    y_lo = htok.take("y_lo", [P, D], F32R)
    o_fin = nc.alloc_sbuf_tensor_at("o_fin", [P, KD, SEQ], F32, offset=nr.at)

    ps = [nc.alloc_psum_tensor(f"ps{b}", [P, 512], F32) for b in range(8)]

    def hslot(k, n):
        slots = KD * SEQ // n
        return hf[:, :, :].rearrange("p k t -> p (k t)")[:, (k % slots) * n:(k % slots) * n + n]

    sems = {}

    def S(name):
        if name not in sems:
            sems[name] = nc.alloc_semaphore(name)
        return sems[name]

    def direct_used(n):
        kind, layer, *rest = direct[n]
        if kind == "mod":
            return S("mod_tile"), MODS * layer + rest[0] + 1
        if kind == "pool":
            return S("pool_full"), earlier("pool_full", layer) + GROUPS
        if kind == "v":
            return S("v_full"), earlier("v_full", layer) + T // P
        if kind == "head":
            return S("qk_full"), earlier("qk_full", layer) + 2 * (rest[0] + 1)
        return S("o_full"), earlier("o_full", layer) + 2 * (rest[0] + 1)

    def c0(layer):
        return 0 if layer == 0 else SEQ

    def streams(layer):
        return (0, 1) if layer == 0 else (1,)

    def tile_c0(layer, j):
        return 0 if TILES[j] in ("kv0", "kv1", "kr") else c0(layer)

    def items(layer):
        tiles = range(4) if layer == 0 else (2, 3)
        return [(h, q, SEQ if q < 2 else T) for h in range(HEADS) for q in tiles]

    norms = [("n1_0", 0), ("n2_0", 0), ("n1_1", 0), ("n2_1", SEQ), ("fin", SEQ)]

    def earlier(name, layer):
        return FIRST_LAYER[name] if layer else 0

    def passed(name, p):
        return FIRST_PASS[name] * p

    def nth(tag):
        return [t for t, _ in norms].index(tag)

    def x_done(tag):
        return {
            "n1_0": (S("x_in"), 16), "n2_0": (S("x_mix"), KD), "n1_1": (S("x_ffn"), 2 * KD),
            "n2_1": (S("x_mix"), 2 * KD), "fin": None,
        }[tag]

    CONSTS = 17

    ctx_block = nc.Block()
    block = ctx_block.__enter__()

    @block.sync
    def _(sp):
        small = [
            (cond_in, A["cond"]), (ones, A["ones"]), (b_mod, A["b_mod"]), (gains, A["gains"]),
            (b_gate, A["b_gate"]), (s_pool, A["s_pool"]), (g_q, A["g_q"]), (g_kv, A["g_kv"]),
            (router, A["router"]), (r_bias, A["r_bias"]), (ident, A["ident"]), (iota, A["iota"]),
            (before, A["before"]), (rope, A["rope"]), (dft_c, A["dft_c"]), (dft_l, A["dft_l"]),
            (inv_n, A["inv_n"]),
        ]
        assert len(small) == CONSTS

        def load_small(t, a):
            full = tuple(slice(None) for _ in t.shape)
            return sp.dma_start(t[full], a)

        load_small(*small[0]).then_inc(S("cond_in"), 16)
        sp.dma_start(xT[:, :, :], A["x"]).then_inc(S("x_in"), 16)
        for t, a in small[1:]:
            load_small(t, a).then_inc(S("consts"), 16)

        def load_direct(n):
            if n >= DIRECT:
                s, v = direct_used(n - DIRECT)
                sp.wait_ge(s, v)
            sp.dma_start(dw[:, n % DIRECT, :, :], A["direct"][n]).then_inc(S(f"direct_in{n % DIRECT}"), 16)

        def load_split(u):
            if u >= 3:
                sp.wait_ge(S("lo_done"), u - 2)
            sp.dma_start(stage[:, u % 3, :], A["split"][u]).then_inc(S(f"split_in{u % 3}"), 16)

        for kind, n in load_order(walk, direct_at):
            if kind == "d":
                load_direct(n)
            else:
                load_split(n)

        def experts(p):
            with sp.Fori(0, EXPERTS // PAIR) as e2:
                for w in range(PAIR * UNITS):
                    sp.wait_ge(S("e_lo_done"), passed("e_lo_done", p) + e2 * (PAIR * UNITS) + (w + 1))
                    sp.dma_start(estage[:, w % STAGE, :],
                                 A["moe"][bass.ds(e2 * (PAIR * UNITS) + w, 1)].rearrange("a p n -> p (a n)"))\
                        .then_inc(S(f"e_in{w % STAGE}"), 16)

        experts(0)
        sp.wait_ge(S("most_ready"), 1)
        most_r = sp.value_load(most_i[0:1, 0:1], min_val=0, max_val=SEQ)
        with sp.If(most_r > SLOTS):
            experts(1)
        sp.wait_ge(S("out_ready"), KD)
        sp.dma_start(A["out"], o_fin[:, :, :]).then_inc(S("out_written"), 16)
        sp.wait_ge(S("out_written"), 16)

    @block.scalar
    def _(act):
        split_at = [0]

        def split_hi(upto):
            while split_at[0] < min(upto, walk.units):
                u = split_at[0]
                act.wait_ge(S(f"split_in{u % 3}"), 16 * (u // 3 + 1))
                if u >= DENSE_SPLIT:
                    act.wait_ge(S("walked"), walk.unit(u - DENSE_SPLIT))
                act.activation(whi[:, u % DENSE_SPLIT, :, :], stage[:, u % 3, :].rearrange("p (b c) -> p b c", c=P), ACT.Copy)\
                    .then_inc(S("hi_done"), 1)
                split_at[0] += 1

        def norm(tag, first):
            n = T - first
            for k in range(KD):
                if k == 0 and x_done(tag):
                    act.wait_ge(*x_done(tag))
                if k >= 2:
                    act.wait_ge(S("norm_ss"), KD * nth(tag) + k - 1)
                act.activation(sq[:, k % 2, 0:n], xT[:, k, first:T], ACT.Square).then_inc(S("norm_sq"), 1)
            act.wait_ge(S("norm_var"), 1 * nth(tag) + 1)
            act.activation(std[:, 0:n], var[:, 0:n], ACT.Sqrt).then_inc(S("norm_std"), 1)
            if tag == "fin":
                for k in range(KD):
                    act.wait_ge(S("norm_nt"), KD * nth("fin") + k + 1)
                    act.activation(o_fin[:, k, :], nt[:, k % 2, 0:n], ACT.Copy,
                                   scale=gains[:, 2 * DEPTH, k:k + 1]).then_inc(S("out_ready"), 1)
                return
            i = int(tag[1]) - 1
            layer = int(tag[3])
            parts = [(s, s * SEQ - first) for s in (0, 1) if s * SEQ >= first]
            slots = KD * SEQ // n

            def hi(k):
                act.wait_ge(S("norm_hf"), 2 * KD * nth(tag) + len(parts) * (k + 1))
                act.activation(h_hi[:, k, first:T], hslot(k, n), ACT.Copy).then_inc(S("norm_hhi"), 1)

            act.wait_ge(S("norm_coef"), 2 * nth(tag) + 2)
            for k in range(KD):
                act.wait_ge(S("norm_nt"), KD * nth(tag) + k + 1)
                if k >= slots:
                    act.wait_ge(S("norm_hlo"), KD * nth(tag) + k - slots + 1)
                for s, at in parts:
                    act.activation(hslot(k, n)[:, at:at + SEQ], nt[:, k % 2, at:at + SEQ], ACT.Identity,
                                   bias=mod[:, layer, s, 3 * i * KD + k:3 * i * KD + k + 1],
                                   scale=coef[:, 2 * layer + i, s, k:k + 1]).then_inc(S("norm_hf"), 1)
                if k >= 1:
                    hi(k - 1)
            hi(KD - 1)

        act.wait_ge(S("cond_in"), 16)
        act.activation(cond_t[:, :, :], cond_in[:, :, :], ACT.Tanh, scale=0.5).then_inc(S("cond_t"), 1)

        for layer in range(DEPTH):
            lc = c0(layer)
            norm(f"n1_{layer}", 0)
            for j, name in enumerate(TILES):
                split_hi(walk.units_up_to("in", layer, j) + 1)
                if name == "kr":
                    continue
                a = tile_c0(layer, j)
                act.wait_ge(S("walked"), walk.tile("in", layer, j))
                src = ps[j % 2][:, 0:T - a]
                if name.startswith("kv"):
                    dst = pkv[:, int(name[2]), a:T]
                elif name.startswith("q"):
                    dst = pq[:, int(name[1]), a:T]
                elif name.startswith("fft"):
                    dst = pf[:, int(name[3]), a:T]
                else:
                    if name == "pool0":
                        act.wait_ge(S("pads"), earlier("pads", layer) + 1)
                    dst = pool_in[:, int(name[4]), a // SEQ:2, PAD:PAD + SEQ]
                    src = src.rearrange("p (s t) -> p s t", t=SEQ)
                act.activation(dst, src, ACT.Copy).then_inc(S("in_evac"), 1)
                if name == "q2":
                    for i in range(KKV + KQ):
                        s0 = 0 if i < KKV else lc
                        if i == 0:
                            act.wait_ge(S("in_evac"), earlier("in_evac", layer) + 5)
                        if i >= 2:
                            act.wait_ge(S("lss"), earlier("lss", layer) + i - 1)
                        rows = pkv[:, i, :] if i < KKV else pq[:, i - KKV, s0:T]
                        act.activation(lsq[:, i % 2, s0:T], rows, ACT.Square).then_inc(S("lsq"), 1)
                if name == "fft1":
                    for i in range(2):
                        act.wait_ge(S("lvar"), earlier("lvar", layer) + i + 1)
                        s0 = (0, lc)[i]
                        act.activation(lstd[:, i, s0:T], lstd[:, i, s0:T], ACT.Sqrt).then_inc(S("lstd"), 1)
            for n in range(GROUPS * len(streams(layer))):
                act.wait_ge(S("fa_full"), earlier("fa_full", layer) + n + 1)
                if n >= 2:
                    act.wait_ge(S("fb_full"), earlier("fb_full", layer) + n - 1)
                act.activation(fg[:, n % 2, :], ps[2 + n % 2][:, :], ACT.Copy).then_inc(S("fg"), 1)
            for g in range(GROUPS):
                act.wait_ge(S("pool_full"), earlier("pool_full", layer) + g + 1)
                act.activation(br[:, 1, g, lc:T], ps[4 + g % 2][:, 0:T - lc], ACT.Copy,
                               scale=s_pool[:, layer, g:g + 1]).then_inc(S("br_b"), 1)
            for t in range(T // P):
                act.wait_ge(S("v_full"), earlier("v_full", layer) + t + 1)
                act.activation(v_sb[:, t, :], ps[2 + t % 2][:, :], ACT.Copy).then_inc(S("v_sb"), 1)

            todo = items(layer)
            per = len(todo) // HEADS

            def head_rows(h):
                act.wait_ge(S("qk_full"), earlier("qk_full", layer) + h + 1)
                act.activation(qT[0:NOPE, h % 2, lc:T], ps[0][0:NOPE, 0:T - lc], ACT.Copy).then_inc(S("qk_rows"), 1)
                act.activation(kT[0:NOPE, h % 2, :], ps[1][0:NOPE, :], ACT.Copy).then_inc(S("qk_rows"), 1)

            def exps(n):
                _, _, keys = todo[n]
                act.wait_ge(S("neg_max"), earlier("neg_max", layer) + n + 1)
                if n >= 3:
                    act.wait_ge(S("t_full"), earlier("t_full", layer) + n - 2)
                act.activation(prob[:, n % 3, 0:keys], ps[2 + n % 2][:, 0:keys], ACT.Exp, scale=SCALE,
                               bias=stat[:, 1, n % 4:n % 4 + 1], accum_out=stat[:, 2, n % 4:n % 4 + 1])\
                    .then_inc(S("prob"), 1)

            def probs_t(n):
                _, _, keys = todo[n]
                act.wait_ge(S("t_full"), earlier("t_full", layer) + n + 1)
                if n >= 2:
                    act.wait_ge(S("pv"), earlier("pv", layer) + n - 1)
                act.activation(pT[:, n % 2, 0:keys], ps[4 + n % 2][:, 0:keys], ACT.Copy).then_inc(S("pT"), 1)

            head_rows(0)
            for n in range(len(todo) + 2):
                if n < len(todo):
                    exps(n)
                    if n % per == 0 and todo[n][0] + 1 < HEADS:
                        head_rows(todo[n][0] + 1)
                if n >= 2:
                    probs_t(n - 2)

            for m in range(KD * BRANCHES):
                split_hi(walk.units_up_to("gate", layer, m) + 1)
                j, b = divmod(m, BRANCHES)
                act.wait_ge(S("walked"), walk.tile("gate", layer, m))
                if m >= 2:
                    act.wait_ge(S("o_used"), earlier("o_used", layer) + m - 1)
                if m == 0:
                    act.wait_ge(S("br_a"), earlier("br_a", layer) + HEADS)
                    act.wait_ge(S("half_b"), 1)
                act.activation(gate[:, m % 2, 0:T - lc], ps[m % 2][:, 0:T - lc], ACT.Tanh, scale=0.5,
                               bias=half_b[:, layer, b * KD + j:b * KD + j + 1]).then_inc(S("gate"), 1)
            for j in range(KD):
                act.wait_ge(S("y_sum"), earlier("y_sum", layer) + j + 1)
                if j == 0:
                    act.wait_ge(S("walked"), walk.tile("gate", layer, KD * BRANCHES - 1))
                act.activation(h_hi[:, j, lc:T], yacc[:, j, lc:T], ACT.Copy, scale=0.5).then_inc(S("y_hi"), 1)
            for j in range(KD):
                split_hi(walk.units_up_to("out", layer, j) + 1)
            norm(f"n2_{layer}", lc)
            if layer == 0:
                def hidden_hi(i):
                    act.wait_ge(S("fu"), i + 1)
                    if i >= USLOTS:
                        act.wait_ge(S("walked"), walk.tile("down", 0, KD - 1))
                    act.activation(u_hi[:, i % USLOTS, :], fu[:, i % 2, :], ACT.Copy).then_inc(S("u_hi"), 1)

                for half, ks in enumerate(DOWN):
                    for i in ks:
                        split_hi(walk.units_up_to("upu", i) + 1)
                        act.wait_ge(S("walked"), walk.tile("upg", i))
                        if i == 0:
                            act.wait_ge(S("norm_hlo"), KD * nth("n2_0") + KD)
                        if i >= 2:
                            act.wait_ge(S("fm"), i - 1)
                        act.activation(ft[:, i % 2, :], ps[i % 2][:, :], ACT.Tanh, scale=0.5).then_inc(S("ft"), 1)
                        split_hi(walk.units_up_to("upu", i) + 2)
                        hidden_hi(i)
                    for j in range(KD):
                        split_hi(walk.units_up_to("down", half, j) + 1)

        for n in range(8):
            act.wait_ge(S("ht_full"), n + 1)
            dst = (htok_hi, htok_lo)[n // 4]
            act.activation(dst[:, n // 2 % 2, n % 2 * 512:n % 2 * 512 + 512], ps[n % 2][:, :], ACT.Copy).then_inc(S("htok"), 1)
        act.wait_ge(S("rt_diff"), 2)
        act.activation(rt_w[:, :, 1], rt_w[:, :, 0], ACT.Exp).then_inc(S("rt_exp"), 1)

        def experts(p):
            used = S("e_used")
            act.wait_ge(S("ht_full"), 8)
            if p == 1:
                act.wait_ge(S("x_add"), KD * (EXPERTS + 1))
            else:
                act.sem_inc(used, SPLIT)

            def hi(v0, w):
                act.wait_ge(S(f"e_in{w % STAGE}"), passed("e_in", p) + v0 * 16 + 16 * (w // STAGE + 1))
                act.wait_ge(used, passed("e_used", p) + v0 * STAGE + (w + 1))
                act.activation(ehi[:, w % SPLIT, :], estage[:, w % STAGE, :], ACT.Copy).then_inc(S("e_hi_done"), 1)

            def gathered(e, x):
                for f in range(2):
                    act.wait_ge(S("ga_full"), passed("ga_full", p) + e * 4 + (4 * x + f + 1))
                    act.activation(xg_hi[:, 4 * f:4 * f + 4, :], ps[5 + f][:, :].rearrange("p (k s) -> p k s", s=SLOTS), ACT.Copy)\
                        .then_inc(S("xg_hi"), 1)
                act.wait_ge(S("st_full"), passed("st_full", p) + e + (x + 1))
                act.activation(selT[:, x % 2, :], ps[7][:, 0:SEQ], ACT.Copy).then_inc(S("selT"), 1)
                act.activation(w_slot[:, x % 2:x % 2 + 1], ps[7][:, SEQ:SEQ + 1], ACT.Copy).then_inc(S("w_slot"), 1)

            gathered(0, 0)
            with act.Fori(0, EXPERTS // PAIR) as e2:
                e = e2 * PAIR
                v0 = e2 * (PAIR * UNITS // STAGE)
                c_ = e2 * (PAIR * CHUNKS)
                for w in range(SPLIT):
                    hi(v0, w)
                for w in range(PAIR * UNITS):
                    x, k = divmod(w, UNITS)
                    kind, c = eunits[k]
                    cc = x * CHUNKS + c
                    if kind == "gb":
                        act.wait_ge(used, passed("e_used", p) + v0 * STAGE + (SPLIT + w + 1))
                        act.activation(et[:, cc % 2, :], ps[cc % 2][:, 0:CW], ACT.Tanh, scale=0.5).then_inc(S("et"), 1)
                    if (kind == "ga" and c >= 1) or (kind == "w" and c == CHUNKS - 1):
                        pc = x * CHUNKS + (c - 1 if kind == "ga" else c)
                        act.wait_ge(S("tr_full"), passed("tr_full", p) + c_ + (pc + 1))
                        act.activation(ehT_hi[:, pc % 2, :, :], ps[2][:, pc % 2 * 256:pc % 2 * 256 + 256].rearrange("p (b s) -> p b s", s=SLOTS), ACT.Copy)\
                            .then_inc(S("ehT_hi"), 1)
                    if w + SPLIT < PAIR * UNITS:
                        hi(v0, w + SPLIT)
                    if k == UNITS - 1:
                        act.wait_ge(used, passed("e_used", p) + v0 * STAGE + (SPLIT + w + 1))
                        act.wait_ge(S("w_slot"), passed("w_slot", p) + e + (x + 1))
                        act.wait_ge(S("sc_full"), passed("sc_full", p) + e * 4 + 4 * (x + 1))
                        for f in range(2):
                            act.activation(y_hi[:, f * 512:f * 512 + 512], ps[3 + f][:, :], ACT.Copy,
                                           scale=w_slot[:, x % 2:x % 2 + 1]).then_inc(S("y_hi_e"), 1)
                        gathered(e, x + 1)

        experts(0)
        act.wait_ge(S("most_ready"), 1)
        most_r = act.value_load(most_i[0:1, 0:1], min_val=0, max_val=SEQ)
        with act.If(most_r > SLOTS):
            experts(1)
        act.wait_ge(S("experts_done"), 1)
        norm("fin", SEQ)

    @block.vector
    def _(dve):
        split_at = [0]

        def split_lo(upto):
            while split_at[0] < min(upto, walk.units):
                u = split_at[0]
                dve.wait_ge(S("hi_done"), u + 1)
                dve.tensor_tensor(wlo[:, u % DENSE_SPLIT, :, :], stage[:, u % 3, :].rearrange("p (b c) -> p b c", c=P),
                                  whi[:, u % DENSE_SPLIT, :, :], ALU.subtract).then_inc(S("lo_done"), 1)
                split_at[0] += 1

        def norm(tag, first):
            n = T - first
            dve.wait_ge(S("norm_ss"), KD * nth(tag) + KD)
            dve.tensor_scalar(var[:, 0:n], ps[6][:, 0:n], 1.0 / D, EPS, ALU.mult, ALU.add).then_inc(S("norm_var"), 1)
            dve.wait_ge(S("norm_std"), 1 * nth(tag) + 1)
            dve.reciprocal(rstd[:, 0:n], std[:, 0:n]).then_inc(S("norm_rstd"), 1)
            dve.wait_ge(S("norm_rstd"), 1 * nth(tag) + 1)

            def lo(k):
                dve.wait_ge(S("norm_hhi"), KD * nth(tag) + k + 1)
                dve.tensor_tensor(h_lo[:, k, first:T], hslot(k, n), h_hi[:, k, first:T], ALU.subtract)\
                    .then_inc(S("norm_hlo"), 1)

            parts = 2 if first == 0 else 1
            for k in range(KD):
                if k >= 2:
                    if tag == "fin":
                        dve.wait_ge(S("out_ready"), k - 1)
                    else:
                        dve.wait_ge(S("norm_hf"), 2 * KD * nth(tag) + parts * (k - 1))
                dve.tensor_tensor(nt[:, k % 2, 0:n], xT[:, k, first:T], rstd[:, 0:n], ALU.mult).then_inc(S("norm_nt"), 1)
                if k >= 2 and tag != "fin":
                    lo(k - 2)
            if tag != "fin":
                lo(KD - 2)
                lo(KD - 1)

        def coefs(layer, i):
            for s in (0, 1):
                at = (3 * i + 1) * KD
                dve.scalar_tensor_tensor(coef[:, 2 * layer + i, s, :], mod[:, layer, s, at:at + KD], 1.0,
                                         gains[:, 2 * layer + i, :], ALU.add, ALU.mult)\
                    .then_inc(S("norm_coef"), 1)

        def mods(layer, first, last):
            dve.wait_ge(S("mod_tile"), MODS * layer + last)
            rows = ps[7][:, 0:2 * MODS].rearrange("p (j s) -> p j s", s=2)
            for s in (0, 1):
                dve.tensor_tensor(mod[:, layer, s, first:last], rows[:, first:last, s], b_mod[:, layer, first:last],
                                  ALU.add).then_inc(S("mods"), 1)

        dve.wait_ge(S("cond_t"), 1)
        dve.scalar_tensor_tensor(cond[:, :, :], cond_t[:, :, :], 1.0, cond_in[:, :, :], ALU.add, ALU.mult)\
            .then_inc(S("cond"), 1)
        dve.wait_ge(S("cond"), 1)
        dve.tensor_scalar(cond_t[:, :, :], cond[:, :, :], 0.5, None, ALU.mult).then_inc(S("cond"), 1)
        dve.wait_ge(S("consts"), 16 * (CONSTS - 1))
        dve.tensor_scalar(half_b[:, :, :], b_gate[:, :, :], 0.5, None, ALU.mult).then_inc(S("half_b"), 1)
        mods(0, 0, 2 * KD)
        dve.wait_ge(S("mods"), 2)
        coefs(0, 0)

        for layer in range(DEPTH):
            lc = c0(layer)
            norm(f"n1_{layer}", 0)
            for j, name in enumerate(TILES):
                split_lo(walk.units_up_to("in", layer, j) + 1)
                if name == "kr":
                    dve.wait_ge(S("walked"), walk.tile("in", layer, j))
                    dve.tensor_tensor(kT[64:96, 0, :], ps[j % 2][64:96, :], rope[64:96, :], ALU.mult)\
                        .then_inc(S("kr"), 1)
                    dve.tensor_tensor(kT[64:96, 1, :], ps[j % 2][96:128, :], rope[96:128, :], ALU.mult)\
                        .then_inc(S("kr"), 1)
                    dve.wait_ge(S("kr"), earlier("kr", layer) + 2)
                    dve.tensor_tensor(kT[64:96, 0, :], kT[64:96, 0, :], kT[64:96, 1, :], ALU.add)\
                        .then_inc(S("kr"), 1)
                    dve.wait_ge(S("kr"), earlier("kr", layer) + 3)
                    dve.tensor_copy(kT[64:96, 1, :], kT[64:96, 0, :]).then_inc(S("kr"), 1)
                if name == "fft1":
                    for i, width in enumerate((KV_LORA, Q_LORA)):
                        s0 = (0, lc)[i]
                        dve.wait_ge(S("lss"), earlier("lss", layer) + (KKV, KKV + KQ)[i])
                        dve.tensor_scalar(lstd[:, i, s0:T], ps[(6, 2)[i]][:, s0:T], 1.0 / width, EPS, ALU.mult, ALU.add)\
                            .then_inc(S("lvar"), 1)
                if name == "fft2":
                    for i in range(2):
                        s0 = (0, lc)[i]
                        dve.wait_ge(S("lstd"), earlier("lstd", layer) + i + 1)
                        dve.reciprocal(lstd[:, i, s0:T], lstd[:, i, s0:T]).then_inc(S("lrstd"), 1)
                    dve.wait_ge(S("in_evac"), earlier("in_evac", layer) + 5)
                    for i in range(KKV + KQ):
                        s0 = 0 if i < KKV else lc
                        rows = pkv[:, i, :] if i < KKV else pq[:, i - KKV, s0:T]
                        gain = g_kv[:, layer, i:i + 1] if i < KKV else g_q[:, layer, i - KKV:i - KKV + 1]
                        if i in (0, KKV):
                            dve.wait_ge(S("lrstd"), earlier("lrstd", layer) + (1 if i == 0 else 2))
                        dve.scalar_tensor_tensor(rows, rows, gain, lstd[:, 0 if i < KKV else 1, s0:T], ALU.mult, ALU.mult)\
                            .then_inc(S("lnorm"), 1)
            if layer == 0:
                mods(0, 2 * KD, MODS)
                dve.wait_ge(S("mods"), 4)
                coefs(0, 1)
            n = 0
            for s in streams(layer):
                for g in range(GROUPS):
                    dve.wait_ge(S("fb_full"), earlier("fb_full", layer) + n + 1)
                    if n == 0:
                        dve.wait_ge(S("lnorm"), earlier("lnorm", layer) + KKV + KQ)
                    dve.tensor_copy(br[:, 2, g, s * SEQ:(s + 1) * SEQ], ps[4 + n % 2][:, 0:SEQ]).then_inc(S("br_c"), 1)
                    n += 1
            todo = items(layer)
            per = len(todo) // HEADS

            def head_rope(h):
                dve.wait_ge(S("qk_full"), earlier("qk_full", layer) + h + 1)
                dve.tensor_tensor(qT[64:96, h % 2, lc:T], ps[0][64:96, 0:T - lc], rope[64:96, lc:T], ALU.mult)\
                    .then_inc(S("q_rope"), 1)
                if h >= 1:
                    dve.wait_ge(S("q_rope"), earlier("q_rope", layer) + 3 * h)
                dve.tensor_tensor(rt[64:96, lc:T], ps[0][96:128, 0:T - lc], rope[96:128, lc:T], ALU.mult)\
                    .then_inc(S("q_rope"), 1)
                dve.wait_ge(S("q_rope"), earlier("q_rope", layer) + 3 * h + 2)
                dve.tensor_tensor(qT[64:96, h % 2, lc:T], qT[64:96, h % 2, lc:T], rt[64:96, lc:T], ALU.add)\
                    .then_inc(S("q_rope"), 1)

            def row_max(n):
                _, _, keys = todo[n]
                dve.wait_ge(S("s_full"), earlier("s_full", layer) + n + 1)
                dve.tensor_reduce(stat[:, 0, n % 4:n % 4 + 1], ps[2 + n % 2][:, 0:keys], AX, ALU.max).then_inc(S("max"), 1)
                dve.wait_ge(S("max"), earlier("max", layer) + n + 1)
                dve.tensor_scalar(stat[:, 1, n % 4:n % 4 + 1], stat[:, 0, n % 4:n % 4 + 1], -SCALE, None, ALU.mult)\
                    .then_inc(S("neg_max"), 1)

            def normalise(n):
                _, _, keys = todo[n]
                dve.wait_ge(S("prob"), earlier("prob", layer) + n + 1)
                dve.reciprocal(stat[:, 3, n % 4:n % 4 + 1], stat[:, 2, n % 4:n % 4 + 1]).then_inc(S("rden"), 1)
                dve.wait_ge(S("rden"), earlier("rden", layer) + n + 1)
                dve.tensor_scalar(prob[:, n % 3, 0:keys], prob[:, n % 3, 0:keys], stat[:, 3, n % 4:n % 4 + 1], None, ALU.mult)\
                    .then_inc(S("pn"), 1)

            def head_out(h):
                dve.wait_ge(S("pv"), earlier("pv", layer) + per * (h + 1))
                if h == 0:
                    dve.wait_ge(S("pool_full"), earlier("pool_full", layer) + GROUPS)
                at = h % 2 * 64
                dve.tensor_copy(br[at:at + 64, 0, h // 2, lc:T], ps[6 + h % 2][0:64, lc:T]).then_inc(S("br_a"), 1)

            head_rope(0)
            for n in range(len(todo) + 3):
                if n < len(todo):
                    row_max(n)
                    if n % per == 0 and todo[n][0] + 1 < HEADS:
                        head_rope(todo[n][0] + 1)
                if 1 <= n <= len(todo):
                    normalise(n - 1)
                if n >= 3 and (n - 3) % per == per - 1:
                    head_out((n - 3) // per)
            for m in range(KD * BRANCHES):
                split_lo(walk.units_up_to("gate", layer, m) + 1)
                j, b = divmod(m, BRANCHES)
                dve.wait_ge(S("o_full"), earlier("o_full", layer) + m + 1)
                dve.wait_ge(S("gate"), earlier("gate", layer) + m + 1)
                o = ps[2 + m % 2][:, 0:T - lc]
                if b == 2:
                    dve.wait_ge(S("y_part"), earlier("y_part", layer) + j + 1)
                if b == 0:
                    dve.scalar_tensor_tensor(yacc[:, j, lc:T], gate[:, m % 2, 0:T - lc], 1.0, o, ALU.add, ALU.mult)\
                        .then_inc(S("o_used"), 1)
                else:
                    if b == 1 and j >= 1:
                        dve.wait_ge(S("y_sum"), earlier("y_sum", layer) + j)
                    dve.scalar_tensor_tensor(gm[:, 0:T - lc], gate[:, m % 2, 0:T - lc], 1.0, o, ALU.add, ALU.mult)\
                        .then_inc(S("o_used"), 1)
                    dve.wait_ge(S("o_used"), earlier("o_used", layer) + m + 1)
                    dve.tensor_tensor(yacc[:, j, lc:T], yacc[:, j, lc:T], gm[:, 0:T - lc], ALU.add)\
                        .then_inc(S("y_part" if b == 1 else "y_sum"), 1)
            for j in range(KD):
                dve.wait_ge(S("y_hi"), earlier("y_hi", layer) + j + 1)
                dve.scalar_tensor_tensor(h_lo[:, j, lc:T], yacc[:, j, lc:T], 0.5, h_hi[:, j, lc:T], ALU.mult, ALU.subtract)\
                    .then_inc(S("y_lo"), 1)
            for j in range(KD):
                split_lo(walk.units_up_to("out", layer, j) + 1)
                dve.wait_ge(S("walked"), walk.tile("out", layer, j))
                for s in streams(layer):
                    at = s * SEQ
                    ins = dve.scalar_tensor_tensor(xT[:, j, at:at + SEQ], ps[4 + j % 2][:, at - lc:at - lc + SEQ],
                                                   mod[:, layer, s, 2 * KD + j:2 * KD + j + 1],
                                                   xT[:, j, at:at + SEQ], ALU.mult, ALU.add)
                ins.then_inc(S("x_mix"), 1)
            norm(f"n2_{layer}", lc)
            if layer == 0:
                for half, ks in enumerate(DOWN):
                    for i in ks:
                        split_lo(walk.units_up_to("upu", i) + 1)
                        dve.wait_ge(S("ft"), i + 1)
                        if i >= 1:
                            dve.wait_ge(S("fu"), i)
                        dve.scalar_tensor_tensor(fm[:, :], ft[:, i % 2, :], 1.0, ps[i % 2][:, :], ALU.add, ALU.mult)\
                            .then_inc(S("fm"), 1)
                        dve.wait_ge(S("fm"), i + 1)
                        dve.wait_ge(S("walked"), walk.tile("upu", i))
                        if i >= 2:
                            dve.wait_ge(S("u_hi"), i - 1)
                        dve.scalar_tensor_tensor(fu[:, i % 2, :], fm[:, :], 0.5, ps[2 + i % 2][:, :], ALU.mult, ALU.mult)\
                            .then_inc(S("fu"), 1)
                        split_lo(walk.units_up_to("upu", i) + 2)
                        dve.wait_ge(S("u_hi"), i + 1)
                        dve.tensor_tensor(u_lo[:, i % USLOTS, :], fu[:, i % 2, :], u_hi[:, i % USLOTS, :], ALU.subtract)\
                            .then_inc(S("u_lo"), 1)
                    for j in range(KD):
                        split_lo(walk.units_up_to("down", half, j) + 1)
                        dve.wait_ge(S("walked"), walk.tile("down", half, j))
                        if half == 1:
                            dve.wait_ge(S("x_ffn"), j + 1)
                        for s in (0, 1):
                            at = s * SEQ
                            ins = dve.scalar_tensor_tensor(xT[:, j, at:at + SEQ], ps[4 + j % 2][:, at:at + SEQ],
                                                           mod[:, 0, s, 5 * KD + j:5 * KD + j + 1],
                                                           xT[:, j, at:at + SEQ], ALU.mult, ALU.add)
                        ins.then_inc(S("x_ffn"), 1)
                mods(1, 0, MODS)
                dve.wait_ge(S("mods"), earlier("mods", 1) + 2)
                coefs(1, 0)
                coefs(1, 1)

        chain = [0]

        def step(ins):
            chain[0] += 1
            ins.then_inc(S("rt_step"), 1)
            dve.wait_ge(S("rt_step"), chain[0])

        dve.wait_ge(S("lg_full"), 1)
        for t in range(2):
            step(dve.tensor_tensor(rt_logit[:, t, :], ps[7][:, t * 8:t * 8 + 8], r_bias[:, :], ALU.add))
            step(dve.max(rt_top[:, t, :], rt_logit[:, t, :]))
            step(dve.max_index(rt_index[:, t, :], rt_top[:, t, :], rt_logit[:, t, :]))
            step(dve.tensor_copy(rt_indexf[:, t, :], rt_index[:, t, :]))
            for r in range(2):
                step(dve.tensor_scalar(rt_one[:, t, r, :], iota[:, 0:EXPERTS], rt_indexf[:, t, r:r + 1], None, ALU.is_equal))
            dve.tensor_tensor(rt_w[:, t, 0:1], rt_top[:, t, 1:2], rt_top[:, t, 0:1], ALU.subtract).then_inc(S("rt_diff"), 1)
            dve.tensor_tensor(mask[:, t, :], rt_one[:, t, 0, :], rt_one[:, t, 1, :], ALU.add).then_inc(S("mask"), 1)
        dve.wait_ge(S("rt_exp"), 1)
        step(dve.memset(comb[:, :, :], 0.0))
        for t in range(2):
            step(dve.tensor_scalar(rt_w[:, t, 2:3], rt_w[:, t, 1:2], 1.0, None, ALU.add))
            step(dve.reciprocal(rt_w[:, t, 3:4], rt_w[:, t, 2:3]))
            step(dve.tensor_tensor(rt_w[:, t, 4:5], rt_w[:, t, 1:2], rt_w[:, t, 3:4], ALU.mult))
            step(dve.tensor_scalar(comb[:, t, 0:EXPERTS], rt_one[:, t, 0, :], rt_w[:, t, 3:4], None, ALU.mult))
            step(dve.scalar_tensor_tensor(comb[:, t, 0:EXPERTS], rt_one[:, t, 1, :], rt_w[:, t, 4:5], comb[:, t, 0:EXPERTS], ALU.mult, ALU.add))
        step(dve.memset(posm[:, :, :, :], -1.0))
        dve.wait_ge(S("cnt_full"), 1)
        for t in range(2):
            step(dve.scalar_tensor_tensor(posm[:, 0, t, 0:EXPERTS], ps[7][:, 32 + t * 8:40 + t * 8], 1.0, mask[:, t, :], ALU.add, ALU.mult))
            step(dve.tensor_scalar(posm[:, 0, t, 0:EXPERTS], posm[:, 0, t, 0:EXPERTS], 1.0, None, ALU.subtract))
            step(dve.tensor_scalar(posm[:, 1, t, 0:EXPERTS], posm[:, 0, t, 0:EXPERTS], float(SLOTS), None, ALU.subtract))
        step(dve.tensor_reduce(most[:, :], ps[7][:, 48:56], AX, ALU.max))
        dve.tensor_copy(most_i[:, :], most[:, :]).then_inc(S("most_ready"), 1)

        def experts(p):
            used = S("e_used")
            if p == 1:
                dve.wait_ge(S("x_add"), KD * (EXPERTS + 1))
            else:
                dve.wait_ge(S("ht_full"), 8)
                dve.sem_inc(S("e_lo_done"), STAGE)
                dve.sem_inc(S("x_add"), KD)

            def lo(v0, w):
                dve.wait_ge(S("e_hi_done"), passed("e_hi_done", p) + v0 * STAGE + (w + 1))
                dve.tensor_tensor(elo[:, w % SPLIT, :], estage[:, w % STAGE, :], ehi[:, w % SPLIT, :], ALU.subtract)\
                    .then_inc(S("e_lo_done"), 1)

            def select(e, x, read):
                if read:
                    dve.wait_ge(S("st_full"), passed("st_full", p) + e + x)
                for t in range(2):
                    at = posm[:, p, t, bass.ds(e + x, 1)] if read else posm[:, p, t, 0:1]
                    dve.tensor_scalar(sel[:, t, :], iota[:, :], at, None, ALU.is_equal).then_inc(S("sel"), 1)

            def gathered(e, x):
                for f in range(2):
                    dve.wait_ge(S("ga_full"), passed("ga_full", p) + e * 4 + (4 * x + f + 3))
                    dve.tensor_copy(xg_lo[:, 4 * f:4 * f + 4, :], ps[5 + f][:, :].rearrange("p (k s) -> p k s", s=SLOTS))\
                        .then_inc(S("xg_lo"), 1)

            select(0, 0, False)
            gathered(0, 0)
            with dve.Fori(0, EXPERTS // PAIR) as e2:
                e = e2 * PAIR
                v0 = e2 * (PAIR * UNITS // STAGE)
                c_ = e2 * (PAIR * CHUNKS)
                for w in range(SPLIT):
                    lo(v0, w)
                for w in range(PAIR * UNITS):
                    x, k = divmod(w, UNITS)
                    kind, c = eunits[k]
                    cc = x * CHUNKS + c
                    if kind == "gb":
                        dve.wait_ge(S("et"), passed("et", p) + c_ + (cc + 1))
                        dve.scalar_tensor_tensor(em[:, cc % 2, :], et[:, cc % 2, :], 1.0, ps[cc % 2][:, 0:CW], ALU.add, ALU.mult)\
                            .then_inc(S("em"), 1)
                        dve.wait_ge(S("em"), passed("em", p) + c_ + (cc + 1))
                        dve.scalar_tensor_tensor(eu[:, cc % 2, :], em[:, cc % 2, :], 0.5, ps[cc % 2][:, CW:2 * CW], ALU.mult, ALU.mult)\
                            .then_inc(S("eu"), 1)
                    if (kind == "ga" and c >= 1) or (kind == "w" and c == CHUNKS - 1):
                        pc = x * CHUNKS + (c - 1 if kind == "ga" else c)
                        dve.wait_ge(S("ehT_hi"), passed("ehT_hi", p) + c_ + (pc + 1))
                        dve.tensor_tensor(ehT_lo[:, pc % 2, :, :], ps[2][:, pc % 2 * 256:pc % 2 * 256 + 256].rearrange("p (b s) -> p b s", s=SLOTS),
                                          ehT_hi[:, pc % 2, :, :], ALU.subtract).then_inc(S("ehT_lo"), 1)
                    if w + SPLIT < PAIR * UNITS:
                        lo(v0, w + SPLIT)
                    if k == 6:
                        select(e, x + 1, True)
                    if k == UNITS - 1:
                        dve.wait_ge(S("w_slot"), passed("w_slot", p) + e + (x + 1))
                        for f in range(2):
                            dve.wait_ge(S("y_hi_e"), passed("y_hi_e", p) + e * 2 + (2 * x + f + 1))
                            dve.scalar_tensor_tensor(y_lo[:, f * 512:f * 512 + 512], ps[3 + f][:, :], w_slot[:, x % 2:x % 2 + 1],
                                                     y_hi[:, f * 512:f * 512 + 512], ALU.mult, ALU.subtract).then_inc(S("y_lo_e"), 1)
                        gathered(e, x + 1)
                        for k4 in range(KD // 2):
                            dve.wait_ge(S("sc_full"), passed("sc_full", p) + e * 4 + (4 * x + k4 + 5))
                            for i in range(2):
                                kk = 2 * k4 + i
                                dve.scalar_tensor_tensor(xT[:, kk, SEQ:T], ps[5 + k4 % 2][:, i * SEQ:(i + 1) * SEQ],
                                                         mod[:, 1, 1, 5 * KD + kk:5 * KD + kk + 1], xT[:, kk, SEQ:T],
                                                         ALU.mult, ALU.add).then_inc(S("x_add"), 1)

        experts(0)
        dve.wait_ge(S("x_add"), KD * (EXPERTS + 1))
        dve.wait_ge(S("most_ready"), 1)
        most_r = dve.value_load(most_i[0:1, 0:1], min_val=0, max_val=SEQ)
        with dve.If(most_r > SLOTS):
            experts(1)
            dve.wait_ge(S("x_add"), passed("x_add", 1) + KD * (EXPERTS + 1))
        dve.sem_inc(S("experts_done"), 1)
        norm("fin", SEQ)

    @block.gpsimd
    def _(pool):
        for layer in range(DEPTH):
            s0 = streams(layer)[0]
            lc = c0(layer)
            pool.wait_ge(S("norm_hlo"), KD * nth(f"n1_{layer}") + KD)
            pool.memset(pool_in[:, :, :, :], 0.0).then_inc(S("pads"), 1)
            n = [0]

            def step(ins):
                n[0] += 1
                ins.then_inc(S("win"), 1)
                pool.wait_ge(S("win"), earlier("win", layer) + n[0])

            for g in range(GROUPS):
                pool.wait_ge(S("in_evac"), earlier("in_evac", layer) + 5 + GROUPS + g + 1)
                rows = pool_in[:, g, s0:2, :]
                src = rows
                for a in range(g + 1):
                    reach = 1 << a
                    start = (2 << a) - 1
                    dst = win[:, a % 2, s0:2, :]
                    step(pool.tensor_tensor(dst[:, :, start:PW], src[:, :, start:PW], src[:, :, start - reach:PW - reach], ALU.add))
                    src = dst
                at = PAD + (1 << g) - 1
                dst = win[:, (g + 1) % 2, s0:2, 0:SEQ]
                for s in range(s0, 2):
                    step(pool.tensor_tensor(win[:, (g + 1) % 2, s, 0:SEQ], win[:, g % 2, s, at:at + SEQ], inv_n[:, g, :], ALU.mult))
                if g == 0:
                    pool.wait_ge(S("lnorm"), earlier("lnorm", layer) + KKV + KQ)
                pool.tensor_tensor(mixed[:, 0, g, lc:T].rearrange("p (s t) -> p s t", t=SEQ), dst, rows[:, :, PAD:PAD + SEQ], ALU.subtract)\
                    .then_inc(S("mixed"), 1)
                pool.wait_ge(S("mixed"), earlier("mixed", layer) + g + 1)

    @block.tensor
    def _(pe):
        at = [0]

        def block_passes(out, key, k, rhs_hi, rhs_lo, first, last):
            b = at[0]
            assert walk.first[key] + k == b or k < 0
            u, i = divmod(b, SPLIT_BLOCKS)
            if i == 0:
                pe.wait_ge(S("lo_done"), u + 1)
            hi, lo = whi[:, u % DENSE_SPLIT, i, :], wlo[:, u % DENSE_SPLIT, i, :]
            pe.matmul(out, hi, rhs_hi, start=first, stop=False)
            pe.matmul(out, hi, rhs_lo, start=False, stop=False)
            ins = pe.matmul(out, lo, rhs_hi, start=False, stop=last)
            if b in walk.number:
                ins.then_inc(S("walked"), 1)
            at[0] += 1
            return ins

        def direct_unit(key):
            n = direct_at[key]
            pe.wait_ge(S(f"direct_in{n % DIRECT}"), 16 * (n // DIRECT + 1))
            return n % DIRECT

        def mod_tiles(layer, first, last):
            for j in range(first, last):
                slot = direct_unit(("mod", layer, j))
                for k in range(KD):
                    ins = pe.matmul(ps[7][:, 2 * j:2 * j + 2], dw[:, slot, k, :], cond_t[:, k, :], start=(k == 0), stop=(k == KD - 1))
                ins.then_inc(S("mod_tile"), 1)

        def norm(tag, first):
            for k in range(KD):
                pe.wait_ge(S("norm_sq"), KD * nth(tag) + k + 1)
                pe.matmul(ps[6][:, 0:T - first], ones[:, :], sq[:, k % 2, 0:T - first], start=(k == 0), stop=(k == KD - 1))\
                    .then_inc(S("norm_ss"), 1)

        pe.wait_ge(S("cond"), 2)
        mod_tiles(0, 0, 2 * KD)
        pe.wait_ge(S("consts"), 16 * (CONSTS - 1))
        for layer in range(DEPTH):
            lc = c0(layer)
            norm(f"n1_{layer}", 0)
            for j, name in enumerate(TILES):
                a = tile_c0(layer, j)
                if j >= 2:
                    if TILES[j - 2] == "kr":
                        pe.wait_ge(S("kr"), earlier("kr", layer) + 2)
                    else:
                        pe.wait_ge(S("in_evac"), earlier("in_evac", layer) + j - 1 - (1 if j - 2 > 2 else 0))
                for k in range(KD):
                    if j == 0:
                        pe.wait_ge(S("norm_hlo"), KD * nth(f"n1_{layer}") + k + 1)
                    block_passes(ps[j % 2][:, 0:T - a], ("in", layer, j), k, h_hi[:, k, a:T], h_lo[:, k, a:T], k == 0, k == KD - 1)
                if name == "fft0":
                    for i in range(KKV + KQ):
                        s0 = 0 if i < KKV else lc
                        first, last = i in (0, KKV), i in (KKV - 1, KKV + KQ - 1)
                        pe.wait_ge(S("lsq"), earlier("lsq", layer) + i + 1)
                        pe.matmul(ps[6 if i < KKV else 2][:, s0:T], ones[:, :], lsq[:, i % 2, s0:T], start=first, stop=last)\
                            .then_inc(S("lss"), 1)
                if layer == 0:
                    mod_tiles(0, 2 * KD + 2 * j, 2 * KD + 2 * j + 2)
            if layer == 0:
                mod_tiles(0, 2 * KD + 2 * NT, MODS)

            todo = [(s, g) for s in streams(layer) for g in range(GROUPS)]

            def channels(n):
                s, g = todo[n]
                if n == 0:
                    pe.wait_ge(S("in_evac"), earlier("in_evac", layer) + 5 + GROUPS)
                    pe.wait_ge(S("lvar"), earlier("lvar", layer) + 2)
                if n >= 2:
                    pe.wait_ge(S("fg"), earlier("fg", layer) + n - 1)
                for t in range(2):
                    c = s * SEQ + t * P
                    ins = pe.matmul(ps[2 + n % 2][:, t * 256:t * 256 + 256], pf[:, g, c:c + P], dft_c[:, :], start=True, stop=True)
                ins.then_inc(S("fa_full"), 1)

            def tokens(n):
                pe.wait_ge(S("fg"), earlier("fg", layer) + n + 1)
                if n >= 2:
                    pe.wait_ge(S("br_c"), earlier("br_c", layer) + n - 1)
                for t in range(2):
                    for part in range(2):
                        c = t * 256 + part * P
                        ins = pe.matmul(ps[4 + n % 2][:, 0:SEQ], fg[:, n % 2, c:c + P], dft_l[:, t, part, :],
                                        start=(t == 0 and part == 0), stop=(t == 1 and part == 1))
                ins.then_inc(S("fb_full"), 1)

            channels(0)
            for n in range(len(todo)):
                if n + 1 < len(todo):
                    channels(n + 1)
                tokens(n)
            slot = direct_unit(("pool", layer))
            for g in range(GROUPS):
                pe.wait_ge(S("mixed"), earlier("mixed", layer) + g + 1)
                if g < 2:
                    pe.wait_ge(S("br_c"), earlier("br_c", layer) + len(todo))
                else:
                    pe.wait_ge(S("br_b"), earlier("br_b", layer) + g - 1)
                pe.matmul(ps[4 + g % 2][:, 0:T - lc], dw[:, slot, g, :], mixed[:, 0, g, lc:T], start=True, stop=True)\
                    .then_inc(S("pool_full"), 1)
            slot = direct_unit(("v", layer))
            pe.wait_ge(S("lnorm"), earlier("lnorm", layer) + KKV + KQ)
            pe.wait_ge(S("fg"), earlier("fg", layer) + len(todo))
            for t in range(T // P):
                if t >= 2:
                    pe.wait_ge(S("v_sb"), earlier("v_sb", layer) + t - 1)
                for i in range(KKV):
                    ins = pe.matmul(ps[2 + t % 2][:, :], pkv[:, i, t * P:(t + 1) * P],
                                    dw[:, slot, 4 * i:4 * i + 4, :].rearrange("p a b -> p (a b)"), start=(i == 0), stop=(i == KKV - 1))
                ins.then_inc(S("v_full"), 1)

            todo_a = items(layer)
            per = len(todo_a) // HEADS

            def head(h):
                slot = direct_unit(("head", layer, h // 2))
                if h == 0:
                    pe.wait_ge(S("in_evac"), earlier("in_evac", layer) + NT - 1)
                else:
                    pe.wait_ge(S("qk_rows"), earlier("qk_rows", layer) + 2 * h)
                    pe.wait_ge(S("q_rope"), earlier("q_rope", layer) + 3 * h)
                o = 4 * (h % 2)
                for i in range(KQ):
                    pe.matmul(ps[0][:, 0:T - lc], dw[:, slot, o + i, :], pq[:, i, lc:T], start=(i == 0), stop=(i == KQ - 1))
                for i in range(KKV):
                    ins = pe.matmul(ps[1][0:NOPE, :], dw[:, slot, o + 3, i * 64:i * 64 + 64], pkv[:, i, :], start=(i == 0), stop=(i == KKV - 1))
                ins.then_inc(S("qk_full"), 1)

            def scores(n):
                h, q, keys = todo_a[n]
                if n % per == 0:
                    pe.wait_ge(S("qk_rows"), earlier("qk_rows", layer) + 2 * h + 2)
                    pe.wait_ge(S("q_rope"), earlier("q_rope", layer) + 3 * h + 3)
                    pe.wait_ge(S("kr"), earlier("kr", layer) + 4)
                if n < 2:
                    pe.wait_ge(S("v_sb"), earlier("v_sb", layer) + T // P)
                else:
                    pe.wait_ge(S("prob"), earlier("prob", layer) + n - 1)
                pe.matmul(ps[2 + n % 2][:, 0:keys], qT[0:QK, h % 2, q * P:(q + 1) * P], kT[0:QK, h % 2, 0:keys], start=True, stop=True)\
                    .then_inc(S("s_full"), 1)

            def turn(n):
                _, _, keys = todo_a[n]
                pe.wait_ge(S("pn"), earlier("pn", layer) + n + 1)
                if n < 2:
                    pe.wait_ge(S("br_b"), earlier("br_b", layer) + GROUPS)
                else:
                    pe.wait_ge(S("pT"), earlier("pT", layer) + n - 1)
                for t in range(keys // P):
                    ins = pe.transpose(ps[4 + n % 2][:, t * P:(t + 1) * P], prob[:, n % 3, t * P:(t + 1) * P], ident[:, :])
                ins.then_inc(S("t_full"), 1)

            def values(n):
                h, q, keys = todo_a[n]
                pe.wait_ge(S("pT"), earlier("pT", layer) + n + 1)
                if n % per == 0:
                    if h < 2:
                        pe.wait_ge(S("mods"), 4)
                        pe.wait_ge(S("lvar"), earlier("lvar", layer) + 1)
                    else:
                        pe.wait_ge(S("br_a"), earlier("br_a", layer) + h - 1)
                for t in range(keys // P):
                    ins = pe.matmul(ps[6 + h % 2][0:64, q * P:(q + 1) * P], v_sb[:, t, h * VD:(h + 1) * VD],
                                    pT[:, n % 2, t * P:(t + 1) * P], start=(t == 0), stop=(t == keys // P - 1))
                ins.then_inc(S("pv"), 1)

            head(0)
            for n in range(len(todo_a) + 2):
                if n < len(todo_a):
                    scores(n)
                    if n % per == 0 and todo_a[n][0] + 1 < HEADS:
                        head(todo_a[n][0] + 1)
                if n >= 2:
                    turn(n - 2)
                    values(n - 2)

            for m in range(KD * BRANCHES):
                j, b = divmod(m, BRANCHES)
                if m < 2:
                    pe.wait_ge(S("qk_rows"), earlier("qk_rows", layer) + 2 * HEADS)
                    pe.wait_ge(S("q_rope"), earlier("q_rope", layer) + 3 * HEADS)
                else:
                    pe.wait_ge(S("gate"), earlier("gate", layer) + m - 1)
                for k in range(KD):
                    block_passes(ps[m % 2][:, 0:T - lc], ("gate", layer, m), k, h_hi[:, k, lc:T], h_lo[:, k, lc:T], k == 0, k == KD - 1)
                slot = direct_unit(("proj", layer, m // 2))
                if m < 2:
                    pe.wait_ge(S("prob"), earlier("prob", layer) + len(todo_a))
                    pe.wait_ge(S("br_a"), earlier("br_a", layer) + HEADS)
                else:
                    pe.wait_ge(S("o_used"), earlier("o_used", layer) + m - 1)
                for k in range(KB):
                    ins = pe.matmul(ps[2 + m % 2][:, 0:T - lc], dw[:, slot, 4 * (m % 2) + k, :], br[:, b, k, lc:T], start=(k == 0), stop=(k == KB - 1))
                ins.then_inc(S("o_full"), 1)
            for j in range(KD):
                if j < 2:
                    pe.wait_ge(S("pT"), earlier("pT", layer) + len(todo_a))
                else:
                    pe.wait_ge(S("x_mix"), earlier("x_mix", layer) + j - 1)
                for k in range(KD):
                    if j == 0:
                        pe.wait_ge(S("y_lo"), earlier("y_lo", layer) + k + 1)
                    block_passes(ps[4 + j % 2][:, 0:T - lc], ("out", layer, j), k, h_hi[:, k, lc:T], h_lo[:, k, lc:T], k == 0, k == KD - 1)
            norm(f"n2_{layer}", lc)
            if layer == 0:
                for half, ks in enumerate(DOWN):
                    for i in ks:
                        if i < 2:
                            pe.wait_ge(S("o_used"), KD * BRANCHES)
                        else:
                            pe.wait_ge(S("fu"), i - 1)
                        for w, key in enumerate(("upg", "upu")):
                            for k in range(KD):
                                if i == 0 and w == 0:
                                    pe.wait_ge(S("norm_hlo"), KD * nth("n2_0") + k + 1)
                                block_passes(ps[2 * w + i % 2][:, :], (key, i), k, h_hi[:, k, :], h_lo[:, k, :], k == 0, k == KD - 1)
                        if 2 * i < MODS:
                            mod_tiles(1, 2 * i, 2 * i + 2)
                    for j in range(KD):
                        if half == 0 and j < 2:
                            pe.wait_ge(S("x_mix"), KD)
                        else:
                            pe.wait_ge(S("x_ffn"), KD * half + j - 1)
                        if j == 0:
                            pe.wait_ge(S("u_lo"), ks[-1] + 1)
                        for n, i in enumerate(ks):
                            block_passes(ps[4 + j % 2][:, :], ("down", half, j), n, u_hi[:, i % USLOTS, :], u_lo[:, i % USLOTS, :], n == 0, n == len(ks) - 1)
                mod_tiles(1, 2 * NF, MODS)

        pe.wait_ge(S("norm_hhi"), KD * nth("n2_1") + KD)
        for t in range(2):
            for k in range(KD):
                ins = pe.matmul(ps[7][:, t * 8:t * 8 + 8], hslot(k, SEQ)[:, t * P:(t + 1) * P], router[:, k, :], start=(k == 0), stop=(k == KD - 1))
        ins.then_inc(S("lg_full"), 1)
        pe.wait_ge(S("norm_hlo"), KD * nth("n2_1") + KD)
        for n in range(8):
            part, t, f = n // 4, n // 2 % 2, n % 2
            if n >= 2:
                pe.wait_ge(S("htok"), n - 1)
            else:
                pe.wait_ge(S("gate"), earlier("gate", 1) + KD * BRANCHES)
            src = (h_hi, h_lo)[part][:, :, :].bitcast(F32)
            for i in range(4):
                ins = pe.transpose(ps[n % 2][:, i * P:(i + 1) * P], src[:, 4 * f + i, SEQ + t * P:SEQ + (t + 1) * P], ident[:, :])
            ins.then_inc(S("ht_full"), 1)
        pe.wait_ge(S("mask"), 2)
        pe.matmul(ps[7][:, 32:40], before[:, :], mask[:, 0, :], start=True, stop=True)
        pe.matmul(ps[7][:, 40:48], before[:, :], mask[:, 1, :], start=True, stop=False)
        pe.matmul(ps[7][:, 40:48], ones[:, :], mask[:, 0, :], start=False, stop=True)
        pe.matmul(ps[7][:, 48:56], ones[:, :], mask[:, 0, :], start=True, stop=False)
        pe.matmul(ps[7][:, 48:56], ones[:, :], mask[:, 1, :], start=False, stop=True).then_inc(S("cnt_full"), 1)
        pe.wait_ge(S("htok"), 8)
        pe.wait_ge(S("most_ready"), 1)

        def experts(p):
            used = S("e_used")
            if p == 1:
                pe.wait_ge(S("x_add"), KD * (EXPERTS + 1))
            else:
                pe.sem_inc(S("sc_full"), 4)
                pe.sem_inc(S("eu"), 2)
                pe.sem_inc(S("y_lo_e"), 2)

            def gather(e, x, first):
                for fill in range(4):
                    part, f = divmod(fill, 2)
                    if part == 0:
                        if fill == 0:
                            pe.wait_ge(S("sel"), passed("sel", p) + e * 2 + 2 * (x + 1))
                        if not first:
                            pe.wait_ge(S("x_add"), passed("x_add", p) + e * KD + KD * x)
                    else:
                        pe.wait_ge(S("xg_hi"), passed("xg_hi", p) + e * 2 + (2 * x + f + 1))
                    for k in range(4):
                        for t in range(2):
                            ins = pe.matmul(ps[5 + f][:, k * SLOTS:(k + 1) * SLOTS], (htok_hi, htok_lo)[part][:, t, (4 * f + k) * P:(4 * f + k + 1) * P],
                                            sel[:, t, :], start=(t == 0), stop=(t == 1))
                    ins.then_inc(S("ga_full"), 1)
                if not first:
                    pe.wait_ge(S("selT"), passed("selT", p) + e + x)
                    pe.wait_ge(S("w_slot"), passed("w_slot", p) + e + x)
                for t in range(2):
                    pe.transpose(ps[7][:, t * P:(t + 1) * P], sel[:, t, :].bitcast(F32), ident[:, :])
                for t in range(2):
                    at = comb[:, t, 0:1] if first else comb[:, t, bass.ds(e + x, 1)]
                    ins = pe.matmul(ps[7][:, SEQ:SEQ + 1], sel[:, t, :].bitcast(F32), at, start=(t == 0), stop=(t == 1))
                ins.then_inc(S("st_full"), 1)

            gather(0, 0, True)
            with pe.Fori(0, EXPERTS // PAIR) as e2:
                e = e2 * PAIR
                v0 = e2 * (PAIR * UNITS)
                c_ = e2 * (PAIR * CHUNKS)
                for w in range(PAIR * UNITS):
                    x, k = divmod(w, UNITS)
                    kind, c = eunits[k]
                    cc = x * CHUNKS + c

                    def turn(pc):
                        pe.wait_ge(S("eu"), passed("eu", p) + c_ + (pc + 3))
                        for i in range(2):
                            ins = pe.transpose(ps[2][:, pc % 2 * 256 + i * P:pc % 2 * 256 + (i + 1) * P], eu[:, pc % 2, i * P:(i + 1) * P], ident[:, :])
                        ins.then_inc(S("tr_full"), 1)

                    if kind == "gb" and c >= 1:
                        turn(cc - 1)
                    if kind == "w" and c == CHUNKS - 1:
                        turn(cc)
                    if kind == "ga" and c == 0:
                        pe.wait_ge(S("xg_hi"), passed("xg_hi", p) + e * 2 + 2 * (x + 1))
                        pe.wait_ge(S("xg_lo"), passed("xg_lo", p) + e * 2 + 2 * (x + 1))
                    pe.wait_ge(S("e_lo_done"), passed("e_lo_done", p) + v0 + (STAGE + w + 1))
                    hi, lo = ehi[:, w % SPLIT, :], elo[:, w % SPLIT, :]
                    if kind in ("ga", "gb"):
                        if kind == "ga":
                            pe.wait_ge(S("eu"), passed("eu", p) + c_ + (cc + 1))
                        for i in range(4):
                            kk = i + (4 if kind == "gb" else 0)
                            o = ps[cc % 2][:, :]
                            cols = slice(i * 512, i * 512 + 512)
                            pe.matmul(o, xg_hi[:, kk, :], hi[:, cols], start=(kk == 0), stop=False)
                            pe.matmul(o, xg_hi[:, kk, :], lo[:, cols], start=False, stop=False)
                            ins = pe.matmul(o, xg_lo[:, kk, :], hi[:, cols], start=False, stop=(kk == KD - 1))
                    else:
                        pe.wait_ge(S("ehT_lo"), passed("ehT_lo", p) + c_ + (cc + 1))
                        if c == 0:
                            pe.wait_ge(S("y_lo_e"), passed("y_lo_e", p) + e * 2 + 2 * (x + 1))
                        for i in range(2):
                            a_hi, a_lo = ehT_hi[:, cc % 2, i, :], ehT_lo[:, cc % 2, i, :]
                            first, last = c == 0 and i == 0, c == CHUNKS - 1 and i == 1
                            for f in range(2):
                                cols = slice(i * D + f * 512, i * D + f * 512 + 512)
                                pe.matmul(ps[3 + f][:, :], a_hi, hi[:, cols], start=first, stop=False)
                                pe.matmul(ps[3 + f][:, :], a_hi, lo[:, cols], start=False, stop=False)
                            for f in range(2):
                                cols = slice(i * D + f * 512, i * D + f * 512 + 512)
                                ins = pe.matmul(ps[3 + f][:, :], a_lo, hi[:, cols], start=False, stop=last)
                    ins.then_inc(used, 1)
                    if k == UNITS - 1:
                        gather(e, x + 1, False)
                        pe.wait_ge(S("y_lo_e"), passed("y_lo_e", p) + e * 2 + (2 * (x + 2)))
                        pe.wait_ge(S("selT"), passed("selT", p) + e + (x + 1))
                        for k4 in range(KD // 2):
                            if k4 < 2:
                                pe.wait_ge(S("xg_lo"), passed("xg_lo", p) + e * 2 + (2 * (x + 1) + k4 + 1))
                            else:
                                pe.wait_ge(S("x_add"), passed("x_add", p) + e * KD + (KD * (x + 1) + 2 * (k4 - 1)))
                            for i in range(2):
                                kk = 2 * k4 + i
                                o = ps[5 + k4 % 2][:, i * SEQ:(i + 1) * SEQ]
                                pe.matmul(o, y_hi[:, kk * P:(kk + 1) * P], selT[:, x % 2, :], start=True, stop=False)
                                ins = pe.matmul(o, y_lo[:, kk * P:(kk + 1) * P], selT[:, x % 2, :], start=False, stop=True)
                            ins.then_inc(S("sc_full"), 1)

        experts(0)
        most_r = pe.value_load(most_i[0:1, 0:1], min_val=0, max_val=SEQ)
        with pe.If(most_r > SLOTS):
            experts(1)
        pe.wait_ge(S("experts_done"), 1)
        norm("fin", SEQ)

    ctx_block.__exit__(None, None, None)


def _blocks(w):
    k, c = w.shape[0] // P, w.shape[1] // P
    return w.reshape(k, P, c, P).transpose(0, 2, 1, 3)


def _constants():
    import numpy as np

    t = np.arange(SEQ)
    half = ROPE // 2
    inv = (10000.0 ** (-np.arange(0, half, 2) / half)).astype(np.float32)
    pos = np.stack([t // 64, t % 64], axis=1).astype(np.float32)
    ang = (pos[:, :, None] * inv).astype(np.float32)
    cos, sin = np.cos(ang), np.sin(ang)
    rope = np.zeros((P, T), np.float32)
    for r in range(ROPE):
        axis, second, f = r // 16, r // 8 % 2, r % 8
        rope[NOPE + r, 0:SEQ] = 1.0
        rope[NOPE + r, SEQ:T] = cos[:, axis, f]
        rope[QK + r, SEQ:T] = sin[:, axis, f] if second else -sin[:, axis, f]
    c = np.arange(P)
    a = 2 * np.pi * np.outer(c, c) / P
    dft_c = np.concatenate([np.cos(a), np.sin(a)], axis=1) / np.sqrt(P)
    b = 2 * np.pi * np.outer(t, t) / SEQ
    dft_l = np.stack([np.cos(b), -np.sin(b)], axis=1) / np.sqrt(SEQ)
    dft_l = dft_l.reshape(2, P, 2, SEQ).transpose(1, 0, 2, 3)
    inv_n = np.zeros((P, GROUPS, SEQ), np.float32)
    for g, w in enumerate((2, 4, 8, 16)):
        left = w // 2
        right = w - 1 - left
        inv_n[:, g, :] = 1.0 / (np.minimum(t + right + 1, SEQ) - np.maximum(t - left, 0))
    out = {
        "ones": np.ones((P, P)), "ident": np.eye(P), "iota": np.tile(np.arange(P), (P, 1)),
        "before": np.triu(np.ones((P, P)), 1), "rope": rope, "dft_c": dft_c, "dft_l": dft_l, "inv_n": inv_n,
    }
    return {k: np.ascontiguousarray(v, dtype=np.float32) for k, v in out.items()}


def layout(i):
    import numpy as np

    i = {k: np.asarray(v) for k, v in i.items()}
    off_kv, off_kr = Q_LORA, Q_LORA + KV_LORA
    off_pool = off_kr + ROPE
    off_fft = off_pool + BRANCH_W
    off_gate = off_fft + BRANCH_W
    partner = np.arange(ROPE) ^ 8

    def cols(v):
        v = v.reshape(*v.shape[:-1], v.shape[-1] // P, P)
        return np.moveaxis(v, -1, 0)

    def tile_columns(layer, name):
        w = i["w_in"][layer]
        g = int(name[-1]) if name[-1].isdigit() else 0
        if name == "kr":
            kr = w[:, off_kr:off_pool]
            return np.concatenate([kr, kr[:, partner], kr, kr[:, partner]], axis=1)
        at = {"kv": off_kv, "q": 0, "fft": off_fft, "pool": off_pool}[name[:-1]] + g * P
        return w[:, at:at + P]

    split = []
    for key, _ in split_stream():
        kind = key[0]
        if kind == "in":
            b = _blocks(tile_columns(key[1], TILES[key[2]]))
        elif kind == "gate":
            j, br = divmod(key[2], BRANCHES)
            at = off_gate + br * D + j * P
            b = _blocks(i["w_in"][key[1]][:, at:at + P])
        elif kind == "out":
            b = _blocks(i["w_out"][key[1]][:, key[2] * P:(key[2] + 1) * P])
        elif kind in ("upg", "upu"):
            w = i["ffn_w1" if kind == "upg" else "ffn_w3"][0]
            b = _blocks(w[:, key[1] * P:(key[1] + 1) * P])
        else:
            ks = DOWN[key[1]]
            b = _blocks(i["ffn_w2"][0][ks[0] * P:(ks[-1] + 1) * P, key[2] * P:(key[2] + 1) * P])
        split.append(b[:, 0])
    split = np.concatenate(split, axis=0)
    split = split.reshape(-1, SPLIT_BLOCKS, P, P).transpose(0, 2, 1, 3).reshape(-1, P, SPLIT_BLOCKS * P)

    direct = []
    for key in direct_stream():
        kind, layer = key[0], key[1]
        unit = np.zeros((P, DIRECT_BLOCKS, P), np.float32)
        if kind == "mod":
            unit[:] = _blocks(i["w_mod"][layer][:, key[2] * P:(key[2] + 1) * P])[:, 0].transpose(1, 0, 2)
        elif kind == "pool":
            unit[:, 0:GROUPS] = i["w_pool"][layer].transpose(1, 0, 2)
        elif kind == "v":
            v = i["w_ukv"][layer][:, :, NOPE:].reshape(KKV, P, HEADS * VD)
            unit[:] = v.transpose(1, 0, 2).reshape(P, DIRECT_BLOCKS, P)
        elif kind == "head":
            for x in range(2):
                h = 2 * key[2] + x
                q = i["w_uq"][layer][:, h, :]
                q = np.concatenate([q, q[:, NOPE:][:, partner]], axis=1)
                unit[:, 4 * x:4 * x + KQ] = _blocks(q)[:, 0].transpose(1, 0, 2)
                k = i["w_ukv"][layer][:, h, 0:NOPE].reshape(KKV, P, NOPE)
                unit[:, 4 * x + 3] = k.transpose(1, 0, 2).reshape(P, P)
        else:
            for x in range(2):
                j, b = divmod(2 * key[2] + x, BRANCHES)
                w = i[("w_oa", "w_ob", "w_oc")[b]][layer]
                unit[:, 4 * x:4 * x + 4] = _blocks(w[:, j * P:(j + 1) * P])[:, 0].transpose(1, 0, 2)
        direct.append(unit)

    up = np.stack([i["moe_w1"][0], i["moe_w3"][0]], axis=0)
    up = up.reshape(2, EXPERTS, 2, 4, P, CHUNKS, CW).transpose(1, 5, 2, 4, 3, 0, 6)
    up = up.reshape(EXPERTS, CHUNKS, 2, P, 4 * 2 * CW)
    down = i["moe_w2"][0].reshape(EXPERTS, CHUNKS, 2, P, D).transpose(0, 1, 3, 2, 4).reshape(EXPERTS, CHUNKS, P, 2 * D)
    moe = np.empty((EXPERTS, UNITS, P, 2 * D), np.float32)
    for n, (kind, c) in enumerate(expert_units()):
        moe[:, n] = down[:, c] if kind == "w" else up[:, c, "gagb".index(kind) // 2]

    gains = np.concatenate([np.stack([i["g_norm1"], i["g_norm2"]], axis=1).reshape(2 * DEPTH, D), i["g_final"][None]], axis=0)
    x = np.concatenate([i["ctx"][0], i["x"][0]], axis=0)
    out = {
        "x": cols(x).transpose(0, 2, 1), "cond": cols(np.stack([i["c_ctx"], i["c"][0]], axis=0)).transpose(0, 2, 1),
        "b_mod": cols(i["b_mod"]), "gains": cols(gains), "b_gate": cols(i["b_gate"]), "s_pool": cols(i["s_pool"]),
        "g_q": cols(i["g_q"]), "g_kv": cols(i["g_kv"]),
        "router": i["moe_router"][0].reshape(KD, P, EXPERTS).transpose(1, 0, 2),
        "r_bias": np.broadcast_to(i["moe_bias"][0], (P, EXPERTS)),
        "split": split, "direct": np.stack(direct), "moe": moe.reshape(EXPERTS * UNITS, P, 2 * D),
    }
    return {k: np.ascontiguousarray(v) for k, v in out.items()} | _constants()


def kernel(**inputs):
    import concourse.bacc as bacc
    import numpy as np
    from concourse.bass_utils import run_bass_kernel_spmd

    arrays = layout(inputs)
    nc = bacc.Bacc("TRN2", target_bir_lowering=False, num_devices=1)
    aps = {k: nc.dram_tensor(f"in_{k}", v.shape, mybir.dt.from_np(v.dtype), kind="ExternalInput").ap() for k, v in arrays.items()}
    aps["out"] = nc.dram_tensor("out_x", (P, KD, SEQ), F32, kind="ExternalOutput").ap()
    build(nc, aps)
    r = run_bass_kernel_spmd(nc, [{f"in_{k}": v for k, v in arrays.items()}], core_ids=[0])
    y = r.results[0]["out_x"]
    return np.ascontiguousarray(y.transpose(2, 1, 0)).reshape(1, SEQ, D)
```

```python
import concourse.bass as bass
from concourse import mybir
from concourse.alu_op_type import AluOpType as ALU

ACT = mybir.ActivationFunctionType
F32 = mybir.dt.float32
F32R = mybir.dt.float32r
I32 = mybir.dt.int32
U32 = mybir.dt.uint32
AX = mybir.AxisListType.X

P = 128
D = 1024
KD = D // P
SEQ = 256
T = 2 * SEQ
DEPTH = 2
HEADS = 8
NOPE = 64
ROPE = 32
QK = NOPE + ROPE
VD = 64
Q_LORA = 384
KV_LORA = 256
KQ = Q_LORA // P
KKV = KV_LORA // P
SCALE = float(QK) ** -0.5
GROUPS = 4
PAD = 8
PW = SEQ + 2 * PAD
BRANCH_W = 512
KB = BRANCH_W // P
BRANCHES = 3
FF = 2816
NF = FF // P
EXPERTS = 8
EPS = 1e-6
MODS = 6 * KD

SPLIT_BLOCKS = 16
DIRECT_BLOCKS = 8
STAGE = 6
SPLIT = 3
DIRECT = 2
DENSE_SPLIT = 2

TILES = ["kv0", "kv1", "kr", "q0", "q1", "q2"] + [f"fft{g}" for g in range(GROUPS)] + [f"pool{g}" for g in range(GROUPS)]
NT = len(TILES)
UP_FIRST = 12
DOWN = [list(range(UP_FIRST)), list(range(UP_FIRST, NF))]
USLOTS = UP_FIRST

CW = 256
CHUNKS = FF // CW
STEPS = ("ga", "gb", "w")
UNITS = len(STEPS) * CHUNKS
PAIR = 2
SLOTS = 128
MOE_UNITS = EXPERTS * UNITS + 1
PASS_UNITS = -(-(EXPERTS * UNITS + SPLIT) // 12) * 12
SCATTER_AT = (1, 2)
GATHER_AT = (4, 6)


def split_stream():
    tiles = []
    for layer in range(DEPTH):
        tiles += [(("in", layer, j), KD) for j in range(NT)]
        tiles += [(("gate", layer, m), KD) for m in range(KD * BRANCHES)]
        tiles += [(("out", layer, j), KD) for j in range(KD)]
        if layer == 0:
            for half, ks in enumerate(DOWN):
                tiles += [((name, i), KD) for i in ks for name in ("upg", "upu")]
                tiles += [(("down", half, j), len(ks)) for j in range(KD)]
    return tiles


class Walk:

    def __init__(self):
        self.first, at, ends = {}, 0, set()
        for key, n in split_stream():
            self.first[key] = at
            at += n
            ends.add(at - 1)
            self.first[key + ("end",)] = at - 1
        self.blocks = at
        self.units = at // SPLIT_BLOCKS
        assert at % SPLIT_BLOCKS == 0
        ends |= {SPLIT_BLOCKS * (u + 1) - 1 for u in range(self.units)}
        self.marks = sorted(ends)
        self.number = {b: n + 1 for n, b in enumerate(self.marks)}

    def tile(self, *key):
        return self.number[self.first[key + ("end",)]]

    def unit(self, u):
        return self.number[SPLIT_BLOCKS * (u + 1) - 1]

    def units_up_to(self, *key):
        return self.first[key + ("end",)] // SPLIT_BLOCKS + 1


EARLY_MODS = 2 * KD
GC = 512
GT = GC // P
GROUP_UNITS = KD // 2
MOD_GROUPS = [(0, g) for g in range(EARLY_MODS // GT, MODS // GT)] + [(1, g) for g in range(MODS // GT)]


def mod_streams(layer, g):
    return (1,) if layer == 1 and g >= 2 * KD // GT else (0, 1)


def mod_plan():
    plan = {("in", 0, j): 1 for j in range(12)}
    plan |= {("gate", 0, m): 1 for m in range(2, 22)}
    plan |= {("out", 0, j): 1 for j in range(KD)}
    plan |= {("upu", i): 2 for i in range(UP_FIRST)}
    plan |= {("down", 0, j): 1 for j in range(KD)}
    plan |= {("upu", i): 1 for i in range(UP_FIRST, UP_FIRST + 8)}
    return plan


MOD_FLUSH = [("in", 0, NT - 1), ("gate", 0, KD * BRANCHES - 1), ("upu", NF - 1)]


def sum_plan():
    tiles = [key for key, _ in split_stream()]
    plan, done, at = {}, 0, 0
    for key in tiles:
        at += mod_plan().get(key, 0)
        upto = (at if key in MOD_FLUSH else at - 3) // GROUP_UNITS
        if upto > done:
            plan[key] = list(range(done, upto))
            done = upto
    assert done == len(MOD_GROUPS)
    return plan


def flushed(n):
    tiles = [key for key, _ in split_stream()]
    return sum(len(v) for key, v in sum_plan().items() if tiles.index(key) <= tiles.index(MOD_FLUSH[n]))


def direct_stream():
    out = []
    for layer in range(DEPTH):
        out += [("pool", layer), ("v", layer)]
        out += [("head", layer, n) for n in range(HEADS // 2)]
        out += [("proj", layer, n) for n in range(KD * BRANCHES // 2)]
    return out


_ITEMS = HEADS * T // P
FIRST_LAYER = {
    "in_evac": NT - 1, "kr": 4, "lsq": KKV + KQ, "lss": KKV + KQ, "lvar": 2, "lstd": 2, "lrstd": 2, "lnorm": KKV + KQ,
    "fa_full": 2 * GROUPS, "fg": 2 * GROUPS, "fb_full": 2 * GROUPS, "br_c": 2 * GROUPS,
    "pads": 1, "win": sum(g + 3 for g in range(GROUPS)), "mixed": GROUPS, "pool_full": GROUPS, "br_b": GROUPS,
    "v_full": T // P, "v_sb": T // P, "qk_full": HEADS, "qk_rows": 2 * HEADS, "q_rope": 3 * HEADS,
    "s_full": _ITEMS, "max": _ITEMS, "neg_max": _ITEMS, "prob": _ITEMS, "rden": _ITEMS, "pn": _ITEMS,
    "t_full": _ITEMS, "pT": _ITEMS, "pv": _ITEMS, "br_a": HEADS,
    "gate": KD * BRANCHES, "o_full": KD * BRANCHES, "o_used": KD * BRANCHES, "y_part": KD, "y_sum": KD,
    "y_hi": KD, "y_lo": KD, "x_mix": KD, "mods": 6,
}
_CHUNKS, _GATHERS = EXPERTS * CHUNKS, EXPERTS + 1
FIRST_PASS = {
    "e_in": 16 * PASS_UNITS // STAGE, "e_hi_done": PASS_UNITS, "e_lo_done": PASS_UNITS, "e_used": PASS_UNITS,
    "et": _CHUNKS, "em": _CHUNKS, "eu": _CHUNKS + 2, "tr_full": _CHUNKS + 1, "ehT_hi": _CHUNKS + 1, "ehT_lo": _CHUNKS + 1,
    "sel": 2 * _GATHERS, "ga_full": 4 * _GATHERS, "xg_hi": 2 * _GATHERS, "xg_lo": 2 * _GATHERS,
    "st_full": _GATHERS, "selT": _GATHERS + 1, "w_slot": _GATHERS + 1,
    "y_hi_e": 2 * _GATHERS, "y_lo_e": 2 * _GATHERS, "sc_full": 4 * _GATHERS, "x_add": KD * _GATHERS,
}


def load_order(walk, direct_at):
    out, seen = [], set()

    def add(item):
        if item not in seen:
            seen.add(item)
            out.append(item)

    def tile(*key):
        for u in range(walk.first[key] // SPLIT_BLOCKS, walk.first[key + ("end",)] // SPLIT_BLOCKS + 1):
            add(("s", u))

    for layer in range(DEPTH):
        for j in range(NT):
            tile("in", layer, j)
        for m in range(2 * DENSE_SPLIT):
            tile("gate", layer, m)
        for key in [("pool", layer), ("v", layer)] + [("head", layer, n) for n in range(HEADS // 2)]:
            add(("d", direct_at[key]))
        for m in range(KD * BRANCHES):
            tile("gate", layer, m)
            add(("d", direct_at[("proj", layer, m // 2)]))
        for j in range(KD):
            tile("out", layer, j)
        if layer == 0:
            for half, ks in enumerate(DOWN):
                for i in ks:
                    tile("upg", i)
                    tile("upu", i)
                for j in range(KD):
                    tile("down", half, j)
    assert len(out) == walk.units + len(direct_at)
    return out


def build(nc, A):
    walk = Walk()
    direct = direct_stream()
    direct_at = {key: n for n, key in enumerate(direct)}

    base = -(-nc.sbuf_base // 32) * 32
    end = nc.sbuf_usable_end

    class Region:

        def __init__(self, at):
            self.at = at

        def take(self, name, shape, dtype=F32):
            size = 4
            for n in shape[1:]:
                size *= n
            t = nc.alloc_sbuf_tensor_at(name, shape, dtype, offset=self.at)
            self.at = -(-(self.at + size) // 32) * 32
            assert self.at <= end, (name, self.at - end)
            return t

    fixed = Region(base)
    xT = fixed.take("xT", [P, KD, T])
    ones = fixed.take("ones", [P, P])
    ident = fixed.take("ident", [P, P])
    iota = fixed.take("iota", [P, P])
    before = fixed.take("before", [P, P])
    cond_in = fixed.take("cond_in", [P, KD, 2])
    cond_t = fixed.take("cond_t", [P, KD, 2])
    cond = fixed.take("cond", [P, KD, 2])
    mod = fixed.take("mod", [P, DEPTH, 2, MODS])
    b_mod = fixed.take("b_mod", [P, DEPTH, MODS])
    gains = fixed.take("gains", [P, 2 * DEPTH + 1, KD])
    coef = fixed.take("coef", [P, 2 * DEPTH, 2, KD])
    b_gate = fixed.take("b_gate", [P, DEPTH, BRANCHES * KD])
    half_b = fixed.take("half_b", [P, DEPTH, BRANCHES * KD])
    s_pool = fixed.take("s_pool", [P, DEPTH, GROUPS])
    g_q = fixed.take("g_q", [P, DEPTH, KQ])
    g_kv = fixed.take("g_kv", [P, DEPTH, KKV])
    router = fixed.take("router", [P, KD, EXPERTS])
    r_bias = fixed.take("r_bias", [P, EXPERTS])
    stat = fixed.take("stat", [P, 4, 4])
    phase = fixed.at

    dense = Region(phase)
    stage = dense.take("stage", [P, 3, SPLIT_BLOCKS * P])
    whi = dense.take("whi", [P, DENSE_SPLIT, SPLIT_BLOCKS, P], F32R)
    wlo = dense.take("wlo", [P, DENSE_SPLIT, SPLIT_BLOCKS, P], F32R)
    dw = dense.take("dw", [P, DIRECT, DIRECT_BLOCKS, P])
    mw_a = Region(dense.at).take("mw_a", [P, EARLY_MODS // 2, KD, P])
    h_hi = dense.take("h_hi", [P, KD, T], F32R)
    h_lo = dense.take("h_lo", [P, KD, T], F32R)
    gw = dense.take("gw", [P, 2, 2, GC])
    acc = dense.take("acc", [P, 2, 2, GC])
    rope = dense.take("rope", [P, T])
    dft_c = dense.take("dft_c", [P, 2 * P])
    dft_l = dense.take("dft_l", [P, 2, 2, SEQ])
    inv_n = dense.take("inv_n", [P, GROUPS, SEQ])
    free = dense.at
    mixer = Region(free)
    br = mixer.take("br", [P, BRANCHES, KB, T])
    late = Region(mixer.at)
    pkv = mixer.take("pkv", [P, KKV, T])
    pq = mixer.take("pq", [P, KQ, T])
    kT = mixer.take("kT", [P, 2, T])
    early = Region(mixer.at)
    pf = mixer.take("pf", [P, GROUPS, T])
    fg = mixer.take("fg", [P, 2, 2 * SEQ])
    pool_in = mixer.take("pool_in", [P, GROUPS, 2, PW])
    win = mixer.take("win", [P, 2, 2, PW])
    mixed = br
    v_sb = early.take("v_sb", [P, T // P, HEADS * VD])
    qT = early.take("qT", [P, 2, T])
    rt = early.take("rt", [P, T])
    prob = early.take("prob", [P, 3, T])
    pT = early.take("pT", [P, 2, T])
    yacc = late.take("yacc", [P, KD, T])
    gate = late.take("gate", [P, 2, T])
    gm = late.take("gm", [P, T])
    nr = Region(free)
    sq = nr.take("sq", [P, 2, T])
    var = nr.take("var", [P, T])
    std = nr.take("std", [P, T])
    rstd = nr.take("rstd", [P, T])
    nt = nr.take("nt", [P, 2, T])
    hf = nr.take("hf", [P, KD, SEQ])
    mw_b = Region(nr.at).take("mw_b", [P, EARLY_MODS // 2, KD, P])
    lr = Region(free)
    lsq = lr.take("lsq", [P, 2, T])
    lstd = lr.take("lstd", [P, 2, T])
    ff = Region(free)
    u_hi = ff.take("u_hi", [P, USLOTS, T], F32R)
    u_lo = ff.take("u_lo", [P, USLOTS, T], F32R)
    ft = ff.take("ft", [P, 2, T])
    fm = ff.take("fm", [P, T])
    fu = ff.take("fu", [P, 2, T])
    ex = Region(phase)
    estage = ex.take("estage", [P, STAGE, 4 * 512])
    ehi = ex.take("ehi", [P, SPLIT, 4 * 512], F32R)
    elo = ex.take("elo", [P, SPLIT, 4 * 512], F32R)
    et = ex.take("et", [P, 2, CW])
    em = ex.take("em", [P, 2, CW])
    eu = ex.take("eu", [P, 2, CW])
    ehT_hi = ex.take("ehT_hi", [P, 2, 2, SLOTS], F32R)
    ehT_lo = ex.take("ehT_lo", [P, 2, 2, SLOTS], F32R)
    y_hi = ex.take("y_hi", [P, D], F32R)
    y_lo = ex.take("y_lo", [P, D], F32R)
    htok = Region(max(ex.at, nr.at))
    htok_hi = htok.take("htok_hi", [P, 2, D], F32R)
    htok_lo = htok.take("htok_lo", [P, 2, D], F32R)
    rt_logit = htok.take("rt_logit", [P, 2, EXPERTS])
    rt_top = htok.take("rt_top", [P, 2, 8])
    rt_index = htok.take("rt_index", [P, 2, 8], U32)
    rt_indexf = htok.take("rt_indexf", [P, 2, 8])
    rt_one = htok.take("rt_one", [P, 2, 2, EXPERTS])
    rt_w = htok.take("rt_w", [P, 2, 5])
    comb = htok.take("comb", [P, 2, 2 * EXPERTS])
    mask = htok.take("mask", [P, 2, EXPERTS])
    posm = htok.take("posm", [P, 2, 2, 2 * EXPERTS])
    most = htok.take("most", [P, 1])
    most_i = htok.take("most_i", [P, 1], I32)
    sel = htok.take("sel", [P, 2, SLOTS], F32R)
    selT = htok.take("selT", [P, 2, SEQ], F32R)
    w_slot = htok.take("w_slot", [P, 2])
    xg_hi = htok.take("xg_hi", [P, 2, KD, SLOTS], F32R)
    xg_lo = htok.take("xg_lo", [P, 2, KD, SLOTS], F32R)
    o_fin = nc.alloc_sbuf_tensor_at("o_fin", [P, KD, SEQ], F32, offset=nr.at)

    ps = [nc.alloc_psum_tensor(f"ps{b}", [P, 512], F32) for b in range(8)]

    def hslot(k, n):
        slots = KD * SEQ // n
        return hf[:, :, :].rearrange("p k t -> p (k t)")[:, (k % slots) * n:(k % slots) * n + n]

    sems = {}

    def S(name):
        if name not in sems:
            sems[name] = nc.alloc_semaphore(name)
        return sems[name]

    def direct_used(n):
        kind, layer, *rest = direct[n]
        if kind == "pool":
            return S("pool_full"), earlier("pool_full", layer) + GROUPS
        if kind == "v":
            return S("v_full"), earlier("v_full", layer) + T // P
        if kind == "head":
            return S("qk_full"), earlier("qk_full", layer) + 2 * (rest[0] + 1)
        return S("o_full"), earlier("o_full", layer) + 2 * (rest[0] + 1)

    def c0(layer):
        return 0 if layer == 0 else SEQ

    def streams(layer):
        return (0, 1) if layer == 0 else (1,)

    def tile_c0(layer, j):
        return 0 if TILES[j] in ("kv0", "kv1", "kr") else c0(layer)

    def items(layer):
        tiles = range(4) if layer == 0 else (2, 3)
        return [(h, q, SEQ if q < 2 else T) for h in range(HEADS) for q in tiles]

    norms = [("n1_0", 0), ("n2_0", 0), ("n1_1", 0), ("n2_1", SEQ), ("fin", SEQ)]

    def earlier(name, layer):
        return FIRST_LAYER[name] if layer else 0

    def passed(name, p):
        return FIRST_PASS[name] * p

    def nth(tag):
        return [t for t, _ in norms].index(tag)

    def x_done(tag):
        return {
            "n1_0": (S("x_in"), 16), "n2_0": (S("x_mix"), KD), "n1_1": (S("x_ffn"), 2 * KD),
            "n2_1": (S("x_mix"), 2 * KD), "fin": None,
        }[tag]

    EARLY_CONSTS = 7
    TABLES = 9
    FLUSH_TILES = [EARLY_MODS, EARLY_MODS + GT * flushed(0), MODS]

    ctx_block = nc.Block()
    block = ctx_block.__enter__()

    @block.sync
    def _(sp):
        small = [
            (ones, A["ones"]), (b_mod, A["b_mod"]), (gains, A["gains"]),
            (b_gate, A["b_gate"]), (s_pool, A["s_pool"]), (g_q, A["g_q"]), (g_kv, A["g_kv"]),
        ]
        tables = [
            (rope, A["rope"]), (dft_c, A["dft_c"]), (dft_l, A["dft_l"]), (inv_n, A["inv_n"]), (ident, A["ident"]),
            (router, A["router"]), (r_bias, A["r_bias"]), (iota, A["iota"]), (before, A["before"]),
        ]
        assert len(small) == EARLY_CONSTS and len(tables) == TABLES

        def load_small(t, a):
            full = tuple(slice(None) for _ in t.shape)
            return sp.dma_start(t[full], a)

        load_small(cond_in, A["cond"]).then_inc(S("cond_in"), 16)
        load_small(*small[0]).then_inc(S("consts"), 16)

        def load_early_mods(q):
            for j in range(4 * q, 4 * q + 4):
                dst = (mw_a, mw_b)[j // (EARLY_MODS // 2)][:, j % (EARLY_MODS // 2), :, :]
                sp.dma_start(dst, A["early"][j]).then_inc(S(f"early_in{q}"), 16)

        load_early_mods(0)
        sp.dma_start(xT[:, :, :], A["x"]).then_inc(S("x_in"), 16)
        for q in range(1, EARLY_MODS // 4):
            load_early_mods(q)
        for t, a in small[1:]:
            load_small(t, a).then_inc(S("consts"), 16)

        def load_direct(n):
            if n >= DIRECT:
                s, v = direct_used(n - DIRECT)
                sp.wait_ge(s, v)
            sp.dma_start(dw[:, n % DIRECT, :, :], A["direct"][n]).then_inc(S(f"direct_in{n % DIRECT}"), 16)

        def load_split(u):
            if u >= 3:
                sp.wait_ge(S("lo_done"), u - 2)
            sp.dma_start(stage[:, u % 3, :], A["split"][u]).then_inc(S(f"split_in{u % 3}"), 16)

        for at, (kind, n) in enumerate(load_order(walk, direct_at)):
            if at == 3:
                for t, a in tables:
                    load_small(t, a).then_inc(S("tables"), 16)
            if kind == "d":
                load_direct(n)
            else:
                load_split(n)

        def experts(p):
            if p == 1:
                sp.wait_ge(S("x_add"), KD * (EXPERTS + 1))

            def load(v0, w, at):
                sp.wait_ge(S("e_lo_done"), passed("e_lo_done", p) + v0 + (w + 1))
                sp.dma_start(estage[:, w % STAGE, :], at).then_inc(S(f"e_in{w % STAGE}"), 16)

            with sp.Fori(0, EXPERTS // PAIR) as e2:
                v0 = e2 * (PAIR * UNITS)
                for w in range(PAIR * UNITS):
                    load(v0, w, A["moe"][bass.ds(v0 + w, 1)].rearrange("a p n -> p (a n)"))
            load(EXPERTS * UNITS, 0, A["moe"][EXPERTS * UNITS])
            for v in range(EXPERTS * UNITS + 1, PASS_UNITS):
                sp.wait_ge(S("e_lo_done"), passed("e_lo_done", p) + (v + 1))
                sp.sem_inc(S(f"e_in{v % STAGE}"), 16)

        experts(0)
        sp.wait_ge(S("most_ready"), 1)
        most_r = sp.value_load(most_i[0:1, 0:1], min_val=0, max_val=SEQ)
        with sp.If(most_r > SLOTS):
            experts(1)
        sp.wait_ge(S("out_ready"), KD)
        sp.dma_start(A["out"], o_fin[:, :, :]).then_inc(S("out_written"), 16)
        sp.wait_ge(S("out_written"), 16)

    @block.scalar
    def _(act):
        split_at = [0]

        def split_hi(upto):
            while split_at[0] < min(upto, walk.units):
                u = split_at[0]
                act.wait_ge(S(f"split_in{u % 3}"), 16 * (u // 3 + 1))
                if u >= DENSE_SPLIT:
                    act.wait_ge(S("walked"), walk.unit(u - DENSE_SPLIT))
                act.activation(whi[:, u % DENSE_SPLIT, :, :], stage[:, u % 3, :].rearrange("p (b c) -> p b c", c=P), ACT.Copy)\
                    .then_inc(S("hi_done"), 1)
                split_at[0] += 1

        def norm(tag, first):
            n = T - first
            for k in range(KD):
                if k == 0 and x_done(tag):
                    act.wait_ge(*x_done(tag))
                if k >= 2:
                    act.wait_ge(S("norm_ss"), KD * nth(tag) + k - 1)
                act.activation(sq[:, k % 2, 0:n], xT[:, k, first:T], ACT.Square).then_inc(S("norm_sq"), 1)
            act.wait_ge(S("norm_var"), 1 * nth(tag) + 1)
            act.activation(std[:, 0:n], var[:, 0:n], ACT.Sqrt).then_inc(S("norm_std"), 1)
            if tag == "fin":
                for k in range(KD):
                    act.wait_ge(S("norm_nt"), KD * nth("fin") + k + 1)
                    act.activation(o_fin[:, k, :], nt[:, k % 2, 0:n], ACT.Copy,
                                   scale=gains[:, 2 * DEPTH, k:k + 1]).then_inc(S("out_ready"), 1)
                return
            i = int(tag[1]) - 1
            layer = int(tag[3])
            parts = [(s, s * SEQ - first) for s in (0, 1) if s * SEQ >= first]
            slots = KD * SEQ // n

            def hi(k):
                act.wait_ge(S("norm_hf"), 2 * KD * nth(tag) + len(parts) * (k + 1))
                act.activation(h_hi[:, k, first:T], hslot(k, n), ACT.Copy).then_inc(S("norm_hhi"), 1)

            act.wait_ge(S("norm_coef"), 2 * nth(tag) + 2)
            for k in range(KD):
                act.wait_ge(S("norm_nt"), KD * nth(tag) + k + 1)
                if k >= slots:
                    act.wait_ge(S("norm_hlo"), KD * nth(tag) + k - slots + 1)
                for s, at in parts:
                    act.activation(hslot(k, n)[:, at:at + SEQ], nt[:, k % 2, at:at + SEQ], ACT.Identity,
                                   bias=mod[:, layer, s, 3 * i * KD + k:3 * i * KD + k + 1],
                                   scale=coef[:, 2 * layer + i, s, k:k + 1]).then_inc(S("norm_hf"), 1)
                if k >= 1:
                    hi(k - 1)
            hi(KD - 1)

        act.wait_ge(S("cond_in"), 16)
        act.activation(cond_t[:, :, :], cond_in[:, :, :], ACT.Tanh, scale=0.5).then_inc(S("cond_t"), 1)

        for layer in range(DEPTH):
            lc = c0(layer)
            norm(f"n1_{layer}", 0)
            for j, name in enumerate(TILES):
                split_hi(walk.units_up_to("in", layer, j) + 1)
                if name == "kr":
                    continue
                a = tile_c0(layer, j)
                act.wait_ge(S("walked"), walk.tile("in", layer, j))
                src = ps[j % 2][:, 0:T - a]
                if name.startswith("kv"):
                    dst = pkv[:, int(name[2]), a:T]
                elif name.startswith("q"):
                    dst = pq[:, int(name[1]), a:T]
                elif name.startswith("fft"):
                    dst = pf[:, int(name[3]), a:T]
                else:
                    if name == "pool0":
                        act.wait_ge(S("pads"), earlier("pads", layer) + 1)
                    dst = pool_in[:, int(name[4]), a // SEQ:2, PAD:PAD + SEQ]
                    src = src.rearrange("p (s t) -> p s t", t=SEQ)
                act.activation(dst, src, ACT.Copy).then_inc(S("in_evac"), 1)
                if name == "q2":
                    for i in range(KKV + KQ):
                        s0 = 0 if i < KKV else lc
                        if i == 0:
                            act.wait_ge(S("in_evac"), earlier("in_evac", layer) + 5)
                        if i >= 2:
                            act.wait_ge(S("lss"), earlier("lss", layer) + i - 1)
                        rows = pkv[:, i, :] if i < KKV else pq[:, i - KKV, s0:T]
                        act.activation(lsq[:, i % 2, s0:T], rows, ACT.Square).then_inc(S("lsq"), 1)
                if name == "fft1":
                    for i in range(2):
                        act.wait_ge(S("lvar"), earlier("lvar", layer) + i + 1)
                        s0 = (0, lc)[i]
                        act.activation(lstd[:, i, s0:T], lstd[:, i, s0:T], ACT.Sqrt).then_inc(S("lstd"), 1)
            for n in range(GROUPS * len(streams(layer))):
                act.wait_ge(S("fa_full"), earlier("fa_full", layer) + n + 1)
                if n >= 2:
                    act.wait_ge(S("fb_full"), earlier("fb_full", layer) + n - 1)
                act.activation(fg[:, n % 2, :], ps[2 + n % 2][:, :], ACT.Copy).then_inc(S("fg"), 1)
            for g in range(GROUPS):
                act.wait_ge(S("pool_full"), earlier("pool_full", layer) + g + 1)
                act.activation(br[:, 1, g, lc:T], ps[4 + g % 2][:, 0:T - lc], ACT.Copy,
                               scale=s_pool[:, layer, g:g + 1]).then_inc(S("br_b"), 1)
            for t in range(T // P):
                act.wait_ge(S("v_full"), earlier("v_full", layer) + t + 1)
                act.activation(v_sb[:, t, :], ps[2 + t % 2][:, :], ACT.Copy).then_inc(S("v_sb"), 1)

            todo = items(layer)
            per = len(todo) // HEADS

            def head_rows(h):
                act.wait_ge(S("qk_full"), earlier("qk_full", layer) + h + 1)
                act.activation(qT[0:NOPE, h % 2, lc:T], ps[0][0:NOPE, 0:T - lc], ACT.Copy).then_inc(S("qk_rows"), 1)
                act.activation(kT[0:NOPE, h % 2, :], ps[1][0:NOPE, :], ACT.Copy).then_inc(S("qk_rows"), 1)

            def exps(n):
                _, _, keys = todo[n]
                act.wait_ge(S("neg_max"), earlier("neg_max", layer) + n + 1)
                if n >= 3:
                    act.wait_ge(S("t_full"), earlier("t_full", layer) + n - 2)
                act.activation(prob[:, n % 3, 0:keys], ps[2 + n % 2][:, 0:keys], ACT.Exp, scale=SCALE,
                               bias=stat[:, 1, n % 4:n % 4 + 1], accum_out=stat[:, 2, n % 4:n % 4 + 1])\
                    .then_inc(S("prob"), 1)

            def probs_t(n):
                _, _, keys = todo[n]
                act.wait_ge(S("t_full"), earlier("t_full", layer) + n + 1)
                if n >= 2:
                    act.wait_ge(S("pv"), earlier("pv", layer) + n - 1)
                act.activation(pT[:, n % 2, 0:keys], ps[4 + n % 2][:, 0:keys], ACT.Copy).then_inc(S("pT"), 1)

            head_rows(0)
            for n in range(len(todo) + 2):
                if n < len(todo):
                    exps(n)
                    if n % per == 0 and todo[n][0] + 1 < HEADS:
                        head_rows(todo[n][0] + 1)
                if n >= 2:
                    probs_t(n - 2)

            for m in range(KD * BRANCHES):
                split_hi(walk.units_up_to("gate", layer, m) + 1)
                j, b = divmod(m, BRANCHES)
                act.wait_ge(S("walked"), walk.tile("gate", layer, m))
                if m >= 2:
                    act.wait_ge(S("o_used"), earlier("o_used", layer) + m - 1)
                if m == 0:
                    act.wait_ge(S("br_a"), earlier("br_a", layer) + HEADS)
                    act.wait_ge(S("half_b"), 1)
                act.activation(gate[:, m % 2, 0:T - lc], ps[m % 2][:, 0:T - lc], ACT.Tanh, scale=0.5,
                               bias=half_b[:, layer, b * KD + j:b * KD + j + 1]).then_inc(S("gate"), 1)
            for j in range(KD):
                act.wait_ge(S("y_sum"), earlier("y_sum", layer) + j + 1)
                if j == 0:
                    act.wait_ge(S("walked"), walk.tile("gate", layer, KD * BRANCHES - 1))
                act.activation(h_hi[:, j, lc:T], yacc[:, j, lc:T], ACT.Copy, scale=0.5).then_inc(S("y_hi"), 1)
            for j in range(KD):
                split_hi(walk.units_up_to("out", layer, j) + 1)
            norm(f"n2_{layer}", lc)
            if layer == 0:
                def hidden_hi(i):
                    act.wait_ge(S("fu"), i + 1)
                    if i >= USLOTS:
                        act.wait_ge(S("walked"), walk.tile("down", 0, KD - 1))
                    act.activation(u_hi[:, i % USLOTS, :], fu[:, i % 2, :], ACT.Copy).then_inc(S("u_hi"), 1)

                for half, ks in enumerate(DOWN):
                    for i in ks:
                        split_hi(walk.units_up_to("upu", i) + 1)
                        act.wait_ge(S("walked"), walk.tile("upg", i))
                        if i == 0:
                            act.wait_ge(S("norm_hlo"), KD * nth("n2_0") + KD)
                        if i >= 2:
                            act.wait_ge(S("fm"), i - 1)
                        act.activation(ft[:, i % 2, :], ps[i % 2][:, :], ACT.Tanh, scale=0.5).then_inc(S("ft"), 1)
                        split_hi(walk.units_up_to("upu", i) + 2)
                        hidden_hi(i)
                    for j in range(KD):
                        split_hi(walk.units_up_to("down", half, j) + 1)

        for n in range(8):
            act.wait_ge(S("ht_full"), n + 1)
            dst = (htok_hi, htok_lo)[n // 4]
            act.activation(dst[:, n // 2 % 2, n % 2 * 512:n % 2 * 512 + 512], ps[n % 2][:, :], ACT.Copy).then_inc(S("htok"), 1)
        act.sem_inc(S("e_used"), SPLIT)
        act.wait_ge(S("rt_diff"), 2)
        act.activation(rt_w[:, :, 1], rt_w[:, :, 0], ACT.Exp).then_inc(S("rt_exp"), 1)

        def experts(p):
            used = S("e_used")
            if p == 1:
                act.wait_ge(S("x_add"), KD * (EXPERTS + 1))

            def hi(v0, w):
                act.wait_ge(S(f"e_in{w % STAGE}"), passed("e_in", p) + v0 * 16 + 16 * (w // STAGE + 1))
                act.wait_ge(used, passed("e_used", p) + v0 * STAGE + (w + 1))
                act.activation(ehi[:, w % SPLIT, :], estage[:, w % STAGE, :], ACT.Copy).then_inc(S("e_hi_done"), 1)

            def gathered_hi(e, x):
                for f in range(2):
                    act.wait_ge(S("ga_full"), passed("ga_full", p) + e * 4 + (4 * x + f + 1))
                    act.activation(xg_hi[:, x % 2, 4 * f:4 * f + 4, :], ps[5 + f][:, :].rearrange("p (k s) -> p k s", s=SLOTS), ACT.Copy)\
                        .then_inc(S("xg_hi"), 1)

            def turned_select(e, x):
                act.wait_ge(S("st_full"), passed("st_full", p) + e + (x + 1))
                act.activation(selT[:, x % 2, :], ps[7][:, 0:SEQ], ACT.Copy).then_inc(S("selT"), 1)
                act.activation(w_slot[:, x % 2:x % 2 + 1], ps[7][:, SEQ:SEQ + 1], ACT.Copy).then_inc(S("w_slot"), 1)

            def hidden_hi(c_, pc):
                act.wait_ge(S("tr_full"), passed("tr_full", p) + c_ + (pc + 2))
                act.activation(ehT_hi[:, pc % 2, :, :], ps[2][:, pc % 2 * 256:pc % 2 * 256 + 256].rearrange("p (b s) -> p b s", s=SLOTS), ACT.Copy)\
                    .then_inc(S("ehT_hi"), 1)

            def rows_hi(e, x, v0, w):
                act.wait_ge(used, passed("e_used", p) + v0 * STAGE + (SPLIT + w + 1))
                act.wait_ge(S("w_slot"), passed("w_slot", p) + e + (x + 1))
                act.wait_ge(S("sc_full"), passed("sc_full", p) + e * 4 + 4 * (x + 1))
                for f in range(2):
                    act.activation(y_hi[:, f * 512:f * 512 + 512], ps[3 + f][:, :], ACT.Copy,
                                   scale=w_slot[:, (x - 1) % 2:(x - 1) % 2 + 1]).then_inc(S("y_hi_e"), 1)

            for w in range(SPLIT):
                hi(0, w)
            gathered_hi(0, 0)
            turned_select(0, 0)
            with act.Fori(0, EXPERTS // PAIR) as e2:
                e = e2 * PAIR
                v0 = e2 * (PAIR * UNITS // STAGE)
                c_ = e2 * (PAIR * CHUNKS)
                for w in range(PAIR * UNITS):
                    x, c, kind = w // UNITS, w % UNITS // 3, STEPS[w % 3]
                    cc = x * CHUNKS + c
                    if kind == "ga":
                        if c == GATHER_AT[0] + 1:
                            gathered_hi(e, x + 1)
                        if c == GATHER_AT[1] + 1:
                            turned_select(e, x + 1)
                        hidden_hi(c_, cc - 1)
                    if kind == "gb":
                        act.wait_ge(used, passed("e_used", p) + v0 * STAGE + (SPLIT + w + 1))
                        act.activation(et[:, cc % 2, :], ps[cc % 2][:, 0:CW], ACT.Tanh, scale=0.5).then_inc(S("et"), 1)
                    if kind == "w" and c == 0:
                        rows_hi(e, x, v0, w)
                    hi(v0, w + SPLIT)
            hidden_hi(EXPERTS * CHUNKS, -1)
            rows_hi(EXPERTS, 0, EXPERTS * UNITS // STAGE, 0)
            act.sem_inc(S("e_hi_done"), PASS_UNITS - EXPERTS * UNITS - SPLIT)

        experts(0)
        act.wait_ge(S("most_ready"), 1)
        most_r = act.value_load(most_i[0:1, 0:1], min_val=0, max_val=SEQ)
        with act.If(most_r > SLOTS):
            experts(1)
        act.wait_ge(S("experts_done"), 1)
        norm("fin", SEQ)

    @block.vector
    def _(dve):
        split_at = [0]

        def split_lo(upto):
            while split_at[0] < min(upto, walk.units):
                u = split_at[0]
                dve.wait_ge(S("hi_done"), u + 1)
                dve.tensor_tensor(wlo[:, u % DENSE_SPLIT, :, :], stage[:, u % 3, :].rearrange("p (b c) -> p b c", c=P),
                                  whi[:, u % DENSE_SPLIT, :, :], ALU.subtract).then_inc(S("lo_done"), 1)
                split_at[0] += 1

        def norm(tag, first):
            n = T - first
            dve.wait_ge(S("norm_ss"), KD * nth(tag) + KD)
            dve.tensor_scalar(var[:, 0:n], ps[6][:, 0:n], 1.0 / D, EPS, ALU.mult, ALU.add).then_inc(S("norm_var"), 1)
            dve.wait_ge(S("norm_std"), 1 * nth(tag) + 1)
            dve.reciprocal(rstd[:, 0:n], std[:, 0:n]).then_inc(S("norm_rstd"), 1)
            dve.wait_ge(S("norm_rstd"), 1 * nth(tag) + 1)

            def lo(k):
                dve.wait_ge(S("norm_hhi"), KD * nth(tag) + k + 1)
                dve.tensor_tensor(h_lo[:, k, first:T], hslot(k, n), h_hi[:, k, first:T], ALU.subtract)\
                    .then_inc(S("norm_hlo"), 1)

            parts = 2 if first == 0 else 1
            for k in range(KD):
                if k >= 2:
                    if tag == "fin":
                        dve.wait_ge(S("out_ready"), k - 1)
                    else:
                        dve.wait_ge(S("norm_hf"), 2 * KD * nth(tag) + parts * (k - 1))
                dve.tensor_tensor(nt[:, k % 2, 0:n], xT[:, k, first:T], rstd[:, 0:n], ALU.mult).then_inc(S("norm_nt"), 1)
                if k >= 2 and tag != "fin":
                    lo(k - 2)
            if tag != "fin":
                lo(KD - 2)
                lo(KD - 1)

        def coefs(layer, i):
            for s in (0, 1):
                at = (3 * i + 1) * KD
                if (layer, i, s) == (1, 1, 0):
                    dve.sem_inc(S("norm_coef"), 1)
                    continue
                dve.scalar_tensor_tensor(coef[:, 2 * layer + i, s, :], mod[:, layer, s, at:at + KD], 1.0,
                                         gains[:, 2 * layer + i, :], ALU.add, ALU.mult)\
                    .then_inc(S("norm_coef"), 1)

        def mods(layer, first, last):
            rows = ps[7][:, 0:2 * MODS].rearrange("p (j s) -> p j s", s=2)
            for s in (0, 1):
                upto = min(last, 2 * KD) if layer == 1 and s == 0 else last
                dve.tensor_tensor(mod[:, layer, s, first:upto], rows[:, first:upto, s], b_mod[:, layer, first:upto],
                                  ALU.add).then_inc(S("mods"), 1)

        group_unit = [0]

        def mod_units(*key):
            for _ in range(mod_plan().get(key, 0)):
                u = group_unit[0]
                n, quarter = divmod(u, GROUP_UNITS)
                dve.wait_ge(S(f"group_in{u % 2}"), 16 * (u // 2 + 1))
                if quarter == 0 and n >= 2:
                    dve.wait_ge(S("mod_sum"), n - 1)
                for half in range(2):
                    k = 2 * quarter + half
                    if k > 0:
                        dve.wait_ge(S("acc_step"), KD * n + k)
                    for s in mod_streams(*MOD_GROUPS[n]):
                        dst, w, c = acc[:, n % 2, s, :], gw[:, u % 2, half, :], cond_t[:, k, s:s + 1]
                        if k == 0:
                            ins = dve.tensor_scalar(dst, w, c, None, ALU.mult)
                        else:
                            ins = dve.scalar_tensor_tensor(dst, w, c, dst, ALU.mult, ALU.add)
                    ins.then_inc(S("acc_step"), 1)
                group_unit[0] += 1

        dve.wait_ge(S("cond_t"), 1)
        dve.scalar_tensor_tensor(cond[:, :, :], cond_t[:, :, :], 1.0, cond_in[:, :, :], ALU.add, ALU.mult)\
            .then_inc(S("cond"), 1)
        dve.wait_ge(S("cond"), 1)
        dve.tensor_scalar(cond_t[:, :, :], cond[:, :, :], 0.5, None, ALU.mult).then_inc(S("cond"), 1)
        dve.wait_ge(S("consts"), 16 * EARLY_CONSTS)
        dve.tensor_scalar(half_b[:, :, :], b_gate[:, :, :], 0.5, None, ALU.mult).then_inc(S("half_b"), 1)
        dve.wait_ge(S("mod_tile"), EARLY_MODS)
        mods(0, 0, EARLY_MODS)
        dve.wait_ge(S("mods"), 2)
        coefs(0, 0)

        for layer in range(DEPTH):
            lc = c0(layer)
            norm(f"n1_{layer}", 0)
            for j, name in enumerate(TILES):
                split_lo(walk.units_up_to("in", layer, j) + 1)
                if name == "kr":
                    dve.wait_ge(S("walked"), walk.tile("in", layer, j))
                    dve.wait_ge(S("tables"), 16 * TABLES)
                    dve.tensor_tensor(kT[64:96, 0, :], ps[j % 2][64:96, :], rope[64:96, :], ALU.mult)\
                        .then_inc(S("kr"), 1)
                    dve.tensor_tensor(kT[64:96, 1, :], ps[j % 2][96:128, :], rope[96:128, :], ALU.mult)\
                        .then_inc(S("kr"), 1)
                    dve.wait_ge(S("kr"), earlier("kr", layer) + 2)
                    dve.tensor_tensor(kT[64:96, 0, :], kT[64:96, 0, :], kT[64:96, 1, :], ALU.add)\
                        .then_inc(S("kr"), 1)
                    dve.wait_ge(S("kr"), earlier("kr", layer) + 3)
                    dve.tensor_copy(kT[64:96, 1, :], kT[64:96, 0, :]).then_inc(S("kr"), 1)
                if name == "fft1":
                    for i, width in enumerate((KV_LORA, Q_LORA)):
                        s0 = (0, lc)[i]
                        dve.wait_ge(S("lss"), earlier("lss", layer) + (KKV, KKV + KQ)[i])
                        dve.tensor_scalar(lstd[:, i, s0:T], ps[(6, 2)[i]][:, s0:T], 1.0 / width, EPS, ALU.mult, ALU.add)\
                            .then_inc(S("lvar"), 1)
                if name == "fft2":
                    for i in range(2):
                        s0 = (0, lc)[i]
                        dve.wait_ge(S("lstd"), earlier("lstd", layer) + i + 1)
                        dve.reciprocal(lstd[:, i, s0:T], lstd[:, i, s0:T]).then_inc(S("lrstd"), 1)
                    dve.wait_ge(S("in_evac"), earlier("in_evac", layer) + 5)
                    for i in range(KKV + KQ):
                        s0 = 0 if i < KKV else lc
                        rows = pkv[:, i, :] if i < KKV else pq[:, i - KKV, s0:T]
                        gain = g_kv[:, layer, i:i + 1] if i < KKV else g_q[:, layer, i - KKV:i - KKV + 1]
                        if i in (0, KKV):
                            dve.wait_ge(S("lrstd"), earlier("lrstd", layer) + (1 if i == 0 else 2))
                        dve.scalar_tensor_tensor(rows, rows, gain, lstd[:, 0 if i < KKV else 1, s0:T], ALU.mult, ALU.mult)\
                            .then_inc(S("lnorm"), 1)
                mod_units("in", layer, j)
            if layer == 0:
                dve.wait_ge(S("mod_sum"), flushed(0))
                mods(0, FLUSH_TILES[0], FLUSH_TILES[1])
            n = 0
            for s in streams(layer):
                for g in range(GROUPS):
                    dve.wait_ge(S("fb_full"), earlier("fb_full", layer) + n + 1)
                    if n == 0:
                        dve.wait_ge(S("lnorm"), earlier("lnorm", layer) + KKV + KQ)
                    dve.tensor_copy(br[:, 2, g, s * SEQ:(s + 1) * SEQ], ps[4 + n % 2][:, 0:SEQ]).then_inc(S("br_c"), 1)
                    n += 1
            todo = items(layer)
            per = len(todo) // HEADS

            def head_rope(h):
                dve.wait_ge(S("qk_full"), earlier("qk_full", layer) + h + 1)
                dve.tensor_tensor(qT[64:96, h % 2, lc:T], ps[0][64:96, 0:T - lc], rope[64:96, lc:T], ALU.mult)\
                    .then_inc(S("q_rope"), 1)
                if h >= 1:
                    dve.wait_ge(S("q_rope"), earlier("q_rope", layer) + 3 * h)
                dve.tensor_tensor(rt[64:96, lc:T], ps[0][96:128, 0:T - lc], rope[96:128, lc:T], ALU.mult)\
                    .then_inc(S("q_rope"), 1)
                dve.wait_ge(S("q_rope"), earlier("q_rope", layer) + 3 * h + 2)
                dve.tensor_tensor(qT[64:96, h % 2, lc:T], qT[64:96, h % 2, lc:T], rt[64:96, lc:T], ALU.add)\
                    .then_inc(S("q_rope"), 1)

            def row_max(n):
                _, _, keys = todo[n]
                dve.wait_ge(S("s_full"), earlier("s_full", layer) + n + 1)
                dve.tensor_reduce(stat[:, 0, n % 4:n % 4 + 1], ps[2 + n % 2][:, 0:keys], AX, ALU.max).then_inc(S("max"), 1)
                dve.wait_ge(S("max"), earlier("max", layer) + n + 1)
                dve.tensor_scalar(stat[:, 1, n % 4:n % 4 + 1], stat[:, 0, n % 4:n % 4 + 1], -SCALE, None, ALU.mult)\
                    .then_inc(S("neg_max"), 1)

            def normalise(n):
                _, _, keys = todo[n]
                dve.wait_ge(S("prob"), earlier("prob", layer) + n + 1)
                dve.reciprocal(stat[:, 3, n % 4:n % 4 + 1], stat[:, 2, n % 4:n % 4 + 1]).then_inc(S("rden"), 1)
                dve.wait_ge(S("rden"), earlier("rden", layer) + n + 1)
                dve.tensor_scalar(prob[:, n % 3, 0:keys], prob[:, n % 3, 0:keys], stat[:, 3, n % 4:n % 4 + 1], None, ALU.mult)\
                    .then_inc(S("pn"), 1)

            def head_out(h):
                dve.wait_ge(S("pv"), earlier("pv", layer) + per * (h + 1))
                if h == 0:
                    dve.wait_ge(S("pool_full"), earlier("pool_full", layer) + GROUPS)
                at = h % 2 * 64
                dve.tensor_copy(br[at:at + 64, 0, h // 2, lc:T], ps[6 + h % 2][0:64, lc:T]).then_inc(S("br_a"), 1)

            head_rope(0)
            for n in range(len(todo) + 3):
                if n < len(todo):
                    row_max(n)
                    if n % per == 0 and todo[n][0] + 1 < HEADS:
                        head_rope(todo[n][0] + 1)
                if 1 <= n <= len(todo):
                    normalise(n - 1)
                if n >= 3 and (n - 3) % per == per - 1:
                    head_out((n - 3) // per)
            for m in range(KD * BRANCHES):
                split_lo(walk.units_up_to("gate", layer, m) + 1)
                j, b = divmod(m, BRANCHES)
                dve.wait_ge(S("o_full"), earlier("o_full", layer) + m + 1)
                dve.wait_ge(S("gate"), earlier("gate", layer) + m + 1)
                o = ps[2 + m % 2][:, 0:T - lc]
                if b == 2:
                    dve.wait_ge(S("y_part"), earlier("y_part", layer) + j + 1)
                if b == 0:
                    dve.scalar_tensor_tensor(yacc[:, j, lc:T], gate[:, m % 2, 0:T - lc], 1.0, o, ALU.add, ALU.mult)\
                        .then_inc(S("o_used"), 1)
                else:
                    if b == 1 and j >= 1:
                        dve.wait_ge(S("y_sum"), earlier("y_sum", layer) + j)
                    dve.scalar_tensor_tensor(gm[:, 0:T - lc], gate[:, m % 2, 0:T - lc], 1.0, o, ALU.add, ALU.mult)\
                        .then_inc(S("o_used"), 1)
                    dve.wait_ge(S("o_used"), earlier("o_used", layer) + m + 1)
                    dve.tensor_tensor(yacc[:, j, lc:T], yacc[:, j, lc:T], gm[:, 0:T - lc], ALU.add)\
                        .then_inc(S("y_part" if b == 1 else "y_sum"), 1)
                mod_units("gate", layer, m)
            if layer == 0:
                dve.wait_ge(S("mod_sum"), flushed(1))
                mods(0, FLUSH_TILES[1], FLUSH_TILES[2])
                dve.wait_ge(S("mods"), 6)
                coefs(0, 1)
            for j in range(KD):
                dve.wait_ge(S("y_hi"), earlier("y_hi", layer) + j + 1)
                dve.scalar_tensor_tensor(h_lo[:, j, lc:T], yacc[:, j, lc:T], 0.5, h_hi[:, j, lc:T], ALU.mult, ALU.subtract)\
                    .then_inc(S("y_lo"), 1)
            for j in range(KD):
                split_lo(walk.units_up_to("out", layer, j) + 1)
                dve.wait_ge(S("walked"), walk.tile("out", layer, j))
                for s in streams(layer):
                    at = s * SEQ
                    ins = dve.scalar_tensor_tensor(xT[:, j, at:at + SEQ], ps[4 + j % 2][:, at - lc:at - lc + SEQ],
                                                   mod[:, layer, s, 2 * KD + j:2 * KD + j + 1],
                                                   xT[:, j, at:at + SEQ], ALU.mult, ALU.add)
                ins.then_inc(S("x_mix"), 1)
                mod_units("out", layer, j)
                if layer == DEPTH - 1 and j == KD - 1:
                    dve.wait_ge(S("lo_done"), walk.units)
                    dve.sem_inc(S("e_lo_done"), STAGE)
            norm(f"n2_{layer}", lc)
            if layer == 0:
                for half, ks in enumerate(DOWN):
                    for i in ks:
                        split_lo(walk.units_up_to("upu", i) + 1)
                        dve.wait_ge(S("ft"), i + 1)
                        if i >= 1:
                            dve.wait_ge(S("fu"), i)
                        dve.scalar_tensor_tensor(fm[:, :], ft[:, i % 2, :], 1.0, ps[i % 2][:, :], ALU.add, ALU.mult)\
                            .then_inc(S("fm"), 1)
                        dve.wait_ge(S("fm"), i + 1)
                        dve.wait_ge(S("walked"), walk.tile("upu", i))
                        if i >= 2:
                            dve.wait_ge(S("u_hi"), i - 1)
                        dve.scalar_tensor_tensor(fu[:, i % 2, :], fm[:, :], 0.5, ps[2 + i % 2][:, :], ALU.mult, ALU.mult)\
                            .then_inc(S("fu"), 1)
                        split_lo(walk.units_up_to("upu", i) + 2)
                        dve.wait_ge(S("u_hi"), i + 1)
                        dve.tensor_tensor(u_lo[:, i % USLOTS, :], fu[:, i % 2, :], u_hi[:, i % USLOTS, :], ALU.subtract)\
                            .then_inc(S("u_lo"), 1)
                        mod_units("upu", i)
                    for j in range(KD):
                        split_lo(walk.units_up_to("down", half, j) + 1)
                        dve.wait_ge(S("walked"), walk.tile("down", half, j))
                        if half == 1:
                            dve.wait_ge(S("x_ffn"), j + 1)
                        for s in (0, 1):
                            at = s * SEQ
                            ins = dve.scalar_tensor_tensor(xT[:, j, at:at + SEQ], ps[4 + j % 2][:, at:at + SEQ],
                                                           mod[:, 0, s, 5 * KD + j:5 * KD + j + 1],
                                                           xT[:, j, at:at + SEQ], ALU.mult, ALU.add)
                        ins.then_inc(S("x_ffn"), 1)
                        mod_units("down", half, j)
                dve.wait_ge(S("mod_sum"), flushed(2))
                mods(1, 0, MODS)
                dve.wait_ge(S("mods"), earlier("mods", 1) + 2)
                coefs(1, 0)
                coefs(1, 1)

        chain = [0]

        def step(ins):
            chain[0] += 1
            ins.then_inc(S("rt_step"), 1)
            dve.wait_ge(S("rt_step"), chain[0])

        dve.wait_ge(S("lg_full"), 1)
        for t in range(2):
            step(dve.tensor_tensor(rt_logit[:, t, :], ps[7][:, t * 8:t * 8 + 8], r_bias[:, :], ALU.add))
            step(dve.max(rt_top[:, t, :], rt_logit[:, t, :]))
            step(dve.max_index(rt_index[:, t, :], rt_top[:, t, :], rt_logit[:, t, :]))
            step(dve.tensor_copy(rt_indexf[:, t, :], rt_index[:, t, :]))
            for r in range(2):
                step(dve.tensor_scalar(rt_one[:, t, r, :], iota[:, 0:EXPERTS], rt_indexf[:, t, r:r + 1], None, ALU.is_equal))
            dve.tensor_tensor(rt_w[:, t, 0:1], rt_top[:, t, 1:2], rt_top[:, t, 0:1], ALU.subtract).then_inc(S("rt_diff"), 1)
            dve.tensor_tensor(mask[:, t, :], rt_one[:, t, 0, :], rt_one[:, t, 1, :], ALU.add).then_inc(S("mask"), 1)
        dve.wait_ge(S("rt_exp"), 1)
        step(dve.memset(comb[:, :, :], 0.0))
        for t in range(2):
            step(dve.tensor_scalar(rt_w[:, t, 2:3], rt_w[:, t, 1:2], 1.0, None, ALU.add))
            step(dve.reciprocal(rt_w[:, t, 3:4], rt_w[:, t, 2:3]))
            step(dve.tensor_tensor(rt_w[:, t, 4:5], rt_w[:, t, 1:2], rt_w[:, t, 3:4], ALU.mult))
            step(dve.tensor_scalar(comb[:, t, 0:EXPERTS], rt_one[:, t, 0, :], rt_w[:, t, 3:4], None, ALU.mult))
            step(dve.scalar_tensor_tensor(comb[:, t, 0:EXPERTS], rt_one[:, t, 1, :], rt_w[:, t, 4:5], comb[:, t, 0:EXPERTS], ALU.mult, ALU.add))
        step(dve.memset(posm[:, :, :, :], -1.0))
        dve.wait_ge(S("cnt_full"), 1)
        for t in range(2):
            step(dve.scalar_tensor_tensor(posm[:, 0, t, 0:EXPERTS], ps[7][:, 32 + t * 8:40 + t * 8], 1.0, mask[:, t, :], ALU.add, ALU.mult))
            step(dve.tensor_scalar(posm[:, 0, t, 0:EXPERTS], posm[:, 0, t, 0:EXPERTS], 1.0, None, ALU.subtract))
            step(dve.tensor_scalar(posm[:, 1, t, 0:EXPERTS], posm[:, 0, t, 0:EXPERTS], float(SLOTS), None, ALU.subtract))
        step(dve.tensor_reduce(most[:, :], ps[7][:, 48:56], AX, ALU.max))
        dve.tensor_copy(most_i[:, :], most[:, :]).then_inc(S("most_ready"), 1)

        def experts(p):
            if p == 1:
                dve.wait_ge(S("x_add"), KD * (EXPERTS + 1))

            def lo(v0, w):
                dve.wait_ge(S("e_hi_done"), passed("e_hi_done", p) + v0 * STAGE + (w + 1))
                dve.tensor_tensor(elo[:, w % SPLIT, :], estage[:, w % STAGE, :], ehi[:, w % SPLIT, :], ALU.subtract)\
                    .then_inc(S("e_lo_done"), 1)

            def select(e, x, first=False):
                if not first:
                    dve.wait_ge(S("st_full"), passed("st_full", p) + e + x)
                for t in range(2):
                    at = posm[:, p, t, 0:1] if first else posm[:, p, t, bass.ds(e + x, 1)]
                    dve.tensor_scalar(sel[:, t, :], iota[:, :], at, None, ALU.is_equal).then_inc(S("sel"), 1)

            def gathered_lo(e, x):
                for f in range(2):
                    dve.wait_ge(S("ga_full"), passed("ga_full", p) + e * 4 + (4 * x + f + 3))
                    dve.tensor_copy(xg_lo[:, x % 2, 4 * f:4 * f + 4, :], ps[5 + f][:, :].rearrange("p (k s) -> p k s", s=SLOTS))\
                        .then_inc(S("xg_lo"), 1)

            def hidden_lo(c_, pc):
                dve.wait_ge(S("ehT_hi"), passed("ehT_hi", p) + c_ + (pc + 2))
                dve.tensor_tensor(ehT_lo[:, pc % 2, :, :], ps[2][:, pc % 2 * 256:pc % 2 * 256 + 256].rearrange("p (b s) -> p b s", s=SLOTS),
                                  ehT_hi[:, pc % 2, :, :], ALU.subtract).then_inc(S("ehT_lo"), 1)

            def rows_lo(e, x):
                slot = w_slot[:, (x - 1) % 2:(x - 1) % 2 + 1]
                dve.wait_ge(S("w_slot"), passed("w_slot", p) + e + (x + 1))
                for f in range(2):
                    dve.wait_ge(S("y_hi_e"), passed("y_hi_e", p) + e * 2 + (2 * x + f + 1))
                    dve.scalar_tensor_tensor(y_lo[:, f * 512:f * 512 + 512], ps[3 + f][:, :], slot,
                                             y_hi[:, f * 512:f * 512 + 512], ALU.mult, ALU.subtract).then_inc(S("y_lo_e"), 1)

            def add_rows(e, x, k4):
                dve.wait_ge(S("sc_full"), passed("sc_full", p) + e * 4 + (4 * x + k4 + 5))
                for i in range(2):
                    kk = 2 * k4 + i
                    dve.scalar_tensor_tensor(xT[:, kk, SEQ:T], ps[5 + k4 % 2][:, i * SEQ:(i + 1) * SEQ],
                                             mod[:, 1, 1, 5 * KD + kk:5 * KD + kk + 1], xT[:, kk, SEQ:T],
                                             ALU.mult, ALU.add).then_inc(S("x_add"), 1)

            select(0, 0, first=True)
            dve.memset(eu[:, :, :], 0.0).then_inc(S("eu"), 2)
            dve.memset(w_slot[:, 1:2], 0.0).then_inc(S("w_slot"), 1)
            for t in range(2):
                ins = dve.tensor_scalar(selT[:, 1, t * P:(t + 1) * P], iota[:, :], 0.0, None, ALU.mult)
            ins.then_inc(S("selT"), 1)
            lo(0, 0)
            gathered_lo(0, 0)
            for w in range(1, SPLIT):
                lo(0, w)
            with dve.Fori(0, EXPERTS // PAIR) as e2:
                e = e2 * PAIR
                v0 = e2 * (PAIR * UNITS // STAGE)
                c_ = e2 * (PAIR * CHUNKS)
                for w in range(PAIR * UNITS):
                    x, c, kind = w // UNITS, w % UNITS // 3, STEPS[w % 3]
                    cc = x * CHUNKS + c
                    if kind == "ga":
                        if c in (SCATTER_AT[0] + 1, SCATTER_AT[1] + 1):
                            for k4 in range(2):
                                add_rows(e, x, 2 * (c - SCATTER_AT[0] - 1) + k4)
                        if c == GATHER_AT[1] + 1:
                            gathered_lo(e, x + 1)
                        hidden_lo(c_, cc - 1)
                    if kind == "gb":
                        dve.wait_ge(S("et"), passed("et", p) + c_ + (cc + 1))
                        dve.scalar_tensor_tensor(em[:, cc % 2, :], et[:, cc % 2, :], 1.0, ps[cc % 2][:, 0:CW], ALU.add, ALU.mult)\
                            .then_inc(S("em"), 1)
                        dve.wait_ge(S("em"), passed("em", p) + c_ + (cc + 1))
                        dve.scalar_tensor_tensor(eu[:, cc % 2, :], em[:, cc % 2, :], 0.5, ps[cc % 2][:, CW:2 * CW], ALU.mult, ALU.mult)\
                            .then_inc(S("eu"), 1)
                    if kind == "w" and c == 0:
                        rows_lo(e, x)
                    if kind == "w" and c == SCATTER_AT[1] + 1:
                        select(e, x + 1)
                    lo(v0, w + SPLIT)
            hidden_lo(EXPERTS * CHUNKS, -1)
            rows_lo(EXPERTS, 0)
            for k4 in range(KD // 2):
                add_rows(EXPERTS, 0, k4)
            dve.sem_inc(S("e_lo_done"), PASS_UNITS - EXPERTS * UNITS - SPLIT)

        experts(0)
        dve.wait_ge(S("x_add"), KD * (EXPERTS + 1))
        dve.wait_ge(S("most_ready"), 1)
        most_r = dve.value_load(most_i[0:1, 0:1], min_val=0, max_val=SEQ)
        with dve.If(most_r > SLOTS):
            experts(1)
            dve.wait_ge(S("x_add"), 2 * KD * (EXPERTS + 1))
        dve.sem_inc(S("experts_done"), 1)
        norm("fin", SEQ)

    @block.gpsimd
    def _(pool):

        def load_groups(first, last):
            for u in range(first, last):
                if u >= 2:
                    pool.wait_ge(S("acc_step"), 2 * (u - 1))
                pool.dma_start(gw[:, u % 2, :, :], A["groups"][u]).then_inc(S(f"group_in{u % 2}"), 16)

        before_windows = GROUP_UNITS * flushed(0)
        for layer in range(DEPTH):
            s0 = streams(layer)[0]
            lc = c0(layer)
            if layer == 0:
                load_groups(0, before_windows)
            pool.wait_ge(S("norm_hlo"), KD * nth(f"n1_{layer}") + KD)
            pool.memset(pool_in[:, :, :, :], 0.0).then_inc(S("pads"), 1)
            n = [0]

            def step(ins):
                n[0] += 1
                ins.then_inc(S("win"), 1)
                pool.wait_ge(S("win"), earlier("win", layer) + n[0])

            pool.wait_ge(S("tables"), 16 * TABLES)
            for g in range(GROUPS):
                pool.wait_ge(S("in_evac"), earlier("in_evac", layer) + 5 + GROUPS + g + 1)
                rows = pool_in[:, g, s0:2, :]
                src = rows
                for a in range(g + 1):
                    reach = 1 << a
                    start = (2 << a) - 1
                    dst = win[:, a % 2, s0:2, :]
                    step(pool.tensor_tensor(dst[:, :, start:PW], src[:, :, start:PW], src[:, :, start - reach:PW - reach], ALU.add))
                    src = dst
                at = PAD + (1 << g) - 1
                dst = win[:, (g + 1) % 2, s0:2, 0:SEQ]
                for s in range(s0, 2):
                    step(pool.tensor_tensor(win[:, (g + 1) % 2, s, 0:SEQ], win[:, g % 2, s, at:at + SEQ], inv_n[:, g, :], ALU.mult))
                if g == 0:
                    pool.wait_ge(S("lnorm"), earlier("lnorm", layer) + KKV + KQ)
                pool.tensor_tensor(mixed[:, 0, g, lc:T].rearrange("p (s t) -> p s t", t=SEQ), dst, rows[:, :, PAD:PAD + SEQ], ALU.subtract)\
                    .then_inc(S("mixed"), 1)
                pool.wait_ge(S("mixed"), earlier("mixed", layer) + g + 1)
            if layer == 0:
                load_groups(before_windows, GROUP_UNITS * len(MOD_GROUPS))

    @block.tensor
    def _(pe):
        at = [0]

        def block_passes(out, key, k, rhs_hi, rhs_lo, first, last):
            b = at[0]
            assert walk.first[key] + k == b or k < 0
            u, i = divmod(b, SPLIT_BLOCKS)
            if i == 0:
                pe.wait_ge(S("lo_done"), u + 1)
            hi, lo = whi[:, u % DENSE_SPLIT, i, :], wlo[:, u % DENSE_SPLIT, i, :]
            pe.matmul(out, hi, rhs_hi, start=first, stop=False)
            pe.matmul(out, hi, rhs_lo, start=False, stop=False)
            ins = pe.matmul(out, lo, rhs_hi, start=False, stop=last)
            if b in walk.number:
                ins.then_inc(S("walked"), 1)
            at[0] += 1
            return ins

        def direct_unit(key):
            n = direct_at[key]
            pe.wait_ge(S(f"direct_in{n % DIRECT}"), 16 * (n // DIRECT + 1))
            return n % DIRECT

        def early_mods():
            for j in range(EARLY_MODS):
                if j % 4 == 0:
                    pe.wait_ge(S(f"early_in{j // 4}"), 16 * 4)
                w = (mw_a, mw_b)[j // (EARLY_MODS // 2)]
                for k in range(KD):
                    ins = pe.matmul(ps[7][:, 2 * j:2 * j + 2], w[:, j % (EARLY_MODS // 2), k, :], cond_t[:, k, :], start=(k == 0), stop=(k == KD - 1))
                ins.then_inc(S("mod_tile"), 1)

        def mod_sums(*key):
            for n in sum_plan().get(key, []):
                layer, g = MOD_GROUPS[n]
                pe.wait_ge(S("acc_step"), KD * (n + 1))
                pe.wait_ge(S("mods"), 2 if n < flushed(0) else 4 if n < flushed(1) else 6)
                for t in range(GT):
                    for s in mod_streams(layer, g):
                        at = 2 * (GT * g + t) + s
                        ins = pe.matmul(ps[7][:, at:at + 1], acc[:, n % 2, s, t * P:(t + 1) * P], ones[:, 0:1], start=True, stop=True)
                ins.then_inc(S("mod_sum"), 1)

        def norm(tag, first):
            for k in range(KD):
                pe.wait_ge(S("norm_sq"), KD * nth(tag) + k + 1)
                pe.matmul(ps[6][:, 0:T - first], ones[:, :], sq[:, k % 2, 0:T - first], start=(k == 0), stop=(k == KD - 1))\
                    .then_inc(S("norm_ss"), 1)

        pe.wait_ge(S("cond"), 2)
        early_mods()
        pe.wait_ge(S("consts"), 16 * EARLY_CONSTS)
        for layer in range(DEPTH):
            lc = c0(layer)
            norm(f"n1_{layer}", 0)
            for j, name in enumerate(TILES):
                a = tile_c0(layer, j)
                if j >= 2:
                    if TILES[j - 2] == "kr":
                        pe.wait_ge(S("kr"), earlier("kr", layer) + 2)
                    else:
                        pe.wait_ge(S("in_evac"), earlier("in_evac", layer) + j - 1 - (1 if j - 2 > 2 else 0))
                for k in range(KD):
                    if j == 0:
                        pe.wait_ge(S("norm_hlo"), KD * nth(f"n1_{layer}") + k + 1)
                    block_passes(ps[j % 2][:, 0:T - a], ("in", layer, j), k, h_hi[:, k, a:T], h_lo[:, k, a:T], k == 0, k == KD - 1)
                if name == "fft0":
                    for i in range(KKV + KQ):
                        s0 = 0 if i < KKV else lc
                        first, last = i in (0, KKV), i in (KKV - 1, KKV + KQ - 1)
                        pe.wait_ge(S("lsq"), earlier("lsq", layer) + i + 1)
                        pe.matmul(ps[6 if i < KKV else 2][:, s0:T], ones[:, :], lsq[:, i % 2, s0:T], start=first, stop=last)\
                            .then_inc(S("lss"), 1)
                mod_sums("in", layer, j)
            if layer == 0:
                pe.wait_ge(S("tables"), 16 * TABLES)

            todo = [(s, g) for s in streams(layer) for g in range(GROUPS)]

            def channels(n):
                s, g = todo[n]
                if n == 0:
                    pe.wait_ge(S("in_evac"), earlier("in_evac", layer) + 5 + GROUPS)
                    pe.wait_ge(S("lvar"), earlier("lvar", layer) + 2)
                if n >= 2:
                    pe.wait_ge(S("fg"), earlier("fg", layer) + n - 1)
                for t in range(2):
                    c = s * SEQ + t * P
                    ins = pe.matmul(ps[2 + n % 2][:, t * 256:t * 256 + 256], pf[:, g, c:c + P], dft_c[:, :], start=True, stop=True)
                ins.then_inc(S("fa_full"), 1)

            def tokens(n):
                pe.wait_ge(S("fg"), earlier("fg", layer) + n + 1)
                if n >= 2:
                    pe.wait_ge(S("br_c"), earlier("br_c", layer) + n - 1)
                for t in range(2):
                    for part in range(2):
                        c = t * 256 + part * P
                        ins = pe.matmul(ps[4 + n % 2][:, 0:SEQ], fg[:, n % 2, c:c + P], dft_l[:, t, part, :],
                                        start=(t == 0 and part == 0), stop=(t == 1 and part == 1))
                ins.then_inc(S("fb_full"), 1)

            channels(0)
            for n in range(len(todo)):
                if n + 1 < len(todo):
                    channels(n + 1)
                tokens(n)
            slot = direct_unit(("pool", layer))
            for g in range(GROUPS):
                pe.wait_ge(S("mixed"), earlier("mixed", layer) + g + 1)
                if g < 2:
                    pe.wait_ge(S("br_c"), earlier("br_c", layer) + len(todo))
                else:
                    pe.wait_ge(S("br_b"), earlier("br_b", layer) + g - 1)
                pe.matmul(ps[4 + g % 2][:, 0:T - lc], dw[:, slot, g, :], mixed[:, 0, g, lc:T], start=True, stop=True)\
                    .then_inc(S("pool_full"), 1)
            slot = direct_unit(("v", layer))
            pe.wait_ge(S("lnorm"), earlier("lnorm", layer) + KKV + KQ)
            pe.wait_ge(S("fg"), earlier("fg", layer) + len(todo))
            for t in range(T // P):
                if t >= 2:
                    pe.wait_ge(S("v_sb"), earlier("v_sb", layer) + t - 1)
                for i in range(KKV):
                    ins = pe.matmul(ps[2 + t % 2][:, :], pkv[:, i, t * P:(t + 1) * P],
                                    dw[:, slot, 4 * i:4 * i + 4, :].rearrange("p a b -> p (a b)"), start=(i == 0), stop=(i == KKV - 1))
                ins.then_inc(S("v_full"), 1)

            todo_a = items(layer)
            per = len(todo_a) // HEADS

            def head(h):
                slot = direct_unit(("head", layer, h // 2))
                if h == 0:
                    pe.wait_ge(S("in_evac"), earlier("in_evac", layer) + NT - 1)
                else:
                    pe.wait_ge(S("qk_rows"), earlier("qk_rows", layer) + 2 * h)
                    pe.wait_ge(S("q_rope"), earlier("q_rope", layer) + 3 * h)
                o = 4 * (h % 2)
                for i in range(KQ):
                    pe.matmul(ps[0][:, 0:T - lc], dw[:, slot, o + i, :], pq[:, i, lc:T], start=(i == 0), stop=(i == KQ - 1))
                for i in range(KKV):
                    ins = pe.matmul(ps[1][0:NOPE, :], dw[:, slot, o + 3, i * 64:i * 64 + 64], pkv[:, i, :], start=(i == 0), stop=(i == KKV - 1))
                ins.then_inc(S("qk_full"), 1)

            def scores(n):
                h, q, keys = todo_a[n]
                if n % per == 0:
                    pe.wait_ge(S("qk_rows"), earlier("qk_rows", layer) + 2 * h + 2)
                    pe.wait_ge(S("q_rope"), earlier("q_rope", layer) + 3 * h + 3)
                    pe.wait_ge(S("kr"), earlier("kr", layer) + 4)
                if n < 2:
                    pe.wait_ge(S("v_sb"), earlier("v_sb", layer) + T // P)
                else:
                    pe.wait_ge(S("prob"), earlier("prob", layer) + n - 1)
                pe.matmul(ps[2 + n % 2][:, 0:keys], qT[0:QK, h % 2, q * P:(q + 1) * P], kT[0:QK, h % 2, 0:keys], start=True, stop=True)\
                    .then_inc(S("s_full"), 1)

            def turn(n):
                _, _, keys = todo_a[n]
                pe.wait_ge(S("pn"), earlier("pn", layer) + n + 1)
                if n < 2:
                    pe.wait_ge(S("br_b"), earlier("br_b", layer) + GROUPS)
                else:
                    pe.wait_ge(S("pT"), earlier("pT", layer) + n - 1)
                for t in range(keys // P):
                    ins = pe.transpose(ps[4 + n % 2][:, t * P:(t + 1) * P], prob[:, n % 3, t * P:(t + 1) * P], ident[:, :])
                ins.then_inc(S("t_full"), 1)

            def values(n):
                h, q, keys = todo_a[n]
                pe.wait_ge(S("pT"), earlier("pT", layer) + n + 1)
                if n % per == 0:
                    if h < 2:
                        pe.wait_ge(S("mods"), 4)
                        pe.wait_ge(S("lvar"), earlier("lvar", layer) + 1)
                    else:
                        pe.wait_ge(S("br_a"), earlier("br_a", layer) + h - 1)
                for t in range(keys // P):
                    ins = pe.matmul(ps[6 + h % 2][0:64, q * P:(q + 1) * P], v_sb[:, t, h * VD:(h + 1) * VD],
                                    pT[:, n % 2, t * P:(t + 1) * P], start=(t == 0), stop=(t == keys // P - 1))
                ins.then_inc(S("pv"), 1)

            head(0)
            for n in range(len(todo_a) + 2):
                if n < len(todo_a):
                    scores(n)
                    if n % per == 0 and todo_a[n][0] + 1 < HEADS:
                        head(todo_a[n][0] + 1)
                if n >= 2:
                    turn(n - 2)
                    values(n - 2)

            for m in range(KD * BRANCHES):
                j, b = divmod(m, BRANCHES)
                if m < 2:
                    pe.wait_ge(S("qk_rows"), earlier("qk_rows", layer) + 2 * HEADS)
                    pe.wait_ge(S("q_rope"), earlier("q_rope", layer) + 3 * HEADS)
                else:
                    pe.wait_ge(S("gate"), earlier("gate", layer) + m - 1)
                for k in range(KD):
                    block_passes(ps[m % 2][:, 0:T - lc], ("gate", layer, m), k, h_hi[:, k, lc:T], h_lo[:, k, lc:T], k == 0, k == KD - 1)
                slot = direct_unit(("proj", layer, m // 2))
                if m < 2:
                    pe.wait_ge(S("prob"), earlier("prob", layer) + len(todo_a))
                    pe.wait_ge(S("br_a"), earlier("br_a", layer) + HEADS)
                else:
                    pe.wait_ge(S("o_used"), earlier("o_used", layer) + m - 1)
                for k in range(KB):
                    ins = pe.matmul(ps[2 + m % 2][:, 0:T - lc], dw[:, slot, 4 * (m % 2) + k, :], br[:, b, k, lc:T], start=(k == 0), stop=(k == KB - 1))
                ins.then_inc(S("o_full"), 1)
                mod_sums("gate", layer, m)
            for j in range(KD):
                if j < 2:
                    pe.wait_ge(S("pT"), earlier("pT", layer) + len(todo_a))
                else:
                    pe.wait_ge(S("x_mix"), earlier("x_mix", layer) + j - 1)
                for k in range(KD):
                    if j == 0:
                        pe.wait_ge(S("y_lo"), earlier("y_lo", layer) + k + 1)
                    block_passes(ps[4 + j % 2][:, 0:T - lc], ("out", layer, j), k, h_hi[:, k, lc:T], h_lo[:, k, lc:T], k == 0, k == KD - 1)
                mod_sums("out", layer, j)
            norm(f"n2_{layer}", lc)
            if layer == 0:
                for half, ks in enumerate(DOWN):
                    for i in ks:
                        if i < 2:
                            pe.wait_ge(S("o_used"), KD * BRANCHES)
                        else:
                            pe.wait_ge(S("fu"), i - 1)
                        for w, key in enumerate(("upg", "upu")):
                            for k in range(KD):
                                if i == 0 and w == 0:
                                    pe.wait_ge(S("norm_hlo"), KD * nth("n2_0") + k + 1)
                                block_passes(ps[2 * w + i % 2][:, :], (key, i), k, h_hi[:, k, :], h_lo[:, k, :], k == 0, k == KD - 1)
                        mod_sums("upu", i)
                    for j in range(KD):
                        if half == 0 and j < 2:
                            pe.wait_ge(S("x_mix"), KD)
                        else:
                            pe.wait_ge(S("x_ffn"), KD * half + j - 1)
                        if j == 0:
                            pe.wait_ge(S("u_lo"), ks[-1] + 1)
                        for n, i in enumerate(ks):
                            block_passes(ps[4 + j % 2][:, :], ("down", half, j), n, u_hi[:, i % USLOTS, :], u_lo[:, i % USLOTS, :], n == 0, n == len(ks) - 1)
                        mod_sums("down", half, j)

        pe.wait_ge(S("norm_hhi"), KD * nth("n2_1") + KD)
        for t in range(2):
            for k in range(KD):
                ins = pe.matmul(ps[7][:, t * 8:t * 8 + 8], hslot(k, SEQ)[:, t * P:(t + 1) * P], router[:, k, :], start=(k == 0), stop=(k == KD - 1))
        ins.then_inc(S("lg_full"), 1)
        pe.wait_ge(S("norm_hlo"), KD * nth("n2_1") + KD)
        for n in range(8):
            part, t, f = n // 4, n // 2 % 2, n % 2
            if n >= 2:
                pe.wait_ge(S("htok"), n - 1)
            else:
                pe.wait_ge(S("gate"), earlier("gate", 1) + KD * BRANCHES)
            src = (h_hi, h_lo)[part][:, :, :].bitcast(F32)
            for i in range(4):
                ins = pe.transpose(ps[n % 2][:, i * P:(i + 1) * P], src[:, 4 * f + i, SEQ + t * P:SEQ + (t + 1) * P], ident[:, :])
            ins.then_inc(S("ht_full"), 1)
        pe.wait_ge(S("mask"), 2)
        pe.matmul(ps[7][:, 32:40], before[:, :], mask[:, 0, :], start=True, stop=True)
        pe.matmul(ps[7][:, 40:48], before[:, :], mask[:, 1, :], start=True, stop=False)
        pe.matmul(ps[7][:, 40:48], ones[:, :], mask[:, 0, :], start=False, stop=True)
        pe.matmul(ps[7][:, 48:56], ones[:, :], mask[:, 0, :], start=True, stop=False)
        pe.matmul(ps[7][:, 48:56], ones[:, :], mask[:, 1, :], start=False, stop=True).then_inc(S("cnt_full"), 1)
        pe.wait_ge(S("htok"), 8)
        pe.wait_ge(S("most_ready"), 1)

        def experts(p):
            used = S("e_used")
            if p == 1:
                pe.wait_ge(S("x_add"), KD * (EXPERTS + 1))
            else:
                pe.sem_inc(S("sc_full"), 4)

            def gather(e, x, part, first=False):
                for f in range(2):
                    if part == 0:
                        if f == 0:
                            pe.wait_ge(S("sel"), passed("sel", p) + e * 2 + 2 * (x + 1))
                        if not first:
                            pe.wait_ge(S("x_add"), passed("x_add", p) + e * KD + KD * x)
                    else:
                        pe.wait_ge(S("xg_hi"), passed("xg_hi", p) + e * 2 + (2 * x + f + 1))
                    for k in range(4):
                        for t in range(2):
                            ins = pe.matmul(ps[5 + f][:, k * SLOTS:(k + 1) * SLOTS], (htok_hi, htok_lo)[part][:, t, (4 * f + k) * P:(4 * f + k + 1) * P],
                                            sel[:, t, :], start=(t == 0), stop=(t == 1))
                    ins.then_inc(S("ga_full"), 1)
                if part == 0:
                    return
                pe.wait_ge(S("selT"), passed("selT", p) + e + (x + 1))
                pe.wait_ge(S("w_slot"), passed("w_slot", p) + e + (x + 1))
                for t in range(2):
                    pe.transpose(ps[7][:, t * P:(t + 1) * P], sel[:, t, :].bitcast(F32), ident[:, :])
                for t in range(2):
                    at = comb[:, t, 0:1] if first else comb[:, t, bass.ds(e + x, 1)]
                    ins = pe.matmul(ps[7][:, SEQ:SEQ + 1], sel[:, t, :].bitcast(F32), at, start=(t == 0), stop=(t == 1))
                ins.then_inc(S("st_full"), 1)

            def turn(c_, pc):
                pe.wait_ge(S("eu"), passed("eu", p) + c_ + (pc + 3))
                for i in range(2):
                    ins = pe.transpose(ps[2][:, pc % 2 * 256 + i * P:pc % 2 * 256 + (i + 1) * P], eu[:, pc % 2, i * P:(i + 1) * P], ident[:, :])
                ins.then_inc(S("tr_full"), 1)

            def split_unit(v0, w):
                pe.wait_ge(S("e_lo_done"), passed("e_lo_done", p) + v0 + (STAGE + w + 1))
                return ehi[:, w % SPLIT, :], elo[:, w % SPLIT, :]

            def up(c_, cc, x, v0, w, second):
                hi, lo = split_unit(v0, w)
                for i in range(4):
                    kk = i + 4 * second
                    o = ps[cc % 2][:, :]
                    cols = slice(i * 512, i * 512 + 512)
                    pe.matmul(o, xg_hi[:, x % 2, kk, :], hi[:, cols], start=(kk == 0), stop=False)
                    pe.matmul(o, xg_hi[:, x % 2, kk, :], lo[:, cols], start=False, stop=False)
                    ins = pe.matmul(o, xg_lo[:, x % 2, kk, :], hi[:, cols], start=False, stop=(kk == KD - 1))
                ins.then_inc(used, 1)

            def down(c_, pc, c, v0, w):
                hi, lo = split_unit(v0, w)
                pe.wait_ge(S("ehT_lo"), passed("ehT_lo", p) + c_ + (pc + 2))
                for i in range(2):
                    a_hi, a_lo = ehT_hi[:, pc % 2, i, :], ehT_lo[:, pc % 2, i, :]
                    first, last = c == 0 and i == 0, c == CHUNKS - 1 and i == 1
                    for f in range(2):
                        cols = slice(i * D + f * 512, i * D + f * 512 + 512)
                        pe.matmul(ps[3 + f][:, :], a_hi, hi[:, cols], start=first, stop=False)
                        pe.matmul(ps[3 + f][:, :], a_hi, lo[:, cols], start=False, stop=False)
                    for f in range(2):
                        cols = slice(i * D + f * 512, i * D + f * 512 + 512)
                        ins = pe.matmul(ps[3 + f][:, :], a_lo, hi[:, cols], start=False, stop=last)
                ins.then_inc(used, 1)

            def scatter(e, x, fills):
                if 0 in fills:
                    pe.wait_ge(S("y_lo_e"), passed("y_lo_e", p) + e * 2 + 2 * (x + 1))
                    pe.wait_ge(S("selT"), passed("selT", p) + e + (x + 1))
                for k4 in fills:
                    if k4 < 2:
                        pe.wait_ge(S("xg_lo"), passed("xg_lo", p) + e * 2 + (2 * x + k4 + 1))
                    else:
                        pe.wait_ge(S("x_add"), passed("x_add", p) + e * KD + (KD * x + 2 * (k4 - 1)))
                    for i in range(2):
                        kk = 2 * k4 + i
                        o = ps[5 + k4 % 2][:, i * SEQ:(i + 1) * SEQ]
                        pe.matmul(o, y_hi[:, kk * P:(kk + 1) * P], selT[:, (x - 1) % 2, :], start=True, stop=False)
                        ins = pe.matmul(o, y_lo[:, kk * P:(kk + 1) * P], selT[:, (x - 1) % 2, :], start=False, stop=True)
                    ins.then_inc(S("sc_full"), 1)

            gather(0, 0, 0, first=True)
            gather(0, 0, 1, first=True)
            for f in range(2):
                pe.matmul(ps[3 + f][:, :], selT[:, 1, 0:P], htok_hi[:, 0, 0:512], start=True, stop=False)
            with pe.Fori(0, EXPERTS // PAIR) as e2:
                e = e2 * PAIR
                v0 = e2 * (PAIR * UNITS)
                c_ = e2 * (PAIR * CHUNKS)
                for w in range(PAIR * UNITS):
                    x, c, kind = w // UNITS, w % UNITS // 3, STEPS[w % 3]
                    cc = x * CHUNKS + c
                    if kind == "ga":
                        if c == 0:
                            pe.wait_ge(S("xg_hi"), passed("xg_hi", p) + e * 2 + 2 * (x + 1))
                            pe.wait_ge(S("xg_lo"), passed("xg_lo", p) + e * 2 + 2 * (x + 1))
                        pe.wait_ge(S("eu"), passed("eu", p) + c_ + (cc + 1))
                        up(c_, cc, x, v0, w, 0)
                    elif kind == "gb":
                        turn(c_, cc - 1)
                        up(c_, cc, x, v0, w, 1)
                    else:
                        if c == 1:
                            pe.wait_ge(S("y_lo_e"), passed("y_lo_e", p) + e * 2 + 2 * (x + 1))
                        down(c_, cc - 1, (c - 1) % CHUNKS, v0, w)
                        if c in SCATTER_AT:
                            scatter(e, x, (0, 1) if c == SCATTER_AT[0] else (2, 3))
                        if c in GATHER_AT:
                            gather(e, x + 1, GATHER_AT.index(c))
            turn(EXPERTS * CHUNKS, -1)
            down(EXPERTS * CHUNKS, -1, CHUNKS - 1, EXPERTS * UNITS, 0)
            scatter(EXPERTS, 0, range(KD // 2))
            pe.sem_inc(used, PASS_UNITS - EXPERTS * UNITS - 1)

        experts(0)
        most_r = pe.value_load(most_i[0:1, 0:1], min_val=0, max_val=SEQ)
        with pe.If(most_r > SLOTS):
            experts(1)
        pe.wait_ge(S("experts_done"), 1)
        norm("fin", SEQ)

    ctx_block.__exit__(None, None, None)


def _blocks(w):
    k, c = w.shape[0] // P, w.shape[1] // P
    return w.reshape(k, P, c, P).transpose(0, 2, 1, 3)


def _constants():
    import numpy as np

    t = np.arange(SEQ)
    half = ROPE // 2
    inv = (10000.0 ** (-np.arange(0, half, 2) / half)).astype(np.float32)
    pos = np.stack([t // 64, t % 64], axis=1).astype(np.float32)
    ang = (pos[:, :, None] * inv).astype(np.float32)
    cos, sin = np.cos(ang), np.sin(ang)
    rope = np.zeros((P, T), np.float32)
    for r in range(ROPE):
        axis, second, f = r // 16, r // 8 % 2, r % 8
        rope[NOPE + r, 0:SEQ] = 1.0
        rope[NOPE + r, SEQ:T] = cos[:, axis, f]
        rope[QK + r, SEQ:T] = sin[:, axis, f] if second else -sin[:, axis, f]
    c = np.arange(P)
    a = 2 * np.pi * np.outer(c, c) / P
    dft_c = np.concatenate([np.cos(a), np.sin(a)], axis=1) / np.sqrt(P)
    b = 2 * np.pi * np.outer(t, t) / SEQ
    dft_l = np.stack([np.cos(b), -np.sin(b)], axis=1) / np.sqrt(SEQ)
    dft_l = dft_l.reshape(2, P, 2, SEQ).transpose(1, 0, 2, 3)
    inv_n = np.zeros((P, GROUPS, SEQ), np.float32)
    for g, w in enumerate((2, 4, 8, 16)):
        left = w // 2
        right = w - 1 - left
        inv_n[:, g, :] = 1.0 / (np.minimum(t + right + 1, SEQ) - np.maximum(t - left, 0))
    out = {
        "ones": np.ones((P, P)), "ident": np.eye(P), "iota": np.tile(np.arange(P), (P, 1)),
        "before": np.triu(np.ones((P, P)), 1), "rope": rope, "dft_c": dft_c, "dft_l": dft_l, "inv_n": inv_n,
    }
    return {k: np.ascontiguousarray(v, dtype=np.float32) for k, v in out.items()}


def layout(i):
    import numpy as np

    i = {k: np.asarray(v) for k, v in i.items()}
    off_kv, off_kr = Q_LORA, Q_LORA + KV_LORA
    off_pool = off_kr + ROPE
    off_fft = off_pool + BRANCH_W
    off_gate = off_fft + BRANCH_W
    partner = np.arange(ROPE) ^ 8

    def cols(v):
        v = v.reshape(*v.shape[:-1], v.shape[-1] // P, P)
        return np.moveaxis(v, -1, 0)

    def tile_columns(layer, name):
        w = i["w_in"][layer]
        g = int(name[-1]) if name[-1].isdigit() else 0
        if name == "kr":
            kr = w[:, off_kr:off_pool]
            return np.concatenate([kr, kr[:, partner], kr, kr[:, partner]], axis=1)
        at = {"kv": off_kv, "q": 0, "fft": off_fft, "pool": off_pool}[name[:-1]] + g * P
        return w[:, at:at + P]

    split = []
    for key, _ in split_stream():
        kind = key[0]
        if kind == "in":
            b = _blocks(tile_columns(key[1], TILES[key[2]]))
        elif kind == "gate":
            j, br = divmod(key[2], BRANCHES)
            at = off_gate + br * D + j * P
            b = _blocks(i["w_in"][key[1]][:, at:at + P])
        elif kind == "out":
            b = _blocks(i["w_out"][key[1]][:, key[2] * P:(key[2] + 1) * P])
        elif kind in ("upg", "upu"):
            w = i["ffn_w1" if kind == "upg" else "ffn_w3"][0]
            b = _blocks(w[:, key[1] * P:(key[1] + 1) * P])
        else:
            ks = DOWN[key[1]]
            b = _blocks(i["ffn_w2"][0][ks[0] * P:(ks[-1] + 1) * P, key[2] * P:(key[2] + 1) * P])
        split.append(b[:, 0])
    split = np.concatenate(split, axis=0)
    split = split.reshape(-1, SPLIT_BLOCKS, P, P).transpose(0, 2, 1, 3).reshape(-1, P, SPLIT_BLOCKS * P)

    direct = []
    for key in direct_stream():
        kind, layer = key[0], key[1]
        unit = np.zeros((P, DIRECT_BLOCKS, P), np.float32)
        if kind == "pool":
            unit[:, 0:GROUPS] = i["w_pool"][layer].transpose(1, 0, 2)
        elif kind == "v":
            v = i["w_ukv"][layer][:, :, NOPE:].reshape(KKV, P, HEADS * VD)
            unit[:] = v.transpose(1, 0, 2).reshape(P, DIRECT_BLOCKS, P)
        elif kind == "head":
            for x in range(2):
                h = 2 * key[2] + x
                q = i["w_uq"][layer][:, h, :]
                q = np.concatenate([q, q[:, NOPE:][:, partner]], axis=1)
                unit[:, 4 * x:4 * x + KQ] = _blocks(q)[:, 0].transpose(1, 0, 2)
                k = i["w_ukv"][layer][:, h, 0:NOPE].reshape(KKV, P, NOPE)
                unit[:, 4 * x + 3] = k.transpose(1, 0, 2).reshape(P, P)
        else:
            for x in range(2):
                j, b = divmod(2 * key[2] + x, BRANCHES)
                w = i[("w_oa", "w_ob", "w_oc")[b]][layer]
                unit[:, 4 * x:4 * x + 4] = _blocks(w[:, j * P:(j + 1) * P])[:, 0].transpose(1, 0, 2)
        direct.append(unit)

    early = np.stack([_blocks(i["w_mod"][0][:, j * P:(j + 1) * P])[:, 0].transpose(1, 0, 2) for j in range(EARLY_MODS)])
    groups = []
    for layer, g in MOD_GROUPS:
        w = i["w_mod"][layer][:, g * GC:(g + 1) * GC].reshape(GROUP_UNITS, 2, P, GC)
        groups.append(w.transpose(0, 2, 1, 3))
    groups = np.concatenate(groups)

    up = np.stack([i["moe_w1"][0], i["moe_w3"][0]], axis=0)
    up = up.reshape(2, EXPERTS, 2, 4, P, CHUNKS, CW).transpose(1, 5, 2, 4, 3, 0, 6)
    up = up.reshape(EXPERTS, CHUNKS, 2, P, 4 * 2 * CW)
    down = i["moe_w2"][0].reshape(EXPERTS, CHUNKS, 2, P, D).transpose(0, 1, 3, 2, 4).reshape(EXPERTS * CHUNKS, P, 2 * D)
    moe = np.zeros((MOE_UNITS, P, 2 * D), np.float32)
    moe[0:-1:3] = up[:, :, 0].reshape(EXPERTS * CHUNKS, P, 2 * D)
    moe[1::3] = up[:, :, 1].reshape(EXPERTS * CHUNKS, P, 2 * D)
    moe[5::3] = down[:-1]
    moe[-1] = down[-1]

    gains = np.concatenate([np.stack([i["g_norm1"], i["g_norm2"]], axis=1).reshape(2 * DEPTH, D), i["g_final"][None]], axis=0)
    x = np.concatenate([i["ctx"][0], i["x"][0]], axis=0)
    out = {
        "x": cols(x).transpose(0, 2, 1), "cond": cols(np.stack([i["c_ctx"], i["c"][0]], axis=0)).transpose(0, 2, 1),
        "b_mod": cols(i["b_mod"]), "gains": cols(gains), "b_gate": cols(i["b_gate"]), "s_pool": cols(i["s_pool"]),
        "g_q": cols(i["g_q"]), "g_kv": cols(i["g_kv"]),
        "router": i["moe_router"][0].reshape(KD, P, EXPERTS).transpose(1, 0, 2),
        "r_bias": np.broadcast_to(i["moe_bias"][0], (P, EXPERTS)),
        "split": split, "direct": np.stack(direct), "early": early, "groups": groups, "moe": moe,
    }
    return {k: np.ascontiguousarray(v) for k, v in out.items()} | _constants()


def kernel(**inputs):
    import concourse.bacc as bacc
    import numpy as np
    from concourse.bass_utils import run_bass_kernel_spmd

    arrays = layout(inputs)
    nc = bacc.Bacc("TRN2", target_bir_lowering=False, num_devices=1)
    aps = {k: nc.dram_tensor(f"in_{k}", v.shape, mybir.dt.from_np(v.dtype), kind="ExternalInput").ap() for k, v in arrays.items()}
    aps["out"] = nc.dram_tensor("out_x", (P, KD, SEQ), F32, kind="ExternalOutput").ap()
    build(nc, aps)
    r = run_bass_kernel_spmd(nc, [{f"in_{k}": v for k, v in arrays.items()}], core_ids=[0])
    y = r.results[0]["out_x"]
    return np.ascontiguousarray(y.transpose(2, 1, 0)).reshape(1, SEQ, D)
```

```python
import concourse.bass as bass
from concourse import mybir
from concourse.alu_op_type import AluOpType as ALU

ACT = mybir.ActivationFunctionType
F32 = mybir.dt.float32
F32R = mybir.dt.float32r
I32 = mybir.dt.int32
U32 = mybir.dt.uint32
AX = mybir.AxisListType.X

P = 128
D = 1024
KD = D // P
SEQ = 256
T = 2 * SEQ
DEPTH = 2
HEADS = 8
NOPE = 64
ROPE = 32
QK = NOPE + ROPE
VD = 64
Q_LORA = 384
KV_LORA = 256
KQ = Q_LORA // P
KKV = KV_LORA // P
SCALE = float(QK) ** -0.5
GROUPS = 4
PAD = 8
PW = SEQ + 2 * PAD
BRANCH_W = 512
KB = BRANCH_W // P
BRANCHES = 3
FF = 2816
NF = FF // P
EXPERTS = 8
EPS = 1e-6
MODS = 6 * KD

SPLIT_BLOCKS = 16
DIRECT_BLOCKS = 8
STAGE = 11
SPLIT = 3
DIRECT = 3
DENSE_STAGE = 3
DENSE_SPLIT = 2

TILES = ["kv0", "kv1", "kr", "q0", "q1", "q2"] + [f"fft{g}" for g in range(GROUPS)] + [f"pool{g}" for g in range(GROUPS)]
NT = len(TILES)
MERGE = [(j, b) for j in range(KD) for b in (1, 2)] + [(j, 0) for j in range(KD)]
NM = len(MERGE)
BESIDE = 2 * KD
UP_FIRST = 12
DOWN = [list(range(UP_FIRST)), list(range(UP_FIRST, NF))]
USLOTS = UP_FIRST

CW = 256
CHUNKS = FF // CW
STEPS = ("ga", "gb", "w")
UNITS = len(STEPS) * CHUNKS
PAIR = 2
SLOTS = 128
MOE_UNITS = EXPERTS * UNITS + 1
PASS_UNITS = -(-(EXPERTS * UNITS + SPLIT) // (STAGE * SPLIT)) * STAGE * SPLIT
SCATTER_AT = (1, 2)
GATHER_AT = (4, 6)


def split_stream():
    tiles = []
    for layer in range(DEPTH):
        tiles += [(("in", layer, j), KD) for j in range(NT)]
        tiles += [(("gate", layer, m), KD) for m in range(KD * BRANCHES)]
        tiles += [(("out", layer, j), KD) for j in range(KD)]
        if layer == 0:
            for half, ks in enumerate(DOWN):
                tiles += [((name, i), KD) for i in ks for name in ("upg", "upu")]
                tiles += [(("down", half, j), len(ks)) for j in range(KD)]
    return tiles


TOGETHER = [(("in", layer, 0), ("in", layer, 1)) for layer in range(DEPTH)] + [(("upg", 0), ("upu", 0))]


class Walk:

    def __init__(self):
        self.first, self.step, at, ends = {}, {}, 0, set()
        for key, n in split_stream():
            pair = [p for p in TOGETHER if key in p]
            step = 2 if pair else 1
            start = at - n + 1 if pair and key == pair[0][1] else at
            self.first[key], self.step[key] = start, step
            at += n
            last = start + step * (n - 1)
            ends.add(last)
            self.first[key + ("end",)] = last
        self.blocks = at
        self.units = at // SPLIT_BLOCKS
        assert at % SPLIT_BLOCKS == 0
        ends |= {SPLIT_BLOCKS * (u + 1) - 1 for u in range(self.units)}
        self.marks = sorted(ends)
        self.number = {b: n + 1 for n, b in enumerate(self.marks)}

    def block(self, key, k):
        return self.first[key] + self.step[key] * k

    def tile(self, *key):
        return self.number[self.first[key + ("end",)]]

    def unit(self, u):
        return self.number[SPLIT_BLOCKS * (u + 1) - 1]

    def units_up_to(self, *key):
        return self.first[key + ("end",)] // SPLIT_BLOCKS + 1


EARLY_MODS = KD
GC = 512
GT = GC // P
GROUP_UNITS = KD // 2
EARLY_GROUPS = EARLY_MODS // GT
EARLY_UNITS = EARLY_GROUPS * GROUP_UNITS
START_UNITS = 2 * GROUP_UNITS
MOD_GROUPS = [(0, g) for g in range(EARLY_MODS // GT, MODS // GT)] + [(1, g) for g in range(MODS // GT)]


def mod_streams(layer, g):
    return (1,) if layer == 1 and g >= 2 * KD // GT else (0, 1)


def mod_plan():
    plan = {("start", 0): START_UNITS // 2, ("start", 1): START_UNITS // 2}
    plan |= {("in", 0, j): n for j, n in enumerate((1, 1, 1, 1, 1, 1, 0, 0, 0, 0, 1, 0, 1, 0))}
    plan |= {("gate", 0, m): 1 + m % 2 for m in range(BESIDE, NM)}
    plan |= {("out", 0, j): 1 for j in range(4)}
    plan |= {("upu", i): 3 if 12 <= i < 18 else 2 for i in range(NF) if i != 4}
    plan |= {("down", 0, j): 1 for j in range(KD)}
    return plan


MOD_FLUSH = [("start", 1), ("in", 0, NT - 1), ("out", 0, KD - 2), ("upu", 4), ("down", 1, 3)]


def sum_plan():
    tiles = [("start", 0), ("start", 1)] + [key for key, _ in split_stream()]
    plan, done, at = {}, 0, 0
    for key in tiles:
        at += mod_plan().get(key, 0)
        upto = (at if key in MOD_FLUSH or key[0] == "start" else at - 3) // GROUP_UNITS
        if upto > done:
            plan[key] = list(range(done, upto))
            done = upto
    assert done == len(MOD_GROUPS)
    return plan


def flushed(n):
    tiles = [("start", 0), ("start", 1)] + [key for key, _ in split_stream()]
    return sum(len(v) for key, v in sum_plan().items() if tiles.index(key) <= tiles.index(MOD_FLUSH[n]))


def direct_stream():
    out = []
    for layer in range(DEPTH):
        out += [("pool", layer), ("v", layer), ("head", layer, 0)]
        for h in range(HEADS):
            if h % 2 == 1 and h + 1 < HEADS:
                out.append(("head", layer, (h + 1) // 2))
            out.append(("proj", layer, h))
        out += [("proj", layer, n) for n in range(HEADS, NM // 2)]
    return out


_ITEMS = HEADS * T // P
FIRST_LAYER = {
    "in_evac": NT - 1, "kr": 4, "lsq": KKV + KQ, "lss": KKV + KQ, "lvar": 2, "lstd": 2, "lrstd": 2, "lnorm": KKV + KQ,
    "fa_full": 2 * GROUPS, "fg": 2 * GROUPS, "fb_full": 2 * GROUPS, "br_c": 2 * GROUPS,
    "pads": 1, "win": sum(g + 3 for g in range(GROUPS)), "mixed": GROUPS, "pool_full": GROUPS, "br_b": GROUPS,
    "v_full": T // P, "v_sb": T // P, "qk_full": 2 * HEADS, "qk_rows": 2 * HEADS, "q_rope": 3 * HEADS,
    "s_full": _ITEMS, "max": _ITEMS, "neg_max": _ITEMS, "prob": _ITEMS, "rden": _ITEMS, "pn": _ITEMS,
    "t_full": _ITEMS, "pT": _ITEMS, "pv": _ITEMS, "br_a": HEADS,
    "gate": KD * BRANCHES, "o_full": KD * BRANCHES, "o_used": KD * BRANCHES, "y_add": 2 * KD,
    "y_hi": KD, "y_lo": KD, "x_mix": KD, "mods": 8,
}
_CHUNKS, _GATHERS = EXPERTS * CHUNKS, EXPERTS + 1
FIRST_PASS = {
    "e_in": 16 * PASS_UNITS // STAGE, "e_hi_done": PASS_UNITS, "e_lo_done": PASS_UNITS, "e_used": PASS_UNITS,
    "et": _CHUNKS, "eu": _CHUNKS + 2, "tr_full": _CHUNKS + 1, "ehT_hi": _CHUNKS + 1, "ehT_lo": _CHUNKS + 1,
    "sel": 2 * _GATHERS, "ga_full": 4 * _GATHERS, "xg_hi": 2 * _GATHERS, "xg_lo": 2 * _GATHERS,
    "st_full": _GATHERS, "selT": _GATHERS + 1, "w_slot": _GATHERS + 1,
    "y_hi_e": 2 * _GATHERS, "y_lo_e": 2 * _GATHERS, "sc_full": 4 * _GATHERS, "x_add": KD * _GATHERS,
}


def load_order(walk, direct_at):
    out, seen = [], set()

    def add(item):
        if item not in seen:
            seen.add(item)
            out.append(item)

    def tile(*key):
        for u in range(walk.first[key] // SPLIT_BLOCKS, walk.first[key + ("end",)] // SPLIT_BLOCKS + 1):
            add(("s", u))

    for layer in range(DEPTH):
        for j in range(NT):
            tile("in", layer, j)
        for m in range(2 * DENSE_SPLIT):
            tile("gate", layer, m)
        for key in [("pool", layer), ("v", layer), ("head", layer, 0)]:
            add(("d", direct_at[key]))
        for m in range(KD * BRANCHES):
            tile("gate", layer, m)
            if m % 4 == 2 and m < 2 * (HEADS - 1):
                add(("d", direct_at[("head", layer, m // 4 + 1)]))
            add(("d", direct_at[("proj", layer, m // 2)]))
        for j in range(KD):
            tile("out", layer, j)
        if layer == 0:
            for half, ks in enumerate(DOWN):
                for i in ks:
                    tile("upg", i)
                    tile("upu", i)
                for j in range(KD):
                    tile("down", half, j)
    assert len(out) == walk.units + len(direct_at)
    return out


def build(nc, A):
    walk = Walk()
    direct = direct_stream()
    direct_at = {key: n for n, key in enumerate(direct)}

    base = -(-nc.sbuf_base // 32) * 32
    end = nc.sbuf_usable_end

    class Region:

        def __init__(self, at):
            self.at = at

        def take(self, name, shape, dtype=F32):
            size = 4
            for n in shape[1:]:
                size *= n
            t = nc.alloc_sbuf_tensor_at(name, shape, dtype, offset=self.at)
            self.at = -(-(self.at + size) // 32) * 32
            assert self.at <= end, (name, self.at - end)
            return t

    fixed = Region(base)
    xT = fixed.take("xT", [P, KD, T])
    y_rows = Region(base).take("y_rows", [P, KD, T], F32R)
    ones = fixed.take("ones", [P, P])
    ident = fixed.take("ident", [P, P])
    iota = fixed.take("iota", [P, P])
    before = fixed.take("before", [P, P])
    cond_in = fixed.take("cond_in", [P, KD, 2])
    cond_t = fixed.take("cond_t", [P, KD, 2])
    cond = fixed.take("cond", [P, KD, 2])
    mod = fixed.take("mod", [P, DEPTH, 2, MODS])
    b_mod = fixed.take("b_mod", [P, DEPTH, MODS])
    gains = fixed.take("gains", [P, 2 * DEPTH + 1, KD])
    coef = fixed.take("coef", [P, 2 * DEPTH, 2, KD])
    b_gate = fixed.take("b_gate", [P, DEPTH, BRANCHES * KD])
    half_b = fixed.take("half_b", [P, DEPTH, BRANCHES * KD])
    s_pool = fixed.take("s_pool", [P, DEPTH, GROUPS])
    g_q = fixed.take("g_q", [P, DEPTH, KQ])
    g_kv = fixed.take("g_kv", [P, DEPTH, KKV])
    router = fixed.take("router", [P, KD, EXPERTS])
    r_bias = fixed.take("r_bias", [P, EXPERTS])
    stat = fixed.take("stat", [P, 4, 4])
    phase = fixed.at

    dense = Region(phase)
    stage = dense.take("stage", [P, DENSE_STAGE, SPLIT_BLOCKS * P])
    whi = dense.take("whi", [P, DENSE_SPLIT, SPLIT_BLOCKS, P], F32R)
    wlo = dense.take("wlo", [P, DENSE_SPLIT, SPLIT_BLOCKS, P], F32R)
    dw = dense.take("dw", [P, DIRECT, DIRECT_BLOCKS, P])
    gw_at = dense.at
    gw = dense.take("gw", [P, 2, 2, GC])
    acc = dense.take("acc", [P, 2, 2, GC])
    aside = Region(gw_at)
    qT = aside.take("qT", [P, 2, T])
    prob = aside.take("prob", [P, 2, T])
    pT = aside.take("pT", [P, 2, T])
    v_a = aside.take("v_a", [P, 2, HEADS * VD])
    assert aside.at == dense.at
    rope = dense.take("rope", [P, T])
    tables_at = dense.at
    dft_c = dense.take("dft_c", [P, 2 * P])
    dft_l = dense.take("dft_l", [P, 2, 2, SEQ])
    inv_n = dense.take("inv_n", [P, GROUPS, SEQ])
    on_tables = Region(tables_at)
    gate = on_tables.take("gate", [P, T])
    gm = on_tables.take("gm", [P, T])
    rt = on_tables.take("rt", [P, T])
    assert on_tables.at <= dense.at
    mw_a = Region(dense.at).take("mw_a", [P, EARLY_UNITS, 2, GC])
    h_hi = dense.take("h_hi", [P, KD, T], F32R)
    h_lo_at = dense.at
    h_lo = dense.take("h_lo", [P, KD, T], F32R)
    free = dense.at
    mixer = Region(free)
    br = mixer.take("br", [P, BRANCHES, KB, T])
    fg = Region(free + KB * T * 4).take("fg", [P, 2, 2 * SEQ])
    pkv = mixer.take("pkv", [P, KKV, T])
    pq = mixer.take("pq", [P, KQ, T])
    kT = mixer.take("kT", [P, 2, T])
    early = Region(mixer.at)
    pf = mixer.take("pf", [P, GROUPS, T])
    pool_in = mixer.take("pool_in", [P, GROUPS, 2, PW])
    win = mixer.take("win", [P, 2, 2, PW])
    mixed = br
    v_b = early.take("v_b", [P, 2, HEADS * VD])
    ym_lo = Region(early.at).take("ym_lo", [P, KD, T], F32R)
    yacc = early.take("yacc", [P, KD, T])
    ym_hi = Region(free + KB * T * 4).take("ym_hi", [P, KD, T], F32R)
    nr = Region(free)
    var = nr.take("var", [P, T // P])
    std = nr.take("std", [P, T // P])
    rstd = nr.take("rstd", [P, T // P])
    diag = nr.take("diag", [P, T // P, P])
    nt = nr.take("nt", [P, 2, T])
    hf = nr.take("hf", [P, KD, SEQ])
    sq_between = Region(h_lo_at).take("sq_between", [P, 2, T])

    def squares(tag):
        return sq_ends if tag in ("n1_0", "fin") else sq_between

    mw_b = Region(nr.at).take("mw_b", [P, START_UNITS, 2, GC])
    m_rows = Region(end // 32 * 32 - 2 * T * 4 - EARLY_GROUPS * GC * 4).take("m_rows", [2, EARLY_GROUPS * GC])
    sq_ends = Region(end // 32 * 32 - 2 * T * 4).take("sq_ends", [P, 2, T])
    lr = Region(free)
    lsq = lr.take("lsq", [P, 2, T])
    lstd = lr.take("lstd", [P, 2, T])
    ff = Region(free)
    u_hi = ff.take("u_hi", [P, USLOTS, T], F32R)
    u_lo = ff.take("u_lo", [P, USLOTS, T], F32R)
    ft = ff.take("ft", [P, 2, T])
    fu = ff.take("fu", [P, 2, T])
    ex = Region(phase)
    estage = ex.take("estage", [P, STAGE, 4 * 512])
    ehi = ex.take("ehi", [P, SPLIT, 4 * 512], F32R)
    elo = ex.take("elo", [P, SPLIT, 4 * 512], F32R)
    et = ex.take("et", [P, 2, CW])
    eu = ex.take("eu", [P, 2, CW])
    ehT_hi = ex.take("ehT_hi", [P, 2, 2, SLOTS], F32R)
    ehT_lo = ex.take("ehT_lo", [P, 2, 2, SLOTS], F32R)
    htok = Region(max(ex.at, nr.at))
    htok_hi = htok.take("htok_hi", [P, 2, D], F32R)
    htok_lo = htok.take("htok_lo", [P, 2, D], F32R)
    rt_logit = htok.take("rt_logit", [P, 2, EXPERTS])
    rt_top = htok.take("rt_top", [P, 2, 8])
    rt_index = htok.take("rt_index", [P, 2, 8], U32)
    rt_indexf = htok.take("rt_indexf", [P, 2, 8])
    rt_one = htok.take("rt_one", [P, 2, 2, EXPERTS])
    rt_w = htok.take("rt_w", [P, 2, 5])
    comb = htok.take("comb", [P, 2, 2 * EXPERTS])
    mask = htok.take("mask", [P, 2, EXPERTS])
    posm = htok.take("posm", [P, 2, 2, 2 * EXPERTS])
    most = htok.take("most", [P, 1])
    most_i = htok.take("most_i", [P, 1], I32)
    sel = htok.take("sel", [P, 2, SLOTS], F32R)
    selT = htok.take("selT", [P, 2, SEQ], F32R)
    w_slot = htok.take("w_slot", [P, 2])
    xg_hi = htok.take("xg_hi", [P, 2, KD, SLOTS], F32R)
    xg_lo = htok.take("xg_lo", [P, 2, KD, SLOTS], F32R)
    o_fin = nc.alloc_sbuf_tensor_at("o_fin", [P, KD, SEQ], F32, offset=nr.at)

    ps = [nc.alloc_psum_tensor(f"ps{b}", [P, 512], F32) for b in range(8)]

    def hslot(k, n):
        slots = KD * SEQ // n
        return hf[:, :, :].rearrange("p k t -> p (k t)")[:, (k % slots) * n:(k % slots) * n + n]

    sems = {}

    def S(name):
        if name not in sems:
            sems[name] = nc.alloc_semaphore(name)
        return sems[name]

    def direct_used(n):
        kind, layer, *rest = direct[n]
        if kind == "pool":
            return S("pool_full"), earlier("pool_full", layer) + GROUPS
        if kind == "v":
            return S("v_full"), earlier("v_full", layer) + T // P
        if kind == "head":
            return S("qk_full"), earlier("qk_full", layer) + 4 * (rest[0] + 1)
        return S("o_full"), earlier("o_full", layer) + 2 * (rest[0] + 1)

    def c0(layer):
        return 0 if layer == 0 else SEQ

    def streams(layer):
        return (0, 1) if layer == 0 else (1,)

    def tile_c0(layer, j):
        return 0 if TILES[j] in ("kv0", "kv1", "kr") else c0(layer)

    def items(layer):
        tiles = range(4) if layer == 0 else (2, 3)
        return [(h, q, SEQ if q < 2 else T) for h in range(HEADS) for q in tiles]

    def v_rows(t):
        return (v_a, v_b)[t // 2][:, t % 2, :]

    def halves(layer, n):
        per = 2 * BESIDE // len(items(layer))
        return [divmod(i, 2) for i in range(per * n, per * (n + 1))]

    norms = [("n1_0", 0), ("n2_0", 0), ("n1_1", 0), ("n2_1", SEQ), ("fin", SEQ)]

    def earlier(name, layer):
        return FIRST_LAYER[name] if layer else 0

    def passed(name, p):
        return FIRST_PASS[name] * p

    def nth(tag):
        return [t for t, _ in norms].index(tag)

    EARLY_CONSTS = 8
    TABLES = 8
    FLUSH_TILES = [EARLY_MODS + GT * flushed(i) for i in range(4)]
    assert FLUSH_TILES[2] >= 5 * KD and FLUSH_TILES[3] == MODS

    ctx_block = nc.Block()
    block = ctx_block.__enter__()

    @block.sync
    def _(sp):
        small = [
            (ones, A["ones"]), (ident, A["ident"]), (b_mod, A["b_mod"]), (gains, A["gains"]),
            (b_gate, A["b_gate"]), (s_pool, A["s_pool"]), (g_q, A["g_q"]), (g_kv, A["g_kv"]),
        ]
        tables = [
            (rope, A["rope"]), (dft_c, A["dft_c"]), (dft_l, A["dft_l"]), (inv_n, A["inv_n"]),
            (router, A["router"]), (r_bias, A["r_bias"]), (iota, A["iota"]), (before, A["before"]),
        ]
        assert len(small) == EARLY_CONSTS and len(tables) == TABLES

        def load_small(t, a):
            full = tuple(slice(None) for _ in t.shape)
            return sp.dma_start(t[full], a)

        load_small(cond_in, A["cond"]).then_inc(S("cond_in"), 16)
        load_small(*small[0]).then_inc(S("consts"), 16)

        def load_early_mods(g):
            for u in range(GROUP_UNITS * g, GROUP_UNITS * (g + 1)):
                dst = mw_a[:, u, :, :] if g < EARLY_GROUPS else mw_b[:, u - EARLY_UNITS, :, :]
                sp.dma_start(dst, A["early"][u]).then_inc(S(f"early_in{g}"), 16)

        for t, a in small[1:]:
            load_small(t, a).then_inc(S("consts"), 16)
        sp.dma_start(xT[:, :, :], A["x"]).then_inc(S("x_in"), 16)
        load_early_mods(EARLY_GROUPS)
        for g in (0, EARLY_GROUPS + 1, 1):
            load_early_mods(g)

        def load_direct(n):
            if n >= DIRECT:
                s, v = direct_used(n - DIRECT)
                sp.wait_ge(s, v)
            sp.dma_start(dw[:, n % DIRECT, :, :], A["direct"][n]).then_inc(S(f"direct_in{n % DIRECT}"), 16)

        def load_split(u):
            if u >= DENSE_STAGE:
                sp.wait_ge(S("lo_done"), u - DENSE_STAGE + 1)
            sp.dma_start(stage[:, u % DENSE_STAGE, :], A["split"][u]).then_inc(S(f"split_in{u % DENSE_STAGE}"), 16)

        for at, (kind, n) in enumerate(load_order(walk, direct_at)):
            if at == 3:
                for t, a in tables:
                    load_small(t, a).then_inc(S("tables"), 16)
            if kind == "s" and n == walk.first[("in", 1, 0)] // SPLIT_BLOCKS:
                sp.wait_ge(S("y_hi"), KD)
                for t, a in tables[1:4]:
                    load_small(t, a).then_inc(S("tables_again"), 16)
            if kind == "d":
                load_direct(n)
            else:
                load_split(n)

        def experts(p):
            if p == 1:
                sp.wait_ge(S("x_add"), KD * (EXPERTS + 1))

            def load(v0, w, at):
                sp.wait_ge(S("e_lo_done"), passed("e_lo_done", p) + v0 + (w + 1))
                sp.dma_start(estage[:, w % STAGE, :], at).then_inc(S(f"e_in{w % STAGE}"), 16)

            with sp.Fori(0, EXPERTS // PAIR) as e2:
                v0 = e2 * (PAIR * UNITS)
                for w in range(PAIR * UNITS):
                    load(v0, w, A["moe"][bass.ds(v0 + w, 1)].rearrange("a p n -> p (a n)"))
            load(EXPERTS * UNITS, 0, A["moe"][EXPERTS * UNITS])
            for v in range(EXPERTS * UNITS + 1, PASS_UNITS):
                sp.wait_ge(S("e_lo_done"), passed("e_lo_done", p) + (v + 1))
                sp.sem_inc(S(f"e_in{v % STAGE}"), 16)

        experts(0)
        sp.wait_ge(S("most_ready"), 1)
        most_r = sp.value_load(most_i[0:1, 0:1], min_val=0, max_val=SEQ)
        with sp.If(most_r > SLOTS):
            experts(1)
        sp.wait_ge(S("out_ready"), KD)
        sp.dma_start(A["out"], o_fin[:, :, :]).then_inc(S("out_written"), 16)
        sp.wait_ge(S("out_written"), 16)

    @block.scalar
    def _(act):
        split_at = [0]

        def split_hi(upto):
            while split_at[0] < min(upto, walk.units):
                u = split_at[0]
                act.wait_ge(S(f"split_in{u % DENSE_STAGE}"), 16 * (u // DENSE_STAGE + 1))
                if u >= DENSE_SPLIT:
                    act.wait_ge(S("walked"), walk.unit(u - DENSE_SPLIT))
                act.activation(whi[:, u % DENSE_SPLIT, :, :], stage[:, u % DENSE_STAGE, :].rearrange("p (b c) -> p b c", c=P), ACT.Copy)\
                    .then_inc(S("hi_done"), 1)
                split_at[0] += 1

        def square(tag, first, k):
            if tag == "n1_0" or tag == "fin":
                if tag == "n1_0" and k == 0:
                    act.wait_ge(S("x_in"), 16)
            elif tag == "n1_1":
                act.wait_ge(S("x_ffn"), KD + k + 1)
            else:
                act.wait_ge(S("x_mix"), KD * int(tag[3]) + k + 1)
            if k >= 2:
                act.wait_ge(S("norm_ss"), KD * nth(tag) + k - 1)
            act.activation(squares(tag)[:, k % 2, 0:T - first], xT[:, k, first:T], ACT.Square).then_inc(S("norm_sq"), 1)

        def root(tag, first):
            n = T - first
            act.wait_ge(S("norm_var"), nth(tag) + 1)
            act.activation(std[:, 0:n // P], var[:, 0:n // P], ACT.Sqrt).then_inc(S("norm_std"), 1)

        def norm(tag, first):
            n = T - first
            if tag != "n1_0":
                root(tag, first)
            if tag == "fin":
                for k in range(KD):
                    act.wait_ge(S("norm_nt"), KD * nth("fin") + k + 1)
                    act.activation(o_fin[:, k, :], nt[:, k % 2, 0:n], ACT.Copy,
                                   scale=gains[:, 2 * DEPTH, k:k + 1]).then_inc(S("out_ready"), 1)
                return
            i = int(tag[1]) - 1
            layer = int(tag[3])
            parts = [(s, s * SEQ - first) for s in (0, 1) if s * SEQ >= first]
            slots = KD * SEQ // n

            def hi(k):
                act.wait_ge(S("norm_hf"), 2 * KD * nth(tag) + len(parts) * (k + 1))
                act.activation(h_hi[:, k, first:T], hslot(k, n), ACT.Copy).then_inc(S("norm_hhi"), 1)

            act.wait_ge(S("norm_coef"), 2 * nth(tag) + 2)
            for k in range(KD):
                act.wait_ge(S("norm_nt"), KD * nth(tag) + k + 1)
                if k >= slots:
                    act.wait_ge(S("norm_hlo"), KD * nth(tag) + k - slots + 1)
                for s, at in parts:
                    act.activation(hslot(k, n)[:, at:at + SEQ], nt[:, k % 2, at:at + SEQ], ACT.Identity,
                                   bias=mod[:, layer, s, 3 * i * KD + k:3 * i * KD + k + 1],
                                   scale=coef[:, 2 * layer + i, s, k:k + 1]).then_inc(S("norm_hf"), 1)
                if k >= 1:
                    hi(k - 1)
            hi(KD - 1)

        act.wait_ge(S("cond_in"), 16)
        act.activation(cond_t[:, :, :], cond_in[:, :, :], ACT.Tanh, scale=0.5).then_inc(S("cond_t"), 1)

        for layer in range(DEPTH):
            lc = c0(layer)
            if layer == 0:
                for k in range(KD):
                    square("n1_0", 0, k)
                root("n1_0", 0)
                for g in range(EARLY_GROUPS):
                    act.wait_ge(S("mod_rows"), g + 1)
                    act.activation(m_rows[:, g * GC:(g + 1) * GC], ps[2 + g][0:2, :], ACT.Copy).then_inc(S("m_rows"), 1)
                    if g == EARLY_GROUPS - 2:
                        split_hi(DENSE_SPLIT)
            norm(f"n1_{layer}", 0)
            for j, name in enumerate(TILES):
                split_hi(walk.units_up_to("in", layer, j) + 1)
                if name == "kr":
                    continue
                a = tile_c0(layer, j)
                act.wait_ge(S("walked"), walk.tile("in", layer, j))
                src = ps[j % 2][:, 0:T - a]
                if name.startswith("kv"):
                    dst = pkv[:, int(name[2]), a:T]
                elif name.startswith("q"):
                    dst = pq[:, int(name[1]), a:T]
                elif name.startswith("fft"):
                    dst = pf[:, int(name[3]), a:T]
                else:
                    if name == "pool0":
                        act.wait_ge(S("pads"), earlier("pads", layer) + 1)
                    dst = pool_in[:, int(name[4]), a // SEQ:2, PAD:PAD + SEQ]
                    src = src.rearrange("p (s t) -> p s t", t=SEQ)
                act.activation(dst, src, ACT.Copy).then_inc(S("in_evac"), 1)
                if name == "q2":
                    for i in range(KKV + KQ):
                        s0 = 0 if i < KKV else lc
                        if i == 0:
                            act.wait_ge(S("in_evac"), earlier("in_evac", layer) + 5)
                        if i >= 2:
                            act.wait_ge(S("lss"), earlier("lss", layer) + i - 1)
                        rows = pkv[:, i, :] if i < KKV else pq[:, i - KKV, s0:T]
                        act.activation(lsq[:, i % 2, s0:T], rows, ACT.Square).then_inc(S("lsq"), 1)
                if name == "fft1":
                    for i in range(2):
                        act.wait_ge(S("lvar"), earlier("lvar", layer) + i + 1)
                        s0 = (0, lc)[i]
                        act.activation(lstd[:, i, s0:T], lstd[:, i, s0:T], ACT.Sqrt).then_inc(S("lstd"), 1)
            for n in range(GROUPS * len(streams(layer))):
                act.wait_ge(S("fa_full"), earlier("fa_full", layer) + n + 1)
                if n >= 2:
                    act.wait_ge(S("fb_full"), earlier("fb_full", layer) + n - 1)
                act.activation(fg[:, n % 2, :], ps[2 + n % 2][:, :], ACT.Copy).then_inc(S("fg"), 1)
            for g in range(GROUPS):
                act.wait_ge(S("pool_full"), earlier("pool_full", layer) + g + 1)
                act.activation(br[:, 1, g, lc:T], ps[4 + g % 2][:, 0:T - lc], ACT.Copy,
                               scale=s_pool[:, layer, g:g + 1]).then_inc(S("br_b"), 1)
            def head_rows(h, which):
                act.wait_ge(S("qk_full"), earlier("qk_full", layer) + 2 * h + which + 1)
                if which == 0:
                    act.activation(qT[0:NOPE, h % 2, lc:T], ps[7][0:NOPE, 0:T - lc], ACT.Copy).then_inc(S("qk_rows"), 1)
                else:
                    act.activation(kT[0:NOPE, h % 2, :], ps[7][0:NOPE, :], ACT.Copy).then_inc(S("qk_rows"), 1)

            for t in range(T // P):
                act.wait_ge(S("v_full"), earlier("v_full", layer) + t + 1)
                if t == 0:
                    head_rows(0, 0)
                act.activation(v_rows(t), ps[2 + t % 2][:, :], ACT.Copy).then_inc(S("v_sb"), 1)

            todo = items(layer)
            per = len(todo) // HEADS

            def exps(n):
                _, _, keys = todo[n]
                act.wait_ge(S("neg_max"), earlier("neg_max", layer) + n + 1)
                if n >= 2:
                    act.wait_ge(S("t_full"), earlier("t_full", layer) + n - 1)
                act.activation(prob[:, n % 2, 0:keys], ps[2 + n % 2][:, 0:keys], ACT.Exp, scale=SCALE,
                               bias=stat[:, 1, n % 4:n % 4 + 1], accum_out=stat[:, 2, n % 4:n % 4 + 1])\
                    .then_inc(S("prob"), 1)

            def probs_t(n):
                _, _, keys = todo[n]
                act.wait_ge(S("t_full"), earlier("t_full", layer) + n + 1)
                if n >= 2:
                    act.wait_ge(S("pv"), earlier("pv", layer) + n - 1)
                act.activation(pT[:, n % 2, 0:keys], ps[4 + n % 2][:, 0:keys], ACT.Copy).then_inc(S("pT"), 1)

            def gate_tanh(m):
                split_hi(walk.units_up_to("gate", layer, m) + 1)
                j, b = MERGE[m]
                act.wait_ge(S("walked"), walk.tile("gate", layer, m))
                if m >= 1:
                    act.wait_ge(S("o_used"), earlier("o_used", layer) + m)
                else:
                    act.wait_ge(S("half_b"), 1)
                act.activation(gate[:, 0:T - lc], ps[0][:, 0:T - lc], ACT.Tanh, scale=0.5,
                               bias=half_b[:, layer, b * KD + j:b * KD + j + 1]).then_inc(S("gate"), 1)

            head_rows(0, 1)
            for n in range(len(todo) + 2):
                if n < len(todo):
                    exps(n)
                    if n % per < 2 and todo[n][0] + 1 < HEADS:
                        head_rows(todo[n][0] + 1, n % per)
                    for m, half in halves(layer, n):
                        if half == 1:
                            gate_tanh(m)
                if 1 <= n <= len(todo):
                    probs_t(n - 1)

            def merged_hi(j):
                act.wait_ge(S("y_add"), earlier("y_add", layer) + KD + j + 1)
                act.activation(ym_hi[:, j, lc:T], yacc[:, j, lc:T], ACT.Copy, scale=0.5).then_inc(S("y_hi"), 1)

            for m in range(BESIDE, NM):
                gate_tanh(m)
                if m > BESIDE:
                    merged_hi(m - BESIDE - 1)
            merged_hi(KD - 1)
            for j in range(KD):
                split_hi(walk.units_up_to("out", layer, j) + 1)
                square(f"n2_{layer}", lc, j)
            norm(f"n2_{layer}", lc)
            if layer == 0:
                def hidden_hi(i):
                    act.wait_ge(S("fu"), i + 1)
                    if i >= USLOTS:
                        act.wait_ge(S("walked"), walk.tile("down", 0, KD - 1))
                    act.activation(u_hi[:, i % USLOTS, :], fu[:, i % 2, :], ACT.Copy).then_inc(S("u_hi"), 1)

                for half, ks in enumerate(DOWN):
                    for i in ks:
                        split_hi(walk.units_up_to("upu", i) + 1)
                        act.wait_ge(S("walked"), walk.tile("upg", i))
                        if i == 0:
                            act.wait_ge(S("norm_hlo"), KD * nth("n2_0") + KD)
                        if i >= 2:
                            act.wait_ge(S("fu"), i - 1)
                        act.activation(ft[:, i % 2, :], ps[i % 2][:, :], ACT.Silu).then_inc(S("ft"), 1)
                        split_hi(walk.units_up_to("upu", i) + 2)
                        hidden_hi(i)
                    for j in range(KD):
                        split_hi(walk.units_up_to("down", half, j) + 1)
                        if half == 1:
                            square("n1_1", 0, j)

        for n in range(8):
            act.wait_ge(S("ht_full"), n + 1)
            dst = (htok_hi, htok_lo)[n // 4]
            act.activation(dst[:, n // 2 % 2, n % 2 * 512:n % 2 * 512 + 512], ps[n % 2][:, :], ACT.Copy).then_inc(S("htok"), 1)
        act.sem_inc(S("e_used"), SPLIT)
        act.wait_ge(S("rt_diff"), 2)
        act.activation(rt_w[:, :, 1], rt_w[:, :, 0], ACT.Exp).then_inc(S("rt_exp"), 1)

        def experts(p):
            used = S("e_used")
            if p == 1:
                act.wait_ge(S("x_add"), KD * (EXPERTS + 1))

            def hi(v0, w):
                act.wait_ge(S(f"e_in{w % STAGE}"), passed("e_in", p) + v0 * 16 + 16 * (w // STAGE + 1))
                act.wait_ge(used, passed("e_used", p) + v0 * STAGE + (w + 1))
                act.activation(ehi[:, w % SPLIT, :], estage[:, w % STAGE, :], ACT.Copy).then_inc(S("e_hi_done"), 1)

            def gathered_hi(e, x):
                for f in range(2):
                    act.wait_ge(S("ga_full"), passed("ga_full", p) + e * 4 + (4 * x + f + 1))
                    act.activation(xg_hi[:, x % 2, 4 * f:4 * f + 4, :], ps[5 + f][:, :].rearrange("p (k s) -> p k s", s=SLOTS), ACT.Copy)\
                        .then_inc(S("xg_hi"), 1)

            def turned_select(e, x):
                act.wait_ge(S("st_full"), passed("st_full", p) + e + (x + 1))
                act.activation(selT[:, x % 2, :], ps[7][:, 0:SEQ], ACT.Copy).then_inc(S("selT"), 1)
                act.activation(w_slot[:, x % 2:x % 2 + 1], ps[7][:, SEQ:SEQ + 1], ACT.Copy).then_inc(S("w_slot"), 1)

            def hidden_hi(c_, pc):
                act.wait_ge(S("tr_full"), passed("tr_full", p) + c_ + (pc + 2))
                act.activation(ehT_hi[:, pc % 2, :, :], ps[2][:, pc % 2 * 256:pc % 2 * 256 + 256].rearrange("p (b s) -> p b s", s=SLOTS), ACT.Copy)\
                    .then_inc(S("ehT_hi"), 1)

            def rows_hi(e, x, v0, w):
                act.wait_ge(used, passed("e_used", p) + v0 * STAGE + (SPLIT + w + 1))
                act.wait_ge(S("w_slot"), passed("w_slot", p) + e + (x + 1))
                act.wait_ge(S("sc_full"), passed("sc_full", p) + e * 4 + 4 * (x + 1))
                for f in range(2):
                    act.activation(y_rows[:, 2 * f:2 * f + 2, 0:SEQ], ps[3 + f][:, :].rearrange("p (a c) -> p a c", a=2), ACT.Copy,
                                   scale=w_slot[:, (x - 1) % 2:(x - 1) % 2 + 1]).then_inc(S("y_hi_e"), 1)

            hi(0, 0)
            gathered_hi(0, 0)
            for w in range(1, SPLIT):
                hi(0, w)
            turned_select(0, 0)
            with act.Fori(0, EXPERTS // PAIR) as e2:
                e = e2 * PAIR
                v0 = e2 * (PAIR * UNITS // STAGE)
                c_ = e2 * (PAIR * CHUNKS)
                for w in range(PAIR * UNITS):
                    x, c, kind = w // UNITS, w % UNITS // 3, STEPS[w % 3]
                    cc = x * CHUNKS + c
                    if kind == "ga":
                        if c == GATHER_AT[0] + 1:
                            gathered_hi(e, x + 1)
                        if c == GATHER_AT[1] + 1:
                            turned_select(e, x + 1)
                        hidden_hi(c_, cc - 1)
                    if kind == "gb":
                        act.wait_ge(used, passed("e_used", p) + v0 * STAGE + (SPLIT + w + 1))
                        act.activation(et[:, cc % 2, :], ps[cc % 2][:, 0:CW], ACT.Silu).then_inc(S("et"), 1)
                    if kind == "w" and c == 0:
                        rows_hi(e, x, v0, w)
                    hi(v0, w + SPLIT)
            hidden_hi(EXPERTS * CHUNKS, -1)
            rows_hi(EXPERTS, 0, EXPERTS * UNITS // STAGE, 0)
            act.sem_inc(S("e_hi_done"), PASS_UNITS - EXPERTS * UNITS - SPLIT)

        experts(0)
        act.wait_ge(S("most_ready"), 1)
        most_r = act.value_load(most_i[0:1, 0:1], min_val=0, max_val=SEQ)
        with act.If(most_r > SLOTS):
            experts(1)
        act.wait_ge(S("experts_done"), 1)
        for k in range(KD):
            square("fin", SEQ, k)
        norm("fin", SEQ)

    @block.vector
    def _(dve):
        split_at = [0]

        def split_lo(upto):
            while split_at[0] < min(upto, walk.units):
                u = split_at[0]
                dve.wait_ge(S("hi_done"), u + 1)
                dve.tensor_tensor(wlo[:, u % DENSE_SPLIT, :, :], stage[:, u % DENSE_STAGE, :].rearrange("p (b c) -> p b c", c=P),
                                  whi[:, u % DENSE_SPLIT, :, :], ALU.subtract).then_inc(S("lo_done"), 1)
                split_at[0] += 1

        def inverse_root(tag, first):
            n = T - first
            dve.wait_ge(S("norm_ss"), KD * nth(tag) + KD)
            dve.tensor_scalar(var[:, 0:n // P], ps[6][:, 0:n // P], 1.0 / D, EPS, ALU.mult, ALU.add).then_inc(S("norm_var"), 1)
            dve.wait_ge(S("norm_std"), 1 * nth(tag) + 1)
            dve.reciprocal(rstd[:, 0:n // P], std[:, 0:n // P]).then_inc(S("norm_rstd"), 1)
            dve.wait_ge(S("norm_rstd"), 1 * nth(tag) + 1)
            for t in range(n // P):
                ins = dve.tensor_scalar(diag[:, t, :], ident[:, :], rstd[:, t:t + 1], None, ALU.mult)
            ins.then_inc(S("norm_diag"), 1)

        def norm(tag, first):
            n = T - first
            if tag != "n1_0":
                inverse_root(tag, first)
            dve.wait_ge(S("norm_all"), nth(tag) + 1)

            def lo(k):
                dve.wait_ge(S("norm_hhi"), KD * nth(tag) + k + 1)
                dve.tensor_tensor(h_lo[:, k, first:T], hslot(k, n), h_hi[:, k, first:T], ALU.subtract)\
                    .then_inc(S("norm_hlo"), 1)

            parts = 2 if first == 0 else 1
            for k in range(KD):
                if k >= 2:
                    if tag == "fin":
                        dve.wait_ge(S("out_ready"), k - 1)
                    else:
                        dve.wait_ge(S("norm_hf"), 2 * KD * nth(tag) + parts * (k - 1))
                dve.tensor_tensor(nt[:, k % 2, 0:n], xT[:, k, first:T], ps[6][:, 0:n], ALU.mult).then_inc(S("norm_nt"), 1)
                if k >= 2 and tag != "fin":
                    lo(k - 2)
            if tag != "fin":
                lo(KD - 2)
                lo(KD - 1)

        def coefs(layer, i):
            for s in (0, 1):
                at = (3 * i + 1) * KD
                if (layer, i, s) == (1, 1, 0):
                    dve.sem_inc(S("norm_coef"), 1)
                    continue
                dve.scalar_tensor_tensor(coef[:, 2 * layer + i, s, :], mod[:, layer, s, at:at + KD], 1.0,
                                         gains[:, 2 * layer + i, :], ALU.add, ALU.mult)\
                    .then_inc(S("norm_coef"), 1)

        def mods(layer, first, last):
            rows = ps[7][:, 0:2 * MODS].rearrange("p (j s) -> p j s", s=2)
            for s in (0, 1):
                upto = min(last, 2 * KD) if layer == 1 and s == 0 else last
                dve.tensor_tensor(mod[:, layer, s, first:upto], rows[:, first:upto, s], b_mod[:, layer, first:upto],
                                  ALU.add).then_inc(S("mods"), 1)

        group_unit = [0]

        def mod_units(*key):
            for _ in range(mod_plan().get(key, 0)):
                u = group_unit[0]
                n, quarter = divmod(u, GROUP_UNITS)
                if u < START_UNITS:
                    dve.wait_ge(S(f"early_in{EARLY_GROUPS + n}"), 16 * GROUP_UNITS)
                    rows = mw_b[:, u, :, :]
                else:
                    at = u - START_UNITS
                    dve.wait_ge(S(f"group_in{at % 2}"), 16 * (at // 2 + 1))
                    rows = gw[:, at % 2, :, :]
                if quarter == 0 and n >= 2:
                    dve.wait_ge(S("mod_sum"), n - 1)
                for half in range(2):
                    k = 2 * quarter + half
                    if k > 0:
                        dve.wait_ge(S("acc_step"), KD * n + k)
                    for s in mod_streams(*MOD_GROUPS[n]):
                        dst, w, c = acc[:, n % 2, s, :], rows[:, half, :], cond_t[:, k, s:s + 1]
                        if k == 0:
                            ins = dve.tensor_scalar(dst, w, c, None, ALU.mult)
                        else:
                            ins = dve.scalar_tensor_tensor(dst, w, c, dst, ALU.mult, ALU.add)
                    ins.then_inc(S("acc_step"), 1)
                group_unit[0] += 1

        dve.wait_ge(S("cond_t"), 1)
        dve.scalar_tensor_tensor(cond[:, :, :], cond_t[:, :, :], 1.0, cond_in[:, :, :], ALU.add, ALU.mult)\
            .then_inc(S("cond"), 1)
        dve.wait_ge(S("cond"), 1)
        dve.tensor_scalar(cond_t[:, :, :], cond[:, :, :], 0.5, None, ALU.mult).then_inc(S("cond"), 1)
        dve.wait_ge(S("cond"), 2)
        mod_units("start", 0)
        inverse_root("n1_0", 0)
        mod_units("start", 1)
        dve.wait_ge(S("consts"), 16 * EARLY_CONSTS)
        dve.tensor_scalar(half_b[:, :, :], b_gate[:, :, :], 0.5, None, ALU.mult).then_inc(S("half_b"), 1)
        split_lo(1)
        dve.wait_ge(S("mod_turned"), EARLY_GROUPS)
        dve.wait_ge(S("mod_sum"), flushed(0))
        mods(0, 0, FLUSH_TILES[0])
        dve.wait_ge(S("mods"), 2)
        coefs(0, 0)

        for layer in range(DEPTH):
            lc = c0(layer)
            norm(f"n1_{layer}", 0)
            for j, name in enumerate(TILES):
                split_lo(walk.units_up_to("in", layer, j) + 1)
                if name == "kr":
                    dve.wait_ge(S("walked"), walk.tile("in", layer, j))
                    dve.wait_ge(S("tables"), 16 * TABLES)
                    dve.tensor_tensor(kT[64:96, 0, :], ps[j % 2][64:96, :], rope[64:96, :], ALU.mult)\
                        .then_inc(S("kr"), 1)
                    dve.tensor_tensor(kT[64:96, 1, :], ps[j % 2][96:128, :], rope[96:128, :], ALU.mult)\
                        .then_inc(S("kr"), 1)
                    dve.wait_ge(S("kr"), earlier("kr", layer) + 2)
                    dve.tensor_tensor(kT[64:96, 0, :], kT[64:96, 0, :], kT[64:96, 1, :], ALU.add)\
                        .then_inc(S("kr"), 1)
                    dve.wait_ge(S("kr"), earlier("kr", layer) + 3)
                    dve.tensor_copy(kT[64:96, 1, :], kT[64:96, 0, :]).then_inc(S("kr"), 1)
                if name == "fft1":
                    for i, width in enumerate((KV_LORA, Q_LORA)):
                        s0 = (0, lc)[i]
                        dve.wait_ge(S("lss"), earlier("lss", layer) + (KKV, KKV + KQ)[i])
                        dve.tensor_scalar(lstd[:, i, s0:T], ps[(6, 2)[i]][:, s0:T], 1.0 / width, EPS, ALU.mult, ALU.add)\
                            .then_inc(S("lvar"), 1)
                if name == "fft2":
                    for i in range(2):
                        s0 = (0, lc)[i]
                        dve.wait_ge(S("lstd"), earlier("lstd", layer) + i + 1)
                        dve.reciprocal(lstd[:, i, s0:T], lstd[:, i, s0:T]).then_inc(S("lrstd"), 1)
                    dve.wait_ge(S("in_evac"), earlier("in_evac", layer) + 5)
                    for i in range(KKV + KQ):
                        s0 = 0 if i < KKV else lc
                        rows = pkv[:, i, :] if i < KKV else pq[:, i - KKV, s0:T]
                        gain = g_kv[:, layer, i:i + 1] if i < KKV else g_q[:, layer, i - KKV:i - KKV + 1]
                        if i in (0, KKV):
                            dve.wait_ge(S("lrstd"), earlier("lrstd", layer) + (1 if i == 0 else 2))
                        dve.scalar_tensor_tensor(rows, rows, gain, lstd[:, 0 if i < KKV else 1, s0:T], ALU.mult, ALU.mult)\
                            .then_inc(S("lnorm"), 1)
                mod_units("in", layer, j)
            if layer == 0:
                dve.wait_ge(S("mod_sum"), flushed(1))
                mods(0, FLUSH_TILES[0], FLUSH_TILES[1])
            n = 0
            for s in streams(layer):
                for g in range(GROUPS):
                    dve.wait_ge(S("fb_full"), earlier("fb_full", layer) + n + 1)
                    if n == 0:
                        dve.wait_ge(S("lnorm"), earlier("lnorm", layer) + KKV + KQ)
                    dve.tensor_copy(br[:, 2, g, s * SEQ:(s + 1) * SEQ], ps[4 + n % 2][:, 0:SEQ]).then_inc(S("br_c"), 1)
                    n += 1
            todo = items(layer)
            per = len(todo) // HEADS

            def head_rope(h):
                dve.wait_ge(S("qk_full"), earlier("qk_full", layer) + 2 * h + 1)
                dve.tensor_tensor(qT[64:96, h % 2, lc:T], ps[7][64:96, 0:T - lc], rope[64:96, lc:T], ALU.mult)\
                    .then_inc(S("q_rope"), 1)
                if h >= 1:
                    dve.wait_ge(S("q_rope"), earlier("q_rope", layer) + 3 * h)
                dve.tensor_tensor(rt[64:96, lc:T], ps[7][96:128, 0:T - lc], rope[96:128, lc:T], ALU.mult)\
                    .then_inc(S("q_rope"), 1)
                dve.wait_ge(S("q_rope"), earlier("q_rope", layer) + 3 * h + 2)
                dve.tensor_tensor(qT[64:96, h % 2, lc:T], qT[64:96, h % 2, lc:T], rt[64:96, lc:T], ALU.add)\
                    .then_inc(S("q_rope"), 1)

            def row_max(n):
                _, _, keys = todo[n]
                dve.wait_ge(S("s_full"), earlier("s_full", layer) + n + 1)
                dve.tensor_reduce(stat[:, 0, n % 4:n % 4 + 1], ps[2 + n % 2][:, 0:keys], AX, ALU.max).then_inc(S("max"), 1)
                dve.wait_ge(S("max"), earlier("max", layer) + n + 1)
                dve.tensor_scalar(stat[:, 1, n % 4:n % 4 + 1], stat[:, 0, n % 4:n % 4 + 1], -SCALE, None, ALU.mult)\
                    .then_inc(S("neg_max"), 1)

            def normalise(n):
                _, _, keys = todo[n]
                dve.wait_ge(S("prob"), earlier("prob", layer) + n + 1)
                dve.reciprocal(stat[:, 3, n % 4:n % 4 + 1], stat[:, 2, n % 4:n % 4 + 1]).then_inc(S("rden"), 1)
                dve.wait_ge(S("rden"), earlier("rden", layer) + n + 1)
                dve.tensor_scalar(prob[:, n % 2, 0:keys], prob[:, n % 2, 0:keys], stat[:, 3, n % 4:n % 4 + 1], None, ALU.mult)\
                    .then_inc(S("pn"), 1)

            def head_out(h):
                dve.wait_ge(S("pv"), earlier("pv", layer) + per * (h + 1))
                if h == 0:
                    dve.wait_ge(S("pool_full"), earlier("pool_full", layer) + GROUPS)
                at = h % 2 * 64
                dve.tensor_copy(br[at:at + 64, 0, h // 2, lc:T], ps[6][0:64, lc:T]).then_inc(S("br_a"), 1)

            def merge(m):
                j, b = MERGE[m]
                dve.wait_ge(S("o_full"), earlier("o_full", layer) + m + 1)
                dve.wait_ge(S("gate"), earlier("gate", layer) + m + 1)
                o = ps[1][:, 0:T - lc]
                if b == 1:
                    dve.scalar_tensor_tensor(yacc[:, j, lc:T], gate[:, 0:T - lc], 1.0, o, ALU.add, ALU.mult)\
                        .then_inc(S("o_used"), 1)
                else:
                    added = earlier("y_add", layer) + (j if b == 2 else KD + j)
                    if added:
                        dve.wait_ge(S("y_add"), added)
                    dve.scalar_tensor_tensor(gm[:, 0:T - lc], gate[:, 0:T - lc], 1.0, o, ALU.add, ALU.mult)\
                        .then_inc(S("o_used"), 1)
                    dve.wait_ge(S("o_used"), earlier("o_used", layer) + m + 1)
                    dve.tensor_tensor(yacc[:, j, lc:T], yacc[:, j, lc:T], gm[:, 0:T - lc], ALU.add)\
                        .then_inc(S("y_add"), 1)

            def after_merge(m):
                split_lo(walk.units_up_to("gate", layer, m) + 1)
                mod_units("gate", layer, m)

            head_rope(0)
            for n in range(len(todo) + 3):
                if n >= 3 and (n - 3) % per == per - 1:
                    head_out((n - 3) // per)
                if n < len(todo):
                    row_max(n)
                    if n % per == 0 and todo[n][0] + 1 < HEADS:
                        head_rope(todo[n][0] + 1)
                if 1 <= n <= len(todo):
                    for m, half in halves(layer, n - 1):
                        if half == 1:
                            merge(m)
                if n < len(todo):
                    normalise(n)
                if 1 <= n <= len(todo):
                    for m, half in halves(layer, n - 1):
                        if half == 1:
                            after_merge(m)

            def merged_lo(j):
                dve.wait_ge(S("y_hi"), earlier("y_hi", layer) + j + 1)
                dve.scalar_tensor_tensor(ym_lo[:, j, lc:T], yacc[:, j, lc:T], 0.5, ym_hi[:, j, lc:T], ALU.mult, ALU.subtract)\
                    .then_inc(S("y_lo"), 1)

            for m in range(BESIDE, NM):
                merge(m)
                after_merge(m)
                if m > BESIDE:
                    merged_lo(m - BESIDE - 1)
            merged_lo(KD - 1)
            for j in range(KD):
                split_lo(walk.units_up_to("out", layer, j) + 1)
                dve.wait_ge(S("walked"), walk.tile("out", layer, j))
                for s in streams(layer):
                    at = s * SEQ
                    ins = dve.scalar_tensor_tensor(xT[:, j, at:at + SEQ], ps[4 + j % 2][:, at - lc:at - lc + SEQ],
                                                   mod[:, layer, s, 2 * KD + j:2 * KD + j + 1],
                                                   xT[:, j, at:at + SEQ], ALU.mult, ALU.add)
                ins.then_inc(S("x_mix"), 1)
                mod_units("out", layer, j)
                if ("out", layer, j) == MOD_FLUSH[2]:
                    dve.wait_ge(S("mod_sum"), flushed(2))
                    mods(0, FLUSH_TILES[1], FLUSH_TILES[2])
                    dve.wait_ge(S("mods"), 6)
                    coefs(0, 1)
                if layer == DEPTH - 1 and j == KD - 1:
                    dve.wait_ge(S("lo_done"), walk.units)
                    dve.sem_inc(S("e_lo_done"), STAGE)
            norm(f"n2_{layer}", lc)
            if layer == 0:
                for half, ks in enumerate(DOWN):
                    for i in ks:
                        split_lo(walk.units_up_to("upu", i) + 1)
                        dve.wait_ge(S("ft"), i + 1)
                        dve.wait_ge(S("walked"), walk.tile("upu", i))
                        if i >= 2:
                            dve.wait_ge(S("u_hi"), i - 1)
                        dve.tensor_tensor(fu[:, i % 2, :], ft[:, i % 2, :], ps[2 + i % 2][:, :], ALU.mult).then_inc(S("fu"), 1)
                        split_lo(walk.units_up_to("upu", i) + 2)
                        dve.wait_ge(S("u_hi"), i + 1)
                        dve.tensor_tensor(u_lo[:, i % USLOTS, :], fu[:, i % 2, :], u_hi[:, i % USLOTS, :], ALU.subtract)\
                            .then_inc(S("u_lo"), 1)
                        mod_units("upu", i)
                        if ("upu", i) == MOD_FLUSH[3]:
                            dve.wait_ge(S("mod_sum"), flushed(3))
                            mods(0, FLUSH_TILES[2], FLUSH_TILES[3])
                    for j in range(KD):
                        split_lo(walk.units_up_to("down", half, j) + 1)
                        dve.wait_ge(S("walked"), walk.tile("down", half, j))
                        if half == 1:
                            dve.wait_ge(S("x_ffn"), j + 1)
                        for s in (0, 1):
                            at = s * SEQ
                            ins = dve.scalar_tensor_tensor(xT[:, j, at:at + SEQ], ps[4 + j % 2][:, at:at + SEQ],
                                                           mod[:, 0, s, 5 * KD + j:5 * KD + j + 1],
                                                           xT[:, j, at:at + SEQ], ALU.mult, ALU.add)
                        ins.then_inc(S("x_ffn"), 1)
                        mod_units("down", half, j)
                dve.wait_ge(S("mod_sum"), flushed(4))
                mods(1, 0, MODS)
                dve.wait_ge(S("mods"), earlier("mods", 1) + 2)
                coefs(1, 0)
                coefs(1, 1)

        chain = [0]

        def step(ins):
            chain[0] += 1
            ins.then_inc(S("rt_step"), 1)
            dve.wait_ge(S("rt_step"), chain[0])

        dve.wait_ge(S("lg_full"), 1)
        for t in range(2):
            step(dve.tensor_tensor(rt_logit[:, t, :], ps[(7, 3)[t]][:, 0:EXPERTS], r_bias[:, :], ALU.add))
            step(dve.max(rt_top[:, t, :], rt_logit[:, t, :]))
            step(dve.max_index(rt_index[:, t, :], rt_top[:, t, :], rt_logit[:, t, :]))
            step(dve.tensor_copy(rt_indexf[:, t, :], rt_index[:, t, :]))
            for r in range(2):
                step(dve.tensor_scalar(rt_one[:, t, r, :], iota[:, 0:EXPERTS], rt_indexf[:, t, r:r + 1], None, ALU.is_equal))
            dve.tensor_tensor(rt_w[:, t, 0:1], rt_top[:, t, 1:2], rt_top[:, t, 0:1], ALU.subtract).then_inc(S("rt_diff"), 1)
            dve.tensor_tensor(mask[:, t, :], rt_one[:, t, 0, :], rt_one[:, t, 1, :], ALU.add).then_inc(S("mask"), 1)
        step(dve.memset(posm[:, :, :, :], -1.0))
        dve.wait_ge(S("cnt_full"), 1)
        place = posm[:, 0, :, 0:EXPERTS]
        step(dve.scalar_tensor_tensor(place, ps[7][:, 32:48].rearrange("p (t e) -> p t e", t=2), 1.0, mask[:, :, :], ALU.add, ALU.mult))
        step(dve.tensor_scalar(place, place, 1.0, None, ALU.subtract))
        step(dve.tensor_scalar(posm[:, 1, :, 0:EXPERTS], place, float(SLOTS), None, ALU.subtract))
        step(dve.tensor_reduce(most[:, :], ps[7][:, 48:56], AX, ALU.max))
        dve.tensor_copy(most_i[:, :], most[:, :]).then_inc(S("most_ready"), 1)

        def combine():
            dve.wait_ge(S("rt_exp"), 1)
            step(dve.memset(comb[:, :, :], 0.0))
            for t in range(2):
                step(dve.tensor_scalar(rt_w[:, t, 2:3], rt_w[:, t, 1:2], 1.0, None, ALU.add))
                step(dve.reciprocal(rt_w[:, t, 3:4], rt_w[:, t, 2:3]))
                step(dve.tensor_tensor(rt_w[:, t, 4:5], rt_w[:, t, 1:2], rt_w[:, t, 3:4], ALU.mult))
                step(dve.tensor_scalar(comb[:, t, 0:EXPERTS], rt_one[:, t, 0, :], rt_w[:, t, 3:4], None, ALU.mult))
                step(dve.scalar_tensor_tensor(comb[:, t, 0:EXPERTS], rt_one[:, t, 1, :], rt_w[:, t, 4:5], comb[:, t, 0:EXPERTS], ALU.mult, ALU.add))

        def experts(p):
            if p == 1:
                dve.wait_ge(S("x_add"), KD * (EXPERTS + 1))

            def lo(v0, w):
                dve.wait_ge(S("e_hi_done"), passed("e_hi_done", p) + v0 * STAGE + (w + 1))
                dve.tensor_tensor(elo[:, w % SPLIT, :], estage[:, w % STAGE, :], ehi[:, w % SPLIT, :], ALU.subtract)\
                    .then_inc(S("e_lo_done"), 1)

            def select(e, x, first=False):
                if not first:
                    dve.wait_ge(S("st_full"), passed("st_full", p) + e + x)
                for t in range(2):
                    at = posm[:, p, t, 0:1] if first else posm[:, p, t, bass.ds(e + x, 1)]
                    dve.tensor_scalar(sel[:, t, :], iota[:, :], at, None, ALU.is_equal).then_inc(S("sel"), 1)

            def gathered_lo(e, x):
                for f in range(2):
                    dve.wait_ge(S("ga_full"), passed("ga_full", p) + e * 4 + (4 * x + f + 3))
                    dve.tensor_copy(xg_lo[:, x % 2, 4 * f:4 * f + 4, :], ps[5 + f][:, :].rearrange("p (k s) -> p k s", s=SLOTS))\
                        .then_inc(S("xg_lo"), 1)

            def hidden_lo(c_, pc):
                dve.wait_ge(S("ehT_hi"), passed("ehT_hi", p) + c_ + (pc + 2))
                dve.tensor_tensor(ehT_lo[:, pc % 2, :, :], ps[2][:, pc % 2 * 256:pc % 2 * 256 + 256].rearrange("p (b s) -> p b s", s=SLOTS),
                                  ehT_hi[:, pc % 2, :, :], ALU.subtract).then_inc(S("ehT_lo"), 1)

            def rows_lo(e, x):
                slot = w_slot[:, (x - 1) % 2:(x - 1) % 2 + 1]
                dve.wait_ge(S("w_slot"), passed("w_slot", p) + e + (x + 1))
                for f in range(2):
                    dve.wait_ge(S("y_hi_e"), passed("y_hi_e", p) + e * 2 + (2 * x + f + 1))
                    dve.scalar_tensor_tensor(y_rows[:, 4 + 2 * f:6 + 2 * f, 0:SEQ], ps[3 + f][:, :].rearrange("p (a c) -> p a c", a=2), slot,
                                             y_rows[:, 2 * f:2 * f + 2, 0:SEQ], ALU.mult, ALU.subtract).then_inc(S("y_lo_e"), 1)

            def add_rows(e, x, k4):
                dve.wait_ge(S("sc_full"), passed("sc_full", p) + e * 4 + (4 * x + k4 + 5))
                for i in range(2):
                    kk = 2 * k4 + i
                    dve.scalar_tensor_tensor(xT[:, kk, SEQ:T], ps[5 + k4 % 2][:, i * SEQ:(i + 1) * SEQ],
                                             mod[:, 1, 1, 5 * KD + kk:5 * KD + kk + 1], xT[:, kk, SEQ:T],
                                             ALU.mult, ALU.add).then_inc(S("x_add"), 1)

            select(0, 0, first=True)
            if p == 0:
                combine()
            dve.memset(eu[:, :, :], 0.0).then_inc(S("eu"), 2)
            dve.memset(w_slot[:, 1:2], 0.0).then_inc(S("w_slot"), 1)
            for t in range(2):
                ins = dve.tensor_scalar(selT[:, 1, t * P:(t + 1) * P], iota[:, :], 0.0, None, ALU.mult)
            ins.then_inc(S("selT"), 1)
            lo(0, 0)
            gathered_lo(0, 0)
            for w in range(1, SPLIT):
                lo(0, w)
            with dve.Fori(0, EXPERTS // PAIR) as e2:
                e = e2 * PAIR
                v0 = e2 * (PAIR * UNITS // STAGE)
                c_ = e2 * (PAIR * CHUNKS)
                for w in range(PAIR * UNITS):
                    x, c, kind = w // UNITS, w % UNITS // 3, STEPS[w % 3]
                    cc = x * CHUNKS + c
                    if kind == "ga":
                        if c in (SCATTER_AT[0] + 1, SCATTER_AT[1] + 1):
                            for k4 in range(2):
                                add_rows(e, x, 2 * (c - SCATTER_AT[0] - 1) + k4)
                        if c == GATHER_AT[1] + 1:
                            gathered_lo(e, x + 1)
                        hidden_lo(c_, cc - 1)
                    if kind == "gb":
                        dve.wait_ge(S("et"), passed("et", p) + c_ + (cc + 1))
                        dve.tensor_tensor(eu[:, cc % 2, :], et[:, cc % 2, :], ps[cc % 2][:, CW:2 * CW], ALU.mult).then_inc(S("eu"), 1)
                    if kind == "w" and c == 0:
                        rows_lo(e, x)
                    if kind == "w" and c == SCATTER_AT[1] + 1:
                        select(e, x + 1)
                    lo(v0, w + SPLIT)
            hidden_lo(EXPERTS * CHUNKS, -1)
            rows_lo(EXPERTS, 0)
            for k4 in range(KD // 2):
                add_rows(EXPERTS, 0, k4)
            dve.sem_inc(S("e_lo_done"), PASS_UNITS - EXPERTS * UNITS - SPLIT)

        experts(0)
        dve.wait_ge(S("x_add"), KD * (EXPERTS + 1))
        dve.wait_ge(S("most_ready"), 1)
        most_r = dve.value_load(most_i[0:1, 0:1], min_val=0, max_val=SEQ)
        with dve.If(most_r > SLOTS):
            experts(1)
            dve.wait_ge(S("x_add"), 2 * KD * (EXPERTS + 1))
        dve.sem_inc(S("experts_done"), 1)
        norm("fin", SEQ)

    @block.gpsimd
    def _(pool):

        def load_groups(first, last):
            for u in range(first, last):
                if u >= 2:
                    pool.wait_ge(S("acc_step"), 2 * (START_UNITS + u - 1))
                pool.dma_start(gw[:, u % 2, :, :], A["groups"][u]).then_inc(S(f"group_in{u % 2}"), 16)

        before_windows = GROUP_UNITS * flushed(1) - START_UNITS
        for layer in range(DEPTH):
            s0 = streams(layer)[0]
            lc = c0(layer)
            if layer == 0:
                pool.wait_ge(S("early_in1"), 16 * GROUP_UNITS)
                load_groups(0, before_windows)
            pool.wait_ge(S("norm_hlo"), KD * nth(f"n1_{layer}") + KD)
            pool.memset(pool_in[:, :, :, :], 0.0).then_inc(S("pads"), 1)
            n = [0]

            def step(ins):
                n[0] += 1
                ins.then_inc(S("win"), 1)
                pool.wait_ge(S("win"), earlier("win", layer) + n[0])

            pool.wait_ge(S("tables"), 16 * TABLES)
            if layer == 1:
                pool.wait_ge(S("tables_again"), 16 * 3)
            for g in range(GROUPS):
                pool.wait_ge(S("in_evac"), earlier("in_evac", layer) + 5 + GROUPS + g + 1)
                rows = pool_in[:, g, s0:2, :]
                src = rows
                for a in range(g + 1):
                    reach = 1 << a
                    start = (2 << a) - 1
                    dst = win[:, a % 2, s0:2, :]
                    step(pool.tensor_tensor(dst[:, :, start:PW], src[:, :, start:PW], src[:, :, start - reach:PW - reach], ALU.add))
                    src = dst
                at = PAD + (1 << g) - 1
                dst = win[:, (g + 1) % 2, s0:2, 0:SEQ]
                for s in range(s0, 2):
                    step(pool.tensor_tensor(win[:, (g + 1) % 2, s, 0:SEQ], win[:, g % 2, s, at:at + SEQ], inv_n[:, g, :], ALU.mult))
                if g == 0:
                    pool.wait_ge(S("lnorm"), earlier("lnorm", layer) + KKV + KQ)
                pool.tensor_tensor(mixed[:, 0, g, lc:T].rearrange("p (s t) -> p s t", t=SEQ), dst, rows[:, :, PAD:PAD + SEQ], ALU.subtract)\
                    .then_inc(S("mixed"), 1)
                pool.wait_ge(S("mixed"), earlier("mixed", layer) + g + 1)
            if layer == 0:
                pool.wait_ge(S("br_a"), HEADS)
                load_groups(before_windows, GROUP_UNITS * len(MOD_GROUPS) - START_UNITS)

    @block.tensor
    def _(pe):
        at = [0]

        def block_passes(out, key, k, rhs_hi, rhs_lo, first, last):
            b = at[0]
            assert walk.block(key, k) == b
            u, i = divmod(b, SPLIT_BLOCKS)
            if i == 0:
                pe.wait_ge(S("lo_done"), u + 1)
            hi, lo = whi[:, u % DENSE_SPLIT, i, :], wlo[:, u % DENSE_SPLIT, i, :]
            pe.matmul(out, hi, rhs_hi, start=first, stop=False)
            pe.matmul(out, hi, rhs_lo, start=False, stop=False)
            ins = pe.matmul(out, lo, rhs_hi, start=False, stop=last)
            if b in walk.number:
                ins.then_inc(S("walked"), 1)
            at[0] += 1
            return ins

        def direct_unit(key):
            n = direct_at[key]
            pe.wait_ge(S(f"direct_in{n % DIRECT}"), 16 * (n // DIRECT + 1))
            return n % DIRECT

        def early_rows(g):
            pe.wait_ge(S(f"early_in{g}"), 16 * GROUP_UNITS)
            for k in range(KD):
                u = GROUP_UNITS * g + k // 2
                ins = pe.matmul(ps[2 + g][0:2, :], cond_t[:, k, :], mw_a[:, u, k % 2, :], start=(k == 0), stop=(k == KD - 1))
            ins.then_inc(S("mod_rows"), 1)

        def early_turn(g):
            pe.wait_ge(S("m_rows"), g + 1)
            for j in range(GT * g, GT * (g + 1)):
                ins = pe.matmul(ps[7][:, 2 * j:2 * j + 2], m_rows[:, j * P:(j + 1) * P], ident[0:2, 0:2], start=True, stop=True)
            ins.then_inc(S("mod_turned"), 1)

        def mod_sums(*key):
            for n in sum_plan().get(key, []):
                layer, g = MOD_GROUPS[n]
                pe.wait_ge(S("acc_step"), KD * (n + 1))
                taken = sum(n >= flushed(i) for i in range(len(MOD_FLUSH)))
                if taken:
                    pe.wait_ge(S("mods"), 2 * taken)
                for t in range(GT):
                    for s in mod_streams(layer, g):
                        at = 2 * (GT * g + t) + s
                        ins = pe.matmul(ps[7][:, at:at + 1], acc[:, n % 2, s, t * P:(t + 1) * P], ones[:, 0:1], start=True, stop=True)
                ins.then_inc(S("mod_sum"), 1)

        def sum_squares(tag, first, k):
            pe.wait_ge(S("norm_sq"), KD * nth(tag) + k + 1)
            tiles = (T - first) // P
            for t in range(tiles):
                ins = pe.matmul(ps[6][:, t:t + 1], squares(tag)[:, k % 2, t * P:(t + 1) * P], ones[:, 0:1],
                                start=(k == 0 and t == 0), stop=(k == KD - 1 and t == tiles - 1))
            ins.then_inc(S("norm_ss"), 1)

        def everywhere(tag, first):
            pe.wait_ge(S("norm_diag"), nth(tag) + 1)
            pe.matmul(ps[6][:, 0:T - first], ones[:, :], diag[:, 0:(T - first) // P, :].rearrange("p t c -> p (t c)"), start=True, stop=True)\
                .then_inc(S("norm_all"), 1)

        pe.wait_ge(S("cond"), 2)
        pe.wait_ge(S("consts"), 16 * EARLY_CONSTS)
        for k in range(KD):
            sum_squares("n1_0", 0, k)
        early_rows(0)
        mod_sums("start", 0)
        early_rows(1)
        early_turn(0)
        everywhere("n1_0", 0)
        mod_sums("start", 1)
        early_turn(1)
        for layer in range(DEPTH):
            lc = c0(layer)
            for j, name in enumerate(TILES):
                a = tile_c0(layer, j)
                if j >= 2:
                    if TILES[j - 2] == "kr":
                        pe.wait_ge(S("kr"), earlier("kr", layer) + 2)
                    else:
                        pe.wait_ge(S("in_evac"), earlier("in_evac", layer) + j - 1 - (1 if j - 2 > 2 else 0))
                for k in range(KD):
                    if j == 0:
                        pe.wait_ge(S("norm_hlo"), KD * nth(f"n1_{layer}") + k + 1)
                    for jj in {0: (0, 1), 1: ()}.get(j, (j,)):
                        block_passes(ps[jj % 2][:, 0:T - a], ("in", layer, jj), k, h_hi[:, k, a:T], h_lo[:, k, a:T], k == 0, k == KD - 1)
                if name == "fft0":
                    for i in range(KKV + KQ):
                        s0 = 0 if i < KKV else lc
                        first, last = i in (0, KKV), i in (KKV - 1, KKV + KQ - 1)
                        pe.wait_ge(S("lsq"), earlier("lsq", layer) + i + 1)
                        pe.matmul(ps[6 if i < KKV else 2][:, s0:T], ones[:, :], lsq[:, i % 2, s0:T], start=first, stop=last)\
                            .then_inc(S("lss"), 1)
                mod_sums("in", layer, j)
            pe.wait_ge(S("tables"), 16 * TABLES)
            if layer == 1:
                pe.wait_ge(S("tables_again"), 16 * 3)

            todo = [(s, g) for s in streams(layer) for g in range(GROUPS)]

            def channels(n):
                s, g = todo[n]
                if n == 0:
                    pe.wait_ge(S("in_evac"), earlier("in_evac", layer) + 5 + GROUPS)
                    pe.wait_ge(S("lvar"), earlier("lvar", layer) + 2)
                if n >= 2:
                    pe.wait_ge(S("fg"), earlier("fg", layer) + n - 1)
                for t in range(2):
                    c = s * SEQ + t * P
                    ins = pe.matmul(ps[2 + n % 2][:, t * 256:t * 256 + 256], pf[:, g, c:c + P], dft_c[:, :], start=True, stop=True)
                ins.then_inc(S("fa_full"), 1)

            def tokens(n):
                pe.wait_ge(S("fg"), earlier("fg", layer) + n + 1)
                if n >= 2:
                    pe.wait_ge(S("br_c"), earlier("br_c", layer) + n - 1)
                for t in range(2):
                    for part in range(2):
                        c = t * 256 + part * P
                        ins = pe.matmul(ps[4 + n % 2][:, 0:SEQ], fg[:, n % 2, c:c + P], dft_l[:, t, part, :],
                                        start=(t == 0 and part == 0), stop=(t == 1 and part == 1))
                ins.then_inc(S("fb_full"), 1)

            channels(0)
            for n in range(len(todo)):
                if n + 1 < len(todo):
                    channels(n + 1)
                tokens(n)
            slot = direct_unit(("pool", layer))
            for g in range(GROUPS):
                pe.wait_ge(S("mixed"), earlier("mixed", layer) + g + 1)
                if g < 2:
                    pe.wait_ge(S("br_c"), earlier("br_c", layer) + len(todo))
                else:
                    pe.wait_ge(S("br_b"), earlier("br_b", layer) + g - 1)
                pe.matmul(ps[4 + g % 2][:, 0:T - lc], dw[:, slot, g, :], mixed[:, 0, g, lc:T], start=True, stop=True)\
                    .then_inc(S("pool_full"), 1)
            def queries(h):
                slot = direct_unit(("head", layer, h // 2))
                if h == 0:
                    pe.wait_ge(S("mods"), 4)
                else:
                    pe.wait_ge(S("qk_rows"), earlier("qk_rows", layer) + 2 * h)
                for i in range(KQ):
                    ins = pe.matmul(ps[7][:, 0:T - lc], dw[:, slot, 4 * (h % 2) + i, :], pq[:, i, lc:T], start=(i == 0), stop=(i == KQ - 1))
                ins.then_inc(S("qk_full"), 1)

            def keys_of(h):
                slot = direct_unit(("head", layer, h // 2))
                pe.wait_ge(S("qk_rows"), earlier("qk_rows", layer) + 2 * h + 1)
                pe.wait_ge(S("q_rope"), earlier("q_rope", layer) + 3 * h + 3)
                for i in range(KKV):
                    ins = pe.matmul(ps[7][0:NOPE, :], dw[:, slot, 4 * (h % 2) + 3, i * 64:i * 64 + 64], pkv[:, i, :], start=(i == 0), stop=(i == KKV - 1))
                ins.then_inc(S("qk_full"), 1)

            pe.wait_ge(S("lnorm"), earlier("lnorm", layer) + KKV + KQ)
            queries(0)
            slot = direct_unit(("v", layer))
            pe.wait_ge(S("fg"), earlier("fg", layer) + len(todo))
            for t in range(T // P):
                if t >= 2:
                    pe.wait_ge(S("v_sb"), earlier("v_sb", layer) + t - 1)
                for i in range(KKV):
                    ins = pe.matmul(ps[2 + t % 2][:, :], pkv[:, i, t * P:(t + 1) * P],
                                    dw[:, slot, 4 * i:4 * i + 4, :].rearrange("p a b -> p (a b)"), start=(i == 0), stop=(i == KKV - 1))
                ins.then_inc(S("v_full"), 1)

            todo_a = items(layer)
            per = len(todo_a) // HEADS

            def scores(n):
                h, q, keys = todo_a[n]
                if n % per == 0:
                    pe.wait_ge(S("qk_rows"), earlier("qk_rows", layer) + 2 * h + 2)
                    pe.wait_ge(S("kr"), earlier("kr", layer) + 4)
                if n < 2:
                    pe.wait_ge(S("v_sb"), earlier("v_sb", layer) + T // P)
                else:
                    pe.wait_ge(S("prob"), earlier("prob", layer) + n - 1)
                pe.matmul(ps[2 + n % 2][:, 0:keys], qT[0:QK, h % 2, q * P:(q + 1) * P], kT[0:QK, h % 2, 0:keys], start=True, stop=True)\
                    .then_inc(S("s_full"), 1)

            def turn(n):
                _, _, keys = todo_a[n]
                pe.wait_ge(S("pn"), earlier("pn", layer) + n + 1)
                if n < 2:
                    pe.wait_ge(S("br_b"), earlier("br_b", layer) + GROUPS)
                else:
                    pe.wait_ge(S("pT"), earlier("pT", layer) + n - 1)
                for t in range(keys // P):
                    ins = pe.transpose(ps[4 + n % 2][:, t * P:(t + 1) * P], prob[:, n % 2, t * P:(t + 1) * P], ident[:, :])
                ins.then_inc(S("t_full"), 1)

            def values(n):
                h, q, keys = todo_a[n]
                pe.wait_ge(S("pT"), earlier("pT", layer) + n + 1)
                if n % per == 0:
                    if h == 0:
                        pe.wait_ge(S("lvar"), earlier("lvar", layer) + 1)
                    else:
                        pe.wait_ge(S("br_a"), earlier("br_a", layer) + h)
                for t in range(keys // P):
                    ins = pe.matmul(ps[6][0:64, q * P:(q + 1) * P], v_rows(t)[:, h * VD:(h + 1) * VD],
                                    pT[:, n % 2, t * P:(t + 1) * P], start=(t == 0), stop=(t == keys // P - 1))
                ins.then_inc(S("pv"), 1)

            def gate_half(m, half):
                if half == 0:
                    if m == 0:
                        pe.wait_ge(S("in_evac"), earlier("in_evac", layer) + NT - 1)
                    else:
                        pe.wait_ge(S("gate"), earlier("gate", layer) + m)
                for k in range(KD // 2 * half, KD // 2 * (half + 1)):
                    block_passes(ps[0][:, 0:T - lc], ("gate", layer, m), k, h_hi[:, k, lc:T], h_lo[:, k, lc:T], k == 0, k == KD - 1)

            def branch(m):
                b = MERGE[m][1]
                slot = direct_unit(("proj", layer, m // 2))
                if m == 0:
                    pe.wait_ge(S("br_b"), earlier("br_b", layer) + GROUPS)
                else:
                    pe.wait_ge(S("o_used"), earlier("o_used", layer) + m)
                if m == BESIDE:
                    pe.wait_ge(S("br_a"), earlier("br_a", layer) + HEADS)
                for k in range(KB):
                    ins = pe.matmul(ps[1][:, 0:T - lc], dw[:, slot, 4 * (m % 2) + k, :], br[:, b, k, lc:T], start=(k == 0), stop=(k == KB - 1))
                ins.then_inc(S("o_full"), 1)
                mod_sums("gate", layer, m)

            keys_of(0)
            for n in range(len(todo_a) + 2):
                if n < len(todo_a):
                    scores(n)
                    if n % per < 2 and todo_a[n][0] + 1 < HEADS:
                        (queries, keys_of)[n % per](todo_a[n][0] + 1)
                    for m, half in halves(layer, n):
                        gate_half(m, half)
                        if half == 1:
                            branch(m)
                if 1 <= n <= len(todo_a):
                    turn(n - 1)
                if n >= 2:
                    values(n - 2)
            for m in range(BESIDE, NM):
                gate_half(m, 0)
                gate_half(m, 1)
                branch(m)
            for j in range(KD):
                if j < 2:
                    pe.wait_ge(S("pT"), earlier("pT", layer) + len(todo_a))
                else:
                    pe.wait_ge(S("x_mix"), earlier("x_mix", layer) + j - 1)
                for k in range(KD):
                    if j == 0:
                        pe.wait_ge(S("y_lo"), earlier("y_lo", layer) + k + 1)
                    block_passes(ps[4 + j % 2][:, 0:T - lc], ("out", layer, j), k, ym_hi[:, k, lc:T], ym_lo[:, k, lc:T], k == 0, k == KD - 1)
                if j >= 1:
                    sum_squares(f"n2_{layer}", lc, j - 1)
                mod_sums("out", layer, j)
            sum_squares(f"n2_{layer}", lc, KD - 1)
            everywhere(f"n2_{layer}", lc)
            if layer == 0:
                for half, ks in enumerate(DOWN):
                    for i in ks:
                        if i < 2:
                            pe.wait_ge(S("o_used"), KD * BRANCHES)
                        else:
                            pe.wait_ge(S("fu"), i - 1)
                        order = [(w, k) for w in (0, 1) for k in range(KD)]
                        if i == 0:
                            order = [(w, k) for k in range(KD) for w in (0, 1)]
                        for w, k in order:
                            if i == 0:
                                pe.wait_ge(S("norm_hlo"), KD * nth("n2_0") + k + 1)
                            block_passes(ps[2 * w + i % 2][:, :], (("upg", "upu")[w], i), k, h_hi[:, k, :], h_lo[:, k, :], k == 0, k == KD - 1)
                        mod_sums("upu", i)
                    for j in range(KD):
                        if half == 0 and j < 2:
                            pe.wait_ge(S("x_mix"), KD)
                        else:
                            pe.wait_ge(S("x_ffn"), KD * half + j - 1)
                        for n, i in enumerate(ks):
                            if j == 0:
                                pe.wait_ge(S("u_lo"), i + 1)
                            block_passes(ps[4 + j % 2][:, :], ("down", half, j), n, u_hi[:, i % USLOTS, :], u_lo[:, i % USLOTS, :], n == 0, n == len(ks) - 1)
                        if half == 1 and j >= 1:
                            sum_squares("n1_1", 0, j - 1)
                        mod_sums("down", half, j)
                sum_squares("n1_1", 0, KD - 1)
                everywhere("n1_1", 0)

        for k in range(KD):
            pe.wait_ge(S("norm_hf"), 2 * KD * nth("n2_1") + k + 1)
            for t in range(2):
                ins = pe.matmul(ps[(7, 3)[t]][:, 0:EXPERTS], hslot(k, SEQ)[:, t * P:(t + 1) * P], router[:, k, :], start=(k == 0), stop=(k == KD - 1))
        ins.then_inc(S("lg_full"), 1)

        def rows_by_token(fills):
            for n in fills:
                part, t, f = n // 4, n // 2 % 2, n % 2
                if n >= 2:
                    pe.wait_ge(S("htok"), n - 1)
                else:
                    pe.wait_ge(S("o_used"), earlier("o_used", 1) + NM)
                src = (h_hi, h_lo)[part][:, :, :].bitcast(F32)
                for i in range(4):
                    ins = pe.transpose(ps[n % 2][:, i * P:(i + 1) * P], src[:, 4 * f + i, SEQ + t * P:SEQ + (t + 1) * P], ident[:, :])
                ins.then_inc(S("ht_full"), 1)

        pe.wait_ge(S("norm_hhi"), KD * nth("n2_1") + KD)
        rows_by_token(range(4))
        pe.wait_ge(S("mask"), 2)
        pe.matmul(ps[7][:, 32:40], before[:, :], mask[:, 0, :], start=True, stop=True)
        pe.matmul(ps[7][:, 40:48], before[:, :], mask[:, 1, :], start=True, stop=False)
        pe.matmul(ps[7][:, 40:48], ones[:, :], mask[:, 0, :], start=False, stop=True)
        pe.matmul(ps[7][:, 48:56], ones[:, :], mask[:, 0, :], start=True, stop=False)
        pe.matmul(ps[7][:, 48:56], ones[:, :], mask[:, 1, :], start=False, stop=True).then_inc(S("cnt_full"), 1)
        pe.wait_ge(S("norm_hlo"), KD * nth("n2_1") + KD)
        rows_by_token(range(4, 8))
        pe.wait_ge(S("htok"), 8)
        pe.wait_ge(S("most_ready"), 1)

        def experts(p):
            used = S("e_used")
            if p == 1:
                pe.wait_ge(S("x_add"), KD * (EXPERTS + 1))
            else:
                pe.sem_inc(S("sc_full"), 4)

            def gather(e, x, part, first=False):
                for f in range(2):
                    if part == 0:
                        if f == 0:
                            pe.wait_ge(S("sel"), passed("sel", p) + e * 2 + 2 * (x + 1))
                        if not first:
                            pe.wait_ge(S("x_add"), passed("x_add", p) + e * KD + KD * x)
                    else:
                        pe.wait_ge(S("xg_hi"), passed("xg_hi", p) + e * 2 + (2 * x + f + 1))
                    for k in range(4):
                        for t in range(2):
                            ins = pe.matmul(ps[5 + f][:, k * SLOTS:(k + 1) * SLOTS], (htok_hi, htok_lo)[part][:, t, (4 * f + k) * P:(4 * f + k + 1) * P],
                                            sel[:, t, :], start=(t == 0), stop=(t == 1))
                    ins.then_inc(S("ga_full"), 1)
                if part == 0:
                    return
                pe.wait_ge(S("selT"), passed("selT", p) + e + (x + 1))
                pe.wait_ge(S("w_slot"), passed("w_slot", p) + e + (x + 1))
                for t in range(2):
                    pe.transpose(ps[7][:, t * P:(t + 1) * P], sel[:, t, :].bitcast(F32), ident[:, :])
                for t in range(2):
                    at = comb[:, t, 0:1] if first else comb[:, t, bass.ds(e + x, 1)]
                    ins = pe.matmul(ps[7][:, SEQ:SEQ + 1], sel[:, t, :].bitcast(F32), at, start=(t == 0), stop=(t == 1))
                ins.then_inc(S("st_full"), 1)

            def turn(c_, pc):
                pe.wait_ge(S("eu"), passed("eu", p) + c_ + (pc + 3))
                for i in range(2):
                    ins = pe.transpose(ps[2][:, pc % 2 * 256 + i * P:pc % 2 * 256 + (i + 1) * P], eu[:, pc % 2, i * P:(i + 1) * P], ident[:, :])
                ins.then_inc(S("tr_full"), 1)

            def split_unit(v0, w):
                pe.wait_ge(S("e_lo_done"), passed("e_lo_done", p) + v0 + (STAGE + w + 1))
                return ehi[:, w % SPLIT, :], elo[:, w % SPLIT, :]

            def up(cc, x, v0, w, second):
                hi, lo = split_unit(v0, w)
                for i in range(4):
                    kk = i + 4 * second
                    o = ps[cc % 2][:, :]
                    cols = slice(i * 512, i * 512 + 512)
                    pe.matmul(o, xg_hi[:, x % 2, kk, :], hi[:, cols], start=(kk == 0), stop=False)
                    pe.matmul(o, xg_hi[:, x % 2, kk, :], lo[:, cols], start=False, stop=False)
                    ins = pe.matmul(o, xg_lo[:, x % 2, kk, :], hi[:, cols], start=False, stop=(kk == KD - 1))
                ins.then_inc(used, 1)

            def down(c_, pc, c, v0, w):
                hi, lo = split_unit(v0, w)
                pe.wait_ge(S("ehT_lo"), passed("ehT_lo", p) + c_ + (pc + 2))
                for i in range(2):
                    a_hi, a_lo = ehT_hi[:, pc % 2, i, :], ehT_lo[:, pc % 2, i, :]
                    first, last = c == 0 and i == 0, c == CHUNKS - 1 and i == 1
                    for f in range(2):
                        cols = slice(i * D + f * 512, i * D + f * 512 + 512)
                        pe.matmul(ps[3 + f][:, :], a_hi, hi[:, cols], start=first, stop=False)
                        pe.matmul(ps[3 + f][:, :], a_hi, lo[:, cols], start=False, stop=False)
                    for f in range(2):
                        cols = slice(i * D + f * 512, i * D + f * 512 + 512)
                        ins = pe.matmul(ps[3 + f][:, :], a_lo, hi[:, cols], start=False, stop=last)
                ins.then_inc(used, 1)

            def scatter(e, x, fills):
                if 0 in fills:
                    pe.wait_ge(S("y_lo_e"), passed("y_lo_e", p) + e * 2 + 2 * (x + 1))
                    pe.wait_ge(S("selT"), passed("selT", p) + e + (x + 1))
                for k4 in fills:
                    if k4 < 2:
                        pe.wait_ge(S("xg_lo"), passed("xg_lo", p) + e * 2 + (2 * x + k4 + 1))
                    else:
                        pe.wait_ge(S("x_add"), passed("x_add", p) + e * KD + (KD * x + 2 * (k4 - 1)))
                    for i in range(2):
                        kk = 2 * k4 + i
                        o = ps[5 + k4 % 2][:, i * SEQ:(i + 1) * SEQ]
                        at = kk % 2 * P
                        pe.matmul(o, y_rows[:, kk // 2, at:at + P], selT[:, (x - 1) % 2, :], start=True, stop=False)
                        ins = pe.matmul(o, y_rows[:, 4 + kk // 2, at:at + P], selT[:, (x - 1) % 2, :], start=False, stop=True)
                    ins.then_inc(S("sc_full"), 1)

            gather(0, 0, 0, first=True)
            gather(0, 0, 1, first=True)
            for f in range(2):
                pe.matmul(ps[3 + f][:, :], selT[:, 1, 0:P], htok_hi[:, 0, 0:512], start=True, stop=False)
            with pe.Fori(0, EXPERTS // PAIR) as e2:
                e = e2 * PAIR
                v0 = e2 * (PAIR * UNITS)
                c_ = e2 * (PAIR * CHUNKS)
                for w in range(PAIR * UNITS):
                    x, c, kind = w // UNITS, w % UNITS // 3, STEPS[w % 3]
                    cc = x * CHUNKS + c
                    if kind == "ga":
                        if c == 0:
                            pe.wait_ge(S("xg_hi"), passed("xg_hi", p) + e * 2 + 2 * (x + 1))
                            pe.wait_ge(S("xg_lo"), passed("xg_lo", p) + e * 2 + 2 * (x + 1))
                        pe.wait_ge(S("eu"), passed("eu", p) + c_ + (cc + 1))
                        up(cc, x, v0, w, 0)
                    elif kind == "gb":
                        turn(c_, cc - 1)
                        up(cc, x, v0, w, 1)
                    else:
                        if c == 1:
                            pe.wait_ge(S("y_lo_e"), passed("y_lo_e", p) + e * 2 + 2 * (x + 1))
                        down(c_, cc - 1, (c - 1) % CHUNKS, v0, w)
                        if c in SCATTER_AT:
                            scatter(e, x, (0, 1) if c == SCATTER_AT[0] else (2, 3))
                        if c in GATHER_AT:
                            gather(e, x + 1, GATHER_AT.index(c))
            turn(EXPERTS * CHUNKS, -1)
            down(EXPERTS * CHUNKS, -1, CHUNKS - 1, EXPERTS * UNITS, 0)
            scatter(EXPERTS, 0, range(KD // 2))
            pe.sem_inc(used, PASS_UNITS - EXPERTS * UNITS - 1)

        experts(0)
        most_r = pe.value_load(most_i[0:1, 0:1], min_val=0, max_val=SEQ)
        with pe.If(most_r > SLOTS):
            experts(1)
        pe.wait_ge(S("experts_done"), 1)
        for k in range(KD):
            sum_squares("fin", SEQ, k)
        everywhere("fin", SEQ)

    ctx_block.__exit__(None, None, None)


def _blocks(w):
    k, c = w.shape[0] // P, w.shape[1] // P
    return w.reshape(k, P, c, P).transpose(0, 2, 1, 3)


def _constants():
    import numpy as np

    t = np.arange(SEQ)
    half = ROPE // 2
    inv = (10000.0 ** (-np.arange(0, half, 2) / half)).astype(np.float32)
    pos = np.stack([t // 64, t % 64], axis=1).astype(np.float32)
    ang = (pos[:, :, None] * inv).astype(np.float32)
    cos, sin = np.cos(ang), np.sin(ang)
    rope = np.zeros((P, T), np.float32)
    for r in range(ROPE):
        axis, second, f = r // 16, r // 8 % 2, r % 8
        rope[NOPE + r, 0:SEQ] = 1.0
        rope[NOPE + r, SEQ:T] = cos[:, axis, f]
        rope[QK + r, SEQ:T] = sin[:, axis, f] if second else -sin[:, axis, f]
    c = np.arange(P)
    a = 2 * np.pi * np.outer(c, c) / P
    dft_c = np.concatenate([np.cos(a), np.sin(a)], axis=1) / np.sqrt(P)
    b = 2 * np.pi * np.outer(t, t) / SEQ
    dft_l = np.stack([np.cos(b), -np.sin(b)], axis=1) / np.sqrt(SEQ)
    dft_l = dft_l.reshape(2, P, 2, SEQ).transpose(1, 0, 2, 3)
    inv_n = np.zeros((P, GROUPS, SEQ), np.float32)
    for g, w in enumerate((2, 4, 8, 16)):
        left = w // 2
        right = w - 1 - left
        inv_n[:, g, :] = 1.0 / (np.minimum(t + right + 1, SEQ) - np.maximum(t - left, 0))
    out = {
        "ones": np.ones((P, P)), "ident": np.eye(P), "iota": np.tile(np.arange(P), (P, 1)),
        "before": np.triu(np.ones((P, P)), 1), "rope": rope, "dft_c": dft_c, "dft_l": dft_l, "inv_n": inv_n,
    }
    return {k: np.ascontiguousarray(v, dtype=np.float32) for k, v in out.items()}


def layout(i):
    import numpy as np

    i = {k: np.asarray(v) for k, v in i.items()}
    off_kv, off_kr = Q_LORA, Q_LORA + KV_LORA
    off_pool = off_kr + ROPE
    off_fft = off_pool + BRANCH_W
    off_gate = off_fft + BRANCH_W
    partner = np.arange(ROPE) ^ 8

    def cols(v):
        v = v.reshape(*v.shape[:-1], v.shape[-1] // P, P)
        return np.moveaxis(v, -1, 0)

    def tile_columns(layer, name):
        w = i["w_in"][layer]
        g = int(name[-1]) if name[-1].isdigit() else 0
        if name == "kr":
            kr = w[:, off_kr:off_pool]
            return np.concatenate([kr, kr[:, partner], kr, kr[:, partner]], axis=1)
        at = {"kv": off_kv, "q": 0, "fft": off_fft, "pool": off_pool}[name[:-1]] + g * P
        return w[:, at:at + P]

    split = []
    for key, _ in split_stream():
        kind = key[0]
        if kind == "in":
            b = _blocks(tile_columns(key[1], TILES[key[2]]))
        elif kind == "gate":
            j, br = MERGE[key[2]]
            at = off_gate + br * D + j * P
            b = _blocks(i["w_in"][key[1]][:, at:at + P])
        elif kind == "out":
            b = _blocks(i["w_out"][key[1]][:, key[2] * P:(key[2] + 1) * P])
        elif kind in ("upg", "upu"):
            w = i["ffn_w1" if kind == "upg" else "ffn_w3"][0]
            b = _blocks(w[:, key[1] * P:(key[1] + 1) * P])
        else:
            ks = DOWN[key[1]]
            b = _blocks(i["ffn_w2"][0][ks[0] * P:(ks[-1] + 1) * P, key[2] * P:(key[2] + 1) * P])
        split.append(b[:, 0])
        if any(key == pair[1] for pair in TOGETHER):
            second, first = split.pop(), split.pop()
            split.append(np.stack([first, second], axis=1).reshape(-1, P, P))
    split = np.concatenate(split, axis=0)
    split = split.reshape(-1, SPLIT_BLOCKS, P, P).transpose(0, 2, 1, 3).reshape(-1, P, SPLIT_BLOCKS * P)

    direct = []
    for key in direct_stream():
        kind, layer = key[0], key[1]
        unit = np.zeros((P, DIRECT_BLOCKS, P), np.float32)
        if kind == "pool":
            unit[:, 0:GROUPS] = i["w_pool"][layer].transpose(1, 0, 2)
        elif kind == "v":
            v = i["w_ukv"][layer][:, :, NOPE:].reshape(KKV, P, HEADS * VD)
            unit[:] = v.transpose(1, 0, 2).reshape(P, DIRECT_BLOCKS, P)
        elif kind == "head":
            for x in range(2):
                h = 2 * key[2] + x
                q = i["w_uq"][layer][:, h, :]
                q = np.concatenate([q, q[:, NOPE:][:, partner]], axis=1)
                unit[:, 4 * x:4 * x + KQ] = _blocks(q)[:, 0].transpose(1, 0, 2)
                k = i["w_ukv"][layer][:, h, 0:NOPE].reshape(KKV, P, NOPE)
                unit[:, 4 * x + 3] = k.transpose(1, 0, 2).reshape(P, P)
        else:
            for x in range(2):
                j, b = MERGE[2 * key[2] + x]
                w = i[("w_oa", "w_ob", "w_oc")[b]][layer]
                unit[:, 4 * x:4 * x + 4] = _blocks(w[:, j * P:(j + 1) * P])[:, 0].transpose(1, 0, 2)
        direct.append(unit)

    def mod_groups(which):
        out = []
        for layer, g in which:
            w = i["w_mod"][layer][:, g * GC:(g + 1) * GC].reshape(GROUP_UNITS, 2, P, GC)
            out.append(w.transpose(0, 2, 1, 3))
        return np.concatenate(out)

    up = np.stack([i["moe_w1"][0], i["moe_w3"][0]], axis=0)
    up = up.reshape(2, EXPERTS, 2, 4, P, CHUNKS, CW).transpose(1, 5, 2, 4, 3, 0, 6)
    up = up.reshape(EXPERTS, CHUNKS, 2, P, 4 * 2 * CW)
    down = i["moe_w2"][0].reshape(EXPERTS, CHUNKS, 2, P, D).transpose(0, 1, 3, 2, 4).reshape(EXPERTS * CHUNKS, P, 2 * D)
    moe = np.zeros((MOE_UNITS, P, 2 * D), np.float32)
    moe[0:-1:3] = up[:, :, 0].reshape(EXPERTS * CHUNKS, P, 2 * D)
    moe[1::3] = up[:, :, 1].reshape(EXPERTS * CHUNKS, P, 2 * D)
    moe[5::3] = down[:-1]
    moe[-1] = down[-1]

    gains = np.concatenate([np.stack([i["g_norm1"], i["g_norm2"]], axis=1).reshape(2 * DEPTH, D), i["g_final"][None]], axis=0)
    x = np.concatenate([i["ctx"][0], i["x"][0]], axis=0)
    out = {
        "x": cols(x).transpose(0, 2, 1), "cond": cols(np.stack([i["c_ctx"], i["c"][0]], axis=0)).transpose(0, 2, 1),
        "b_mod": cols(i["b_mod"]), "gains": cols(gains), "b_gate": cols(i["b_gate"]), "s_pool": cols(i["s_pool"]),
        "g_q": cols(i["g_q"]), "g_kv": cols(i["g_kv"]),
        "router": i["moe_router"][0].reshape(KD, P, EXPERTS).transpose(1, 0, 2),
        "r_bias": np.broadcast_to(i["moe_bias"][0], (P, EXPERTS)),
        "split": split, "direct": np.stack(direct), "early": mod_groups([(0, g) for g in range((EARLY_UNITS + START_UNITS) // GROUP_UNITS)]),
        "groups": mod_groups(MOD_GROUPS[START_UNITS // GROUP_UNITS:]), "moe": moe,
    }
    return {k: np.ascontiguousarray(v) for k, v in out.items()} | _constants()


def kernel(**inputs):
    import concourse.bacc as bacc
    import numpy as np
    from concourse.bass_utils import run_bass_kernel_spmd

    arrays = layout(inputs)
    nc = bacc.Bacc("TRN2", target_bir_lowering=False, num_devices=1)
    aps = {k: nc.dram_tensor(f"in_{k}", v.shape, mybir.dt.from_np(v.dtype), kind="ExternalInput").ap() for k, v in arrays.items()}
    aps["out"] = nc.dram_tensor("out_x", (P, KD, SEQ), F32, kind="ExternalOutput").ap()
    build(nc, aps)
    r = run_bass_kernel_spmd(nc, [{f"in_{k}": v for k, v in arrays.items()}], core_ids=[0])
    y = r.results[0]["out_x"]
    return np.ascontiguousarray(y.transpose(2, 1, 0)).reshape(1, SEQ, D)
```
